# Optimizing a Trainium2 kernel written in Bass

```python
import math, functools
import jax, jax.numpy as jnp
from jax import lax
import numpy as np

D_MODEL = 1024
BATCH = 1
SEQ = 1024
DEPTH = 1
DEC_BATCH = 8
DEC_SEQ = 1
PAST_LEN = 512
PAGE_SIZE = 128

R_HEADS = 4
R_DK = 128
R_DV = 256
R_CHUNK = 128
R_ROT_BASE = 10000.0
A_HEADS = 4
A_DQ = 64
A_DV = 2 * A_DQ
A_QBLOCK = 128
ROPE_THETA = 500000.0
ROT_DIM = A_DQ // 4
R_QK_W = R_HEADS * R_DK
R_V_W = R_HEADS * R_DV
A_QK_W = A_HEADS * 2 * A_DQ
A_V_W = A_HEADS * A_DV
_IN_SIZES = (R_QK_W, R_QK_W, R_V_W, A_QK_W, A_QK_W, A_V_W, D_MODEL, D_MODEL)
IN_COLS = sum(_IN_SIZES)
IN_SPLITS = tuple(int(s) for s in np.cumsum(_IN_SIZES)[:-1])
P_HEADS = 8
P_NKEYS = 128
P_NEXPERTS = P_NKEYS * P_NKEYS
P_DKEY = 256
P_TOPK = 16
P_TOKBLOCK = 128
NORM_EPS = 1e-6
SUBLN_EPS = 1e-5

kernel_name = 'retention_diffattn_peer_hybrid_step'

def rms_norm(x, g=None, eps=NORM_EPS):
    xf = x.astype(jnp.float32)
    y = xf * lax.rsqrt(jnp.mean(xf * xf, axis=-1, keepdims=True) + eps)
    if g is not None:
        y = y * g.astype(jnp.float32)
    return y.astype(x.dtype)

def retention_rotate(x, posf):
    angle = 1.0 / (R_ROT_BASE ** jnp.linspace(0.0, 1.0, R_DK // 2, dtype=jnp.float32))
    ang = posf[:, None] * angle[None, :]
    cos = jnp.cos(ang)[None, :, None, :].astype(x.dtype)
    sin = jnp.sin(ang)[None, :, None, :].astype(x.dtype)
    xr = x.reshape(x.shape[:-1] + (R_DK // 2, 2))
    x1, x2 = xr[..., 0], xr[..., 1]
    out = jnp.stack([x1 * cos - x2 * sin, x2 * cos + x1 * sin], axis=-1)
    return out.reshape(x.shape)

def partial_rotary(x, posf):
    half = ROT_DIM // 2
    inv = ROPE_THETA ** (-jnp.arange(0, ROT_DIM, 2, dtype=jnp.float32) / ROT_DIM)
    ang = posf[:, None] * inv[None, :]
    cos = jnp.cos(ang)[None, :, None, None, :].astype(x.dtype)
    sin = jnp.sin(ang)[None, :, None, None, :].astype(x.dtype)
    x1 = x[..., :half]
    x2 = x[..., half:ROT_DIM]
    return jnp.concatenate([x1 * cos - x2 * sin, x2 * cos + x1 * sin, x[..., ROT_DIM:]], axis=-1)

def retention_chunk(q, k, v, state, log_decay):
    L = q.shape[1]
    idx = jnp.arange(L, dtype=jnp.float32)
    rel = idx[:, None] - idx[None, :]
    dmask = jnp.where((rel >= 0)[None], jnp.exp(log_decay[:, None, None] * jnp.maximum(rel, 0.0)[None]), 0.0)
    qf, kf, vf = q.astype(jnp.float32), k.astype(jnp.float32), v.astype(jnp.float32)
    scores = jnp.einsum('blhd,bmhd->bhlm', qf, kf) * dmask[None]
    intra = jnp.einsum('bhlm,bmhe->blhe', scores, vf)
    q_decay = jnp.exp(log_decay[None, :] * (idx[:, None] + 1.0))
    inter = jnp.einsum('blhd,bhde->blhe', qf, state) * q_decay[None, :, :, None]
    k_decay = jnp.exp(log_decay[None, :] * (L - 1.0 - idx[:, None]))
    new_state = (state * jnp.exp(log_decay * L)[None, :, None, None]
                 + jnp.einsum('blhd,lh,blhe->bhde', kf, k_decay, vf))
    return intra + inter, new_state

def retention_prompt(q, k, v, log_decay):
    B, S = q.shape[:2]
    n = S // R_CHUNK

    def to_chunks(t):
        return t.reshape((B, n, R_CHUNK) + t.shape[2:]).swapaxes(0, 1)

    def step(state, qkv):
        out, state = retention_chunk(qkv[0], qkv[1], qkv[2], state, log_decay)
        return state, out

    s0 = jnp.zeros((B, R_HEADS, R_DK, R_DV), jnp.float32)
    s_final, outs = lax.scan(step, s0, (to_chunks(q), to_chunks(k), to_chunks(v)))
    return outs.swapaxes(0, 1).reshape(B, S, R_HEADS, R_DV), s_final

def retention_sample(q, k, v, log_decay, state):
    return retention_chunk(q, k, v, state.astype(jnp.float32), log_decay)

def diff_attention(q, k, v, q_pos, k_pos, lam):
    s = jnp.einsum('bqhcd,bkhcd->bhcqk', q, k).astype(jnp.float32) * (A_DQ ** -0.5)
    mask = k_pos[None, :] <= q_pos[:, None]
    s = jnp.where(mask, s, -1e30)
    p = jax.nn.softmax(s, axis=-1)
    a = p[:, :, 0] - lam * p[:, :, 1]
    return jnp.einsum('bhqk,bkhe->bqhe', a.astype(v.dtype), v)

def attention_prompt(q, k, v, lam):
    B, S = q.shape[:2]
    nblk = S // A_QBLOCK
    pos = jnp.arange(S, dtype=jnp.int32)
    qb = q.reshape((B, nblk, A_QBLOCK) + q.shape[2:]).swapaxes(0, 1)
    qpos = pos.reshape(nblk, A_QBLOCK)
    out = lax.map(lambda xs: diff_attention(xs[0], k, v, xs[1], pos, lam), (qb, qpos))
    return out.swapaxes(0, 1).reshape(B, S, A_HEADS, A_DV)

def attention_sample(q, k, v, lam, past_k, past_v, past_len):
    L = q.shape[1]
    k_all = jnp.concatenate([past_k.astype(k.dtype), k], axis=1)
    v_all = jnp.concatenate([past_v.astype(v.dtype), v], axis=1)
    k_pos = jnp.arange(past_len + L, dtype=jnp.int32)
    q_pos = past_len + jnp.arange(L, dtype=jnp.int32)
    return diff_attention(q, k_all, v_all, q_pos, k_pos, lam)

def gather_pages(cache_l, page_table):
    g = jnp.take(cache_l, page_table, axis=0)
    return g.reshape((g.shape[0], g.shape[1] * g.shape[2]) + g.shape[3:])

def peer(z, w_query, sub_keys, expert_u, expert_v):
    T = z.shape[0]
    qry = (z @ w_query).reshape(T, P_HEADS, 2, P_DKEY // 2)
    sc = jnp.einsum('thcd,hcnd->thcn', qry, sub_keys).astype(jnp.float32)
    s_half, i_half = lax.top_k(sc, P_TOPK)
    cand_s = (s_half[:, :, 0, :, None] + s_half[:, :, 1, None, :]).reshape(T, P_HEADS, P_TOPK * P_TOPK)
    cand_i = (i_half[:, :, 0, :, None] * P_NKEYS + i_half[:, :, 1, None, :]).reshape(T, P_HEADS, P_TOPK * P_TOPK)
    top_s, top_pos = lax.top_k(cand_s, P_TOPK)
    ids = jnp.take_along_axis(cand_i, top_pos, axis=-1)
    gate = jax.nn.softmax(top_s, axis=-1)
    u = jnp.take(expert_u, ids, axis=0)
    act = jax.nn.gelu(jnp.einsum('thkd,td->thk', u, z).astype(jnp.float32), approximate=False) * gate
    v = jnp.take(expert_v, ids, axis=0)
    return jnp.einsum('thk,thkd->td', act.astype(z.dtype), v)

def hybrid_layer(x, pos, ret_fn, att_fn, blocked_peer, layer_idx,
                 g_mix, w_in, lam_q1, lam_k1, lam_q2, lam_k2, g_subln,
                 w_br_ret, w_br_att, w_out, g_ffn, w_query, sub_keys, expert_u, expert_v):
    B, L, D = x.shape
    posf = pos.astype(jnp.float32)
    z = rms_norm(x, g_mix)
    rq, rk, rv, aq, ak, av, ga, gb = jnp.split(z @ w_in, IN_SPLITS, axis=-1)
    rq = retention_rotate(rq.reshape(B, L, R_HEADS, R_DK), posf)
    rk = retention_rotate(rk.reshape(B, L, R_HEADS, R_DK), posf) * (R_DK ** -0.5)
    rv = rv.reshape(B, L, R_HEADS, R_DV)
    aq = partial_rotary(aq.reshape(B, L, A_HEADS, 2, A_DQ), posf)
    ak = partial_rotary(ak.reshape(B, L, A_HEADS, 2, A_DQ), posf)
    av = av.reshape(B, L, A_HEADS, A_DV)
    log_decay = jnp.log(1.0 - 2.0 ** (-5.0 - jnp.arange(R_HEADS, dtype=jnp.float32)))
    r_out, r_state = ret_fn(rq, rk, rv, log_decay)
    r_out = rms_norm(r_out).astype(x.dtype).reshape(B, L, R_V_W)
    lam_init = 0.8 - 0.6 * math.exp(-0.3 * layer_idx)
    lam = (jnp.exp(jnp.sum(lam_q1.astype(jnp.float32) * lam_k1.astype(jnp.float32)))
           - jnp.exp(jnp.sum(lam_q2.astype(jnp.float32) * lam_k2.astype(jnp.float32))) + lam_init)
    a_out = att_fn(aq, ak, av, lam)
    a_out = (rms_norm(a_out, g_subln, SUBLN_EPS) * (1.0 - lam_init)).reshape(B, L, A_V_W)
    m = jax.nn.sigmoid(ga) * (r_out @ w_br_ret) + jax.nn.sigmoid(gb) * (a_out @ w_br_att)
    h = x + m @ w_out
    z2 = rms_norm(h, g_ffn).reshape(B * L, D)
    if blocked_peer:
        f = lax.map(lambda zz: peer(zz, w_query, sub_keys, expert_u, expert_v),
                    z2.reshape(-1, P_TOKBLOCK, D))
    else:
        f = peer(z2, w_query, sub_keys, expert_u, expert_v)
    h = h + f.reshape(B, L, D)
    return h, r_state, ak.reshape(B, L, A_HEADS, 2 * A_DQ), av

def setup_inputs(seed: int = 0) -> dict:
    key = jax.random.key(seed)
    ks = jax.random.split(key, 24)
    f32 = jnp.float32
    n_pages = PAST_LEN // PAGE_SIZE
    n_pool = (DEC_BATCH * n_pages * 5) // 4

    def nrm(k, shape, scale):
        return jax.random.normal(k, shape, f32) * scale

    def gain(k, shape):
        return 1.0 + 0.01 * jax.random.normal(k, shape, f32)

    page_table = jax.random.permutation(ks[5], n_pool)[:DEC_BATCH * n_pages].reshape(DEC_BATCH, n_pages).astype(jnp.int32)
    return {
        'x_prompt': nrm(ks[0], (BATCH, SEQ, D_MODEL), 1.0),
        'x_sample': nrm(ks[1], (DEC_BATCH, DEC_SEQ, D_MODEL), 1.0),
        'state_ret': nrm(ks[2], (DEPTH, DEC_BATCH, R_HEADS, R_DK, R_DV), 0.5),
        'cache_k': nrm(ks[3], (DEPTH, n_pool, PAGE_SIZE, A_HEADS, 2 * A_DQ), 1.0),
        'cache_v': nrm(ks[4], (DEPTH, n_pool, PAGE_SIZE, A_HEADS, A_DV), 1.0),
        'page_table': page_table,
        'g_mix': gain(ks[6], (DEPTH, D_MODEL)),
        'w_in': nrm(ks[7], (DEPTH, D_MODEL, IN_COLS), D_MODEL ** -0.5),
        'lam_q1': nrm(ks[8], (DEPTH, A_DQ), 0.1),
        'lam_k1': nrm(ks[9], (DEPTH, A_DQ), 0.1),
        'lam_q2': nrm(ks[10], (DEPTH, A_DQ), 0.1),
        'lam_k2': nrm(ks[11], (DEPTH, A_DQ), 0.1),
        'g_subln': gain(ks[12], (DEPTH, A_DV)),
        'w_br_ret': nrm(ks[13], (DEPTH, R_V_W, D_MODEL), R_V_W ** -0.5),
        'w_br_att': nrm(ks[14], (DEPTH, A_V_W, D_MODEL), A_V_W ** -0.5),
        'w_out': nrm(ks[15], (DEPTH, D_MODEL, D_MODEL), D_MODEL ** -0.5),
        'g_ffn': gain(ks[16], (DEPTH, D_MODEL)),
        'w_query': nrm(ks[17], (DEPTH, D_MODEL, P_HEADS * P_DKEY), D_MODEL ** -0.5),
        'sub_keys': nrm(ks[18], (DEPTH, P_HEADS, 2, P_NKEYS, P_DKEY // 2), (P_DKEY // 2) ** -0.5),
        'expert_u': nrm(ks[19], (DEPTH, P_NEXPERTS, D_MODEL), D_MODEL ** -0.5),
        'expert_v': nrm(ks[20], (DEPTH, P_NEXPERTS, D_MODEL), 0.5),
        'g_final': gain(ks[21], (D_MODEL,)),
    }

def reference(x_prompt, x_sample, state_ret, cache_k, cache_v, page_table, g_mix, w_in,
              lam_q1, lam_k1, lam_q2, lam_k2, g_subln, w_br_ret, w_br_att, w_out, g_ffn,
              w_query, sub_keys, expert_u, expert_v, g_final):
    S = x_prompt.shape[1]
    DB, L = x_sample.shape[0], x_sample.shape[1]
    past_len = page_table.shape[1] * cache_k.shape[2]
    pos_p = jnp.arange(S, dtype=jnp.int32)
    pos_s = past_len + jnp.arange(L, dtype=jnp.int32)
    hp, hs = x_prompt, x_sample
    rs_p, k_p, v_p, rs_s, k_s, v_s = [], [], [], [], [], []
    for l in range(DEPTH):
        w = (g_mix[l], w_in[l], lam_q1[l], lam_k1[l], lam_q2[l], lam_k2[l], g_subln[l],
             w_br_ret[l], w_br_att[l], w_out[l], g_ffn[l], w_query[l], sub_keys[l], expert_u[l], expert_v[l])
        hp, st, kr, vr = hybrid_layer(hp, pos_p, retention_prompt, attention_prompt, True, l, *w)
        rs_p.append(st)
        k_p.append(kr)
        v_p.append(vr)
        past_k = gather_pages(cache_k[l], page_table).reshape(DB, past_len, A_HEADS, 2, A_DQ)
        past_v = gather_pages(cache_v[l], page_table)
        ret_fn = functools.partial(retention_sample, state=state_ret[l])
        att_fn = functools.partial(attention_sample, past_k=past_k, past_v=past_v, past_len=past_len)
        hs, st, kr, vr = hybrid_layer(hs, pos_s, ret_fn, att_fn, False, l, *w)
        rs_s.append(st)
        k_s.append(kr)
        v_s.append(vr)
    y_prompt = rms_norm(hp, g_final)
    y_sample = rms_norm(hs, g_final)
    return (y_prompt, y_sample, jnp.stack(rs_p), jnp.stack(k_p), jnp.stack(v_p),
            jnp.stack(rs_s), jnp.stack(k_s), jnp.stack(v_s))


_drawn_inputs = setup_inputs


def setup_inputs(seed=0):
    import zlib

    import numpy as np

    out = dict(_drawn_inputs(seed))
    spreads = {}
    factors = {'lam_k1': 3.374, 'lam_q2': 3.456, 'g_subln': 65.031, 'g_final': 161.74, 'g_ffn': 18.113}
    for name, (base, spread) in spreads.items():
        noise = np.random.default_rng([zlib.crc32(name.encode()), seed]).standard_normal(out[name].shape)
        drawn = base * np.exp(spread * noise) if base else spread * noise
        out[name] = __import__('jax').numpy.asarray(drawn.astype(out[name].dtype))
    for name, factor in factors.items():
        out[name] = (out[name] * factor).astype(out[name].dtype)
    return out
```

```python
from contextlib import ExitStack

import numpy as np
import concourse.bass as bass
from concourse import mybir
from concourse.alu_op_type import AluOpType as ALU

F32 = mybir.dt.float32
U32 = mybir.dt.uint32
I32 = mybir.dt.int32
ACT = mybir.ActivationFunctionType
AX_X = mybir.AxisListType.X
ds = bass.ds

P = 128
D = 1024
KD = D // P
SEQ = 1024
NS = 8
T = SEQ + NS
NT = SEQ // P
TB = T // 3
BLOCKS = [(b * TB, (b + 1) * TB) for b in range(3)]
BANK = 512
RH, RDK, RDV = 4, 128, 256
AH, ADQ, ADV = 4, 64, 128
ROT = ADQ // 4
PAST, PAGE = 512, 128
NPAGE = PAST // PAGE
POOL = 40
PH, NK, TOPK = 8, 128, 16
WR = 2 * RH * RDK + RH * RDV
WA = 2 * AH * 2 * ADQ + AH * ADV
EPS, SUB_EPS = 1e-6, 1e-5
LAM_INIT = 0.8 - 0.6
NEG = -1e30
GC = 4
TILES = [(t, t * P, P) for t in range(NT)] + [(NT, SEQ, NS)]


class Chain:

    def __init__(self, eng, sem, base=0):
        self.eng, self.sem, self.base, self.n = eng, sem, base, 0

    def __call__(self, ins):
        ins.then_inc(self.sem, 1)
        self.n += 1
        self.eng.wait_ge(self.sem, self.base + self.n)


class Scope(ExitStack):

    def __init__(self, nc):
        super().__init__()
        self.nc, self.sems = nc, []

    def sem(self, name):
        self.sems.append(self.enter_context(self.nc.semaphore(name)))
        return self.sems[-1]

    def __exit__(self, *error):
        for s in self.sems:
            self.nc.gpsimd.sem_clear(s)
        self.nc.all_engine_barrier()
        return super().__exit__(*error)


def build(nc, a, stop=99):
    top = ExitStack()
    with top:
        def sb(name, shape, dt=F32, ctx=top):
            return ctx.enter_context(nc.sbuf_tensor(name, shape, dt))

        def sem(name, ctx=top):
            return ctx.enter_context(nc.semaphore(name))

        h_dram = nc.dram_tensor("h_scratch", [T, D], F32, kind="Internal").ap()
        g_dram = nc.dram_tensor("gate_scratch", [NK, P, SEQ], F32, kind="Internal").ap()

        ps = top.enter_context(nc.psum_tensor("ps", [P, 8, BANK], F32))
        ident = sb("ident", [P, P])
        lam = sb("lam", [P, 1])

        s_const = sem("const_loaded")
        with ExitStack() as mid:
            zT = sb("zT", [P, KD, T], ctx=mid)
            rT = sb("rT", [P, KD, T], ctx=mid)
            aT = sb("aT", [P, AH, T], ctx=mid)
            s_rqk = sb("s_rqk", [NS, 2 * RH * RDK], ctx=mid)
            s_rv = sb("s_rv", [NS, RH * RDV], ctx=mid)
            s_aqk = sb("s_aqk", [NS, 2 * AH * 2 * ADQ], ctx=mid)
            s_av = sb("s_av", [NS, AH * ADV], ctx=mid)
            norm_phase(nc, a, ps, ident, s_const, zT, lam)
            if stop >= 2:
                retention_phase(nc, a, ps, ident, zT, rT, s_rqk, s_rv)
            with ExitStack() as att:
                QT = sb("QT", [P, AH, SEQ], ctx=att)
                KT = sb("KT", [P, AH, SEQ], ctx=att)
                VA = sb("VA", [P, NT, AH * ADV], ctx=att)
                if stop >= 3:
                    attention_projection(nc, a, ps, ident, zT, QT, KT, VA, s_aqk, s_av)
                if stop >= 4:
                    attention_phase(nc, a, ps, ident, QT, KT, VA, aT, lam)
            if stop >= 5:
                sample_phase(nc, a, ps, ident, s_rqk, s_rv, s_aqk, s_av, rT, aT, lam)
            if stop >= 6:
                mT = sb("mT", [P, KD, T], ctx=mid)
                merge_phase(nc, a, ps, zT, rT, aT, mT)
                residual_phase(nc, a, ps, mT, h_dram)
        if stop >= 7:
            z2T = sb("z2T", [P, KD, T])
            g_sample = sb("g_sample", [P, NK, NS])
            norm2_phase(nc, a, ps, ident, z2T, h_dram)
            with ExitStack() as route:
                gT = sb("gT", [P, T], ctx=route)
                iT = sb("iT", [P, T], ctx=route)
                jT = sb("jT", [P, T], ctx=route)
                routing_phase(nc, a, ps, ident, z2T, gT, iT, jT)
                gate_phase(nc, a, ps, gT, iT, jT, g_dram, g_sample)
            expert_phase(nc, a, ps, z2T, g_dram, g_sample, h_dram)


def norm_rows(nc, name, ctx, block, ps, ident, zT, src, gain_cols, const_ready,
              extra_sync=None):
    def sb(n, shape):
        return ctx.enter_context(nc.sbuf_tensor(f"{name}_{n}", shape, F32))

    def sem(n):
        return ctx.sem(f"{name}_{n}")

    x = sb("x", [P, 2, D])
    z = sb("z", [P, 2, D])
    junk = sb("junk", [P, D])
    st = sb("st", [P, 2, 4])
    loaded = [sem(f"rows_loaded{u}") for u in range(2)]
    squared = [sem(f"squares_summed{u}") for u in range(2)]
    mean = [sem(f"mean_ready{u}") for u in range(2)]
    root = [sem(f"root_ready{u}") for u in range(2)]
    inverse = [sem(f"inverse_ready{u}") for u in range(2)]
    scaled = [sem(f"rows_scaled{u}") for u in range(2)]
    turned = [sem(f"rows_turned{u}") for u in range(2)]
    kept = [sem(f"columns_kept{u}") for u in range(2)]

    def over_tiles(eng, step):
        with eng.Fori(0, NT // 2) as it:
            for u in range(2):
                step(it, u, P)
        step(NT // 2, 0, NS)

    @block.sync
    def _(sp):
        if extra_sync:
            extra_sync(sp)

        def step(it, u, rows):
            sp.wait_ge(scaled[u], it)
            row = (2 * it + u) * P
            sp.dma_start(x[0:rows, u, :], src[ds(row, rows), :]).then_inc(loaded[u], 16)
        over_tiles(sp, step)

    @block.scalar
    def _(act):
        def step(it, u, rows):
            act.wait_ge(loaded[u], 16 * it + 16)
            nc.scalar.activation(junk[0:rows, :], x[0:rows, u, :], ACT.Square,
                                 accum_out=st[0:rows, u, 0:1]).then_inc(squared[u], 1)
            act.wait_ge(mean[u], it + 1)
            nc.scalar.activation(st[0:rows, u, 2:3], st[0:rows, u, 1:2], ACT.Sqrt).then_inc(root[u], 1)
        over_tiles(act, step)

    @block.vector
    def _(dve):
        def step(it, u, rows):
            dve.wait_ge(squared[u], it + 1)
            nc.vector.tensor_scalar(st[0:rows, u, 1:2], st[0:rows, u, 0:1], 1.0 / D, EPS,
                                    ALU.mult, ALU.add).then_inc(mean[u], 1)
            dve.wait_ge(root[u], it + 1)
            nc.vector.reciprocal(st[0:rows, u, 3:4], st[0:rows, u, 2:3]).then_inc(inverse[u], 1)
            dve.wait_ge(inverse[u], it + 1)
            dve.wait_ge(turned[u], it)
            nc.vector.tensor_scalar(z[0:rows, u, :], x[0:rows, u, :], st[0:rows, u, 3:4], None,
                                    ALU.mult).then_inc(scaled[u], 1)
            dve.wait_ge(turned[u], it + 1)
            col = (2 * it + u) * P
            nc.vector.tensor_tensor(
                zT[:, :, ds(col, rows)],
                ps[:, 2 * u:2 * u + 2, :].rearrange("p b (c r) -> p (b c) r", r=P)[:, :, 0:rows],
                gain_cols[:, :].unsqueeze(2).to_broadcast([P, KD, rows]), ALU.mult).then_inc(kept[u], 1)
        over_tiles(dve, step)

    @block.tensor
    def _(pe):
        pe.wait_ge(*const_ready)

        def step(it, u, rows):
            pe.wait_ge(scaled[u], it + 1)
            pe.wait_ge(kept[u], it)
            for c in range(KD):
                last = nc.tensor.transpose(ps[:, 2 * u + c // 4, (c % 4) * P:(c % 4) * P + rows],
                                           z[0:rows, u, c * P:(c + 1) * P], ident[0:rows, 0:rows])
            last.then_inc(turned[u], 1)
        over_tiles(pe, step)


def norm_phase(nc, a, ps, ident, s_const, zT, lam):
    with Scope(nc) as ctx, nc.Block() as block:
        gain = ctx.enter_context(nc.sbuf_tensor("gain_mix", [P, KD], F32))
        lv = ctx.enter_context(nc.sbuf_tensor("lam_vectors", [P, 4, ADQ], F32))
        lp = ctx.enter_context(nc.sbuf_tensor("lam_products", [P, 2, ADQ], F32))
        le = ctx.enter_context(nc.sbuf_tensor("lam_parts", [P, 4], F32))
        s_step = ctx.sem("lam_step")
        s_sum = ctx.sem("lam_sums")
        s_exp = ctx.sem("lam_exps")
        n = 16 * 3
        def consts(sp):
            sp.dma_start(ident[:, :], a["ident"]).then_inc(s_const, 16)
            sp.dma_start(gain[:, :], a["g_mix"]).then_inc(s_const, 16)
            sp.dma_start(lv[:, :, :], a["lams"].partition_broadcast(P)).then_inc(s_const, 16)

        @block.vector
        def _(dve):
            link = Chain(dve, s_step)
            dve.wait_ge(s_const, n)
            link(nc.vector.tensor_tensor(lp[:, :, :], lv[:, 0:4:2, :], lv[:, 1:4:2, :], ALU.mult))
            nc.vector.tensor_reduce(le[:, 0:2], lp[:, :, :], AX_X, ALU.add).then_inc(s_sum, 1)

        @block.scalar
        def _(act):
            act.wait_ge(s_sum, 1)
            nc.scalar.activation(le[:, 2:4], le[:, 0:2], ACT.Exp).then_inc(s_exp, 1)

        @block.gpsimd
        def _(pool):
            pool.wait_ge(s_exp, 1)
            nc.gpsimd.tensor_tensor(le[:, 0:1], le[:, 2:3], le[:, 3:4], ALU.subtract).then_inc(s_exp, 1)
            pool.wait_ge(s_exp, 2)
            nc.gpsimd.tensor_scalar(lam[:, :], le[:, 0:1], LAM_INIT, None, ALU.add).then_inc(s_exp, 1)

        norm_rows(nc, "mix", ctx, block, ps, ident, zT, a["x"], gain, (s_const, n), consts)


def norm2_phase(nc, a, ps, ident, z2T, h_dram):
    with Scope(nc) as ctx, nc.Block() as block:
        gain = ctx.enter_context(nc.sbuf_tensor("gain_ffn", [P, KD], F32))
        s_gain = ctx.sem("gain_ffn_loaded")
        def consts(sp):
            sp.dma_start(gain[:, :], a["g_ffn"]).then_inc(s_gain, 16)

        norm_rows(nc, "ffn", ctx, block, ps, ident, z2T, h_dram, gain, (s_gain, 16), consts)


def retention_phase(nc, a, ps, ident, zT, rT, s_rqk, s_rv):
    with Scope(nc) as ctx, nc.Block() as block:
        def sb(n, shape, dt=F32):
            return ctx.enter_context(nc.sbuf_tensor("ret_" + n, shape, dt))

        def sem(n):
            return ctx.sem("ret_" + n)

        W = sb("w", [P, KD, WR])
        zc = sb("z_tile", [P, KD, P])
        cosr, sinr = sb("cos", [P, NT + 1, 64]), sb("sin", [P, NT + 1, 64])
        maskT = sb("maskT", [P, RH, P])
        qdec = sb("q_decay", [P, RH, P])
        kdec = sb("k_decay", [P, RH])
        rot = sb("rotated", [P, 2 * RH, 64, 2])
        t1, t2 = sb("t1", [P, 2 * RH, 64]), sb("t2", [P, 2 * RH, 64])
        kd = sb("k_decayed", [P, RH, P])
        v = sb("v", [P, RH * RDV])
        qT, qdT, kT, sT = (sb(n, [P, RH, P]) for n in ("qT", "qdT", "kT", "sT"))
        state = sb("state", [P, RH, RDV])
        rn = sb("normed", [P, RH, RDV])
        junk = sb("junk", [P, RDV])
        st = sb("st", [P, 4, RH])

        s_w, s_tab = [sem("w_loaded_qk"), sem("w_loaded_v")], sem("tables_loaded")
        state_zero, inv, sq_step = sem("state_zero"), sem("inverse"), sem("square_step")
        z_ready, qk_ready, v_ready = sem("z_tile_ready"), sem("qk_projected"), sem("v_projected")
        v_kept = sem("v_kept")
        chain, rotated, k_dec_ready = sem("chain"), sem("rotated_ready"), sem("kd_ready")
        qk_turned, qk_kept = sem("qk_turned"), sem("qk_kept")
        s_ready, s_kept = sem("scores_ready"), sem("scores_kept")
        out_ready, state_ready, state_kept = sem("out_ready"), sem("state_update_ready"), sem("state_kept")
        squares, mean, root, normed = sem("squares"), sem("mean"), sem("root"), sem("normed_ready")
        turned, kept, stored = sem("out_turned"), sem("out_kept"), sem("stored")
        ACT_V, PROJ = 3, WR // BANK
        SCALE = float(RDK) ** -0.5
        log_decay = np.log(1.0 - 2.0 ** (-5.0 - np.arange(RH)))
        g_chunk = [float(np.exp(x * P)) for x in log_decay]
        NLINK = 5

        @block.sync
        def _(sp):
            sp.dma_start(W[:, :, 0:2 * BANK], a["w_ret"][:, :, 0:2 * BANK]).then_inc(s_w[0], 16)
            for d_, s_ in ((cosr, "ret_cos"), (sinr, "ret_sin")):
                sp.dma_start(d_[:, :, :], a[s_].rearrange("t p f -> p t f")).then_inc(s_tab, 16)
            for d_, s_ in ((maskT, "ret_maskT"), (qdec, "ret_qdec")):
                sp.dma_start(d_[:, :, :], a[s_]).then_inc(s_tab, 16)
            sp.dma_start(kdec[:, :], a["ret_kdec"]).then_inc(s_tab, 16)
            sp.dma_start(W[:, :, 2 * BANK:WR], a["w_ret"][:, :, 2 * BANK:WR]).then_inc(s_w[1], 16)
            sp.wait_ge(state_kept, NT)
            sp.dma_start(a["o_ret_p"].rearrange("h k v -> k h v"), state[:, :, :]).then_inc(stored, 16)
            sp.wait_ge(stored, 16)

        @block.gpsimd
        def _(pool):
            def copy_tile(t):
                pool.wait_ge(v_ready, t)
                nc.gpsimd.tensor_copy(zc[:, :, :], zT[:, :, ds(t * P, P)]).then_inc(z_ready, 1)
            nc.gpsimd.memset(state[:, :, :], 0.0).then_inc(state_zero, 1)
            with pool.Fori(0, NT) as t:
                copy_tile(t)

        @block.tensor
        def _(pe):
            def project(t, rows, lhs):
                pe.wait_ge(rotated, t)
                for b in range(PROJ):
                    if b == 2:
                        pe.wait_ge(v_kept, t)
                    for c in range(KD):
                        last = nc.tensor.matmul(ps[0:rows, b, :], lhs(c), W[:, c, b * BANK:(b + 1) * BANK],
                                                start=(c == 0), stop=(c == KD - 1))
                    if b == 1:
                        last.then_inc(qk_ready, 1)
                last.then_inc(v_ready, 1)

            def tile_project(t):
                pe.wait_ge(z_ready, t + 1)
                project(t, P, lambda c: zc[:, c, :])

            def chunk(t):
                pe.wait_ge(rotated, t + 1)
                pe.wait_ge(normed, t)
                for i in range(2 * RH):
                    last = nc.tensor.transpose(ps[:, 4 + i // RH, (i % RH) * P:(i % RH + 1) * P],
                                               rot[:, i, :, :].rearrange("p f two -> p (f two)"), ident[:, :])
                last.then_inc(qk_turned, 1)
                pe.wait_ge(qk_kept, t + 1)
                pe.wait_ge(kept, t)
                for h in range(RH):
                    last = nc.tensor.matmul(ps[:, 6, h * P:(h + 1) * P], kT[:, h, :], qT[:, h, :],
                                            start=True, stop=True)
                last.then_inc(s_ready, 1)
                pe.wait_ge(s_kept, t + 1)
                pe.wait_ge(v_kept, t + 1)
                pe.wait_ge(state_kept, t)
                for h in range(RH):
                    o = ps[:, 4 + h // 2, (h % 2) * RDV:(h % 2 + 1) * RDV]
                    vh = v[:, h * RDV:(h + 1) * RDV]
                    nc.tensor.matmul(o, sT[:, h, :], vh, start=True, stop=False)
                    last = nc.tensor.matmul(o, qdT[:, h, :], state[:, h, :], start=False, stop=True)
                last.then_inc(out_ready, 1)
                pe.wait_ge(k_dec_ready, t + 1)
                for h in range(RH):
                    last = nc.tensor.matmul(ps[:, 6 + h // 2, (h % 2) * RDV:(h % 2 + 1) * RDV], kd[:, h, :],
                                            v[:, h * RDV:(h + 1) * RDV], start=True, stop=True)
                last.then_inc(state_ready, 1)

            def turn_out(t):
                pe.wait_ge(normed, t + 1)
                pe.wait_ge(state_kept, t + 1)
                for c in range(KD):
                    last = nc.tensor.transpose(ps[:, 6 + c // 4, (c % 4) * P:(c % 4 + 1) * P],
                                               rn[:, :, :].rearrange("p h e -> p (h e)")[:, c * P:(c + 1) * P],
                                               ident[:, :])
                last.then_inc(turned, 1)

            pe.wait_ge(s_w[0], 16)
            pe.wait_ge(s_w[1], 16)
            pe.wait_ge(state_zero, 1)
            tile_project(0)
            with pe.Fori(0, NT - 1) as t:
                chunk(t)
                tile_project(t + 1)
                turn_out(t)
            chunk(NT - 1)
            project(NT, NS, lambda c: zT[:, c, SEQ:T])
            turn_out(NT - 1)

        @block.vector
        def _(dve):
            def rotate(t, rows, out, base):
                dve.wait_ge(qk_ready, t + 1)
                dve.wait_ge(state_ready, t)
                x = ps[0:rows, 0:2, :].rearrange("p b (h f two) -> p (b h) f two", h=RH, two=2)
                cb = cosr[0:rows, ds(t, 1), :].to_broadcast([rows, 2 * RH, 64])
                sb_ = sinr[0:rows, ds(t, 1), :].to_broadcast([rows, 2 * RH, 64])
                link = Chain(dve, chain, base)
                u1, u2 = t1[0:rows], t2[0:rows]
                link(nc.vector.tensor_tensor(u1, x[:, :, :, 0], cb, ALU.mult))
                link(nc.vector.tensor_tensor(u2, x[:, :, :, 1], sb_, ALU.mult))
                link(nc.vector.tensor_tensor(out[:, :, :, 0], u1, u2, ALU.subtract))
                link(nc.vector.tensor_tensor(u1, x[:, :, :, 1], cb, ALU.mult))
                link(nc.vector.tensor_tensor(u2, x[:, :, :, 0], sb_, ALU.mult))
                nc.vector.tensor_tensor(out[:, :, :, 1], u1, u2, ALU.add).then_inc(rotated, 1)

            def tile_rotate(t):
                rotate(t, P, rot[:, :, :, :], t * NLINK)
                dve.wait_ge(rotated, t + 1)
                nc.vector.tensor_tensor(kd[:, :, :], rot[:, RH:, :, :].rearrange("p h f two -> p h (f two)"),
                                        kdec[:, :].unsqueeze(2).to_broadcast([P, RH, P]),
                                        ALU.mult).then_inc(k_dec_ready, 1)

            def chunk(t):
                dve.wait_ge(qk_turned, t + 1)
                q_ps = ps[:, 4, :].rearrange("p (h l) -> p h l", h=RH)
                nc.vector.tensor_copy(qT[:, :, :], q_ps)
                nc.vector.tensor_tensor(qdT[:, :, :], q_ps, qdec[:, :, :], ALU.mult)
                nc.vector.tensor_scalar(kT[:, :, :], ps[:, 5, :].rearrange("p (h l) -> p h l", h=RH), SCALE,
                                        None, ALU.mult).then_inc(qk_kept, 1)
                dve.wait_ge(s_ready, t + 1)
                nc.vector.tensor_tensor(sT[:, :, :], ps[:, 6, :].rearrange("p (h l) -> p h l", h=RH),
                                        maskT[:, :, :], ALU.mult).then_inc(s_kept, 1)
                dve.wait_ge(squares, t + 1)
                nc.vector.tensor_scalar(st[:, 1, :], st[:, 0, :], 1.0 / RDV, EPS, ALU.mult,
                                        ALU.add).then_inc(mean, 1)
                dve.wait_ge(root, t + 1)
                nc.vector.reciprocal(st[:, 3, :], st[:, 2, :]).then_inc(inv, 1)
                dve.wait_ge(state_ready, t + 1)
                for h in range(RH):
                    last = nc.vector.scalar_tensor_tensor(
                        out=state[:, h, :], in0=state[:, h, :], scalar=g_chunk[h],
                        in1=ps[:, 6 + h // 2, (h % 2) * RDV:(h % 2 + 1) * RDV], op0=ALU.mult, op1=ALU.add)
                last.then_inc(state_kept, 1)
                dve.wait_ge(inv, t + 1)
                dve.wait_ge(turned, t)
                nc.vector.tensor_tensor(rn[:, :, :], ps[:, 4:6, :].rearrange("p b (h e) -> p (b h) e", h=2),
                                        st[:, 3, :].unsqueeze(2).to_broadcast([P, RH, RDV]),
                                        ALU.mult).then_inc(normed, 1)

            dve.wait_ge(s_tab, 16 * 5)
            tile_rotate(0)
            with dve.Fori(0, NT - 1) as t:
                chunk(t)
                tile_rotate(t + 1)
            chunk(NT - 1)
            rotate(NT, NS, s_rqk[:, :].rearrange("p (h f two) -> p h f two", f=64, two=2), NT * NLINK)

        @block.scalar
        def _(act):
            def keep_v(t, rows, out):
                act.wait_ge(v_ready, t + 1)
                nc.scalar.activation(out, ps[0:rows, 2:4, :].rearrange("p b n -> p (b n)"),
                                     ACT.Copy).then_inc(v_kept, 1)

            def chunk(t):
                act.wait_ge(out_ready, t + 1)
                for h in range(RH):
                    if h:
                        act.wait_ge(sq_step, (RH - 1) * t + h)
                    ins = nc.scalar.activation(junk[:, :], ps[:, 4 + h // 2, (h % 2) * RDV:(h % 2 + 1) * RDV],
                                               ACT.Square, accum_out=st[:, 0, h:h + 1])
                    ins.then_inc(sq_step if h < RH - 1 else squares, 1)
                act.wait_ge(mean, t + 1)
                nc.scalar.activation(st[:, 2, :], st[:, 1, :], ACT.Sqrt).then_inc(root, 1)

            def keep_out(t):
                act.wait_ge(turned, t + 1)
                nc.scalar.activation(rT[:, :, ds(t * P, P)],
                                     ps[:, 6:8, :].rearrange("p b (c r) -> p (b c) r", r=P),
                                     ACT.Copy).then_inc(kept, 1)

            keep_v(0, P, v[:, :])
            with act.Fori(0, NT - 1) as t:
                chunk(t)
                act.wait_ge(state_ready, t + 1)
                keep_v(t + 1, P, v[:, :])
                keep_out(t)
            chunk(NT - 1)
            keep_v(NT, NS, s_rv[:, :])
            keep_out(NT - 1)


def attention_projection(nc, a, ps, ident, zT, QT, KT, VA, s_aqk, s_av):
    with Scope(nc) as ctx, nc.Block() as block:
        def sb(n, shape, dt=F32):
            return ctx.enter_context(nc.sbuf_tensor("ap_" + n, shape, dt))

        def sem(n):
            return ctx.sem("ap_" + n)

        W = sb("w", [P, KD, WA])
        zc = sb("z_tile", [P, KD, P])
        cosa, sina = sb("cos", [P, NT + 1, 8]), sb("sin", [P, NT + 1, 8])
        NG = 4 * AH
        qk = sb("qk", [P, NG, ADQ])
        u = sb("u", [P, 4, NG, 8])
        s_w, s_tab, z_ready = sem("w_loaded"), sem("tables_loaded"), sem("z_tile_ready")
        projected, copied, rotated = sem("projected"), sem("straight_part_kept"), sem("rotated")
        prods, v_kept, turned, kept = sem("products"), sem("v_kept"), sem("qk_turned"), sem("qk_kept")
        k_stored, v_stored = sem("k_rows_stored"), sem("v_rows_stored")

        @block.sync
        def _(sp):
            sp.dma_start(W[:, :, :], a["w_att"]).then_inc(s_w, 16)
            for d_, s_ in ((cosa, "att_cos"), (sina, "att_sin")):
                sp.dma_start(d_[:, :, :], a[s_].rearrange("t p f -> p t f")).then_inc(s_tab, 16)
            with sp.Fori(0, NT) as t:
                sp.wait_ge(rotated, t + 1)
                sp.dma_start(a["o_k_p"][ds(t * P, P), :], qk[:, NG // 2:, :]).then_inc(k_stored, 16)
            sp.wait_ge(rotated, NT + 1)
            sp.dma_start(a["o_k_s"], s_aqk[:, 512:1024]).then_inc(k_stored, 16)
            sp.wait_ge(v_kept, NT + 1)
            sp.dma_start(a["o_v_p"].rearrange("(t p) n -> p t n", p=P), VA[:, :, :]).then_inc(v_stored, 16)
            sp.dma_start(a["o_v_s"], s_av[:, :]).then_inc(v_stored, 16)
            sp.wait_ge(k_stored, 16 * (NT + 1))
            sp.wait_ge(v_stored, 32)

        @block.gpsimd
        def _(pool):
            with pool.Fori(0, NT) as t:
                pool.wait_ge(projected, t)
                nc.gpsimd.tensor_copy(zc[:, :, :], zT[:, :, ds(t * P, P)]).then_inc(z_ready, 1)

        @block.tensor
        def _(pe):
            def project(t, rows, lhs):
                pe.wait_ge(rotated, t)
                pe.wait_ge(v_kept, t)
                for b in range(3):
                    for c in range(KD):
                        last = nc.tensor.matmul(ps[0:rows, b, :], lhs(c), W[:, c, b * BANK:(b + 1) * BANK],
                                                start=(c == 0), stop=(c == KD - 1))
                last.then_inc(projected, 1)

            pe.wait_ge(s_w, 16)
            with pe.Fori(0, NT) as t:
                pe.wait_ge(z_ready, t + 1)
                project(t, P, lambda c: zc[:, c, :])
                pe.wait_ge(rotated, t + 1)
                pe.wait_ge(kept, t)
                for i in range(2 * AH):
                    last = nc.tensor.transpose(ps[:, 4 + i // AH, (i % AH) * P:(i % AH + 1) * P],
                                               qk[:, 2 * i:2 * i + 2, :].rearrange("p c d -> p (c d)"), ident[:, :])
                last.then_inc(turned, 1)
            project(NT, NS, lambda c: zT[:, c, SEQ:T])

        @block.vector
        def _(dve):
            def rotate(t, rows, out, x):
                dve.wait_ge(projected, t + 1)
                dve.wait_ge(copied, t + 1)
                cb = cosa[0:rows, ds(t, 1), :].to_broadcast([rows, NG, 8])
                sb_ = sina[0:rows, ds(t, 1), :].to_broadcast([rows, NG, 8])
                x1, x2 = x[:, :, 0:8], x[:, :, 8:16]
                w = u[0:rows]
                nc.vector.tensor_tensor(w[:, 0], x1, cb, ALU.mult)
                nc.vector.tensor_tensor(w[:, 1], x2, sb_, ALU.mult)
                nc.vector.tensor_tensor(w[:, 2], x2, cb, ALU.mult)
                nc.vector.tensor_tensor(w[:, 3], x1, sb_, ALU.mult).then_inc(prods, 1)
                dve.wait_ge(prods, t + 1)
                nc.vector.tensor_tensor(out[:, :, 0:8], w[:, 0], w[:, 1], ALU.subtract)
                nc.vector.tensor_tensor(out[:, :, 8:16], w[:, 2], w[:, 3], ALU.add).then_inc(rotated, 1)

            dve.wait_ge(s_tab, 32)
            with dve.Fori(0, NT) as t:
                rotate(t, P, qk[:, :, :], ps[:, 0:2, :].rearrange("p b (g d) -> p (b g) d", d=ADQ))
                dve.wait_ge(turned, t + 1)
                nc.vector.tensor_copy(QT[:, :, ds(t * P, P)], ps[:, 4, :].rearrange("p (h l) -> p h l", h=AH))
                nc.vector.tensor_copy(KT[:, :, ds(t * P, P)],
                                      ps[:, 5, :].rearrange("p (h l) -> p h l", h=AH)).then_inc(kept, 1)
            rotate(NT, NS, s_aqk[:, :].rearrange("p (g d) -> p g d", d=ADQ),
                   ps[0:NS, 0:2, :].rearrange("p b (g d) -> p (b g) d", d=ADQ))

        @block.scalar
        def _(act):
            def keep(t, rows, out, vout):
                act.wait_ge(projected, t + 1)
                act.wait_ge(turned, t)
                act.wait_ge(k_stored, 16 * t)
                x = ps[0:rows, 0:2, :].rearrange("p b (g d) -> p (b g) d", d=ADQ)
                nc.scalar.activation(out[:, :, ROT:ADQ], x[:, :, ROT:ADQ], ACT.Copy).then_inc(copied, 1)
                nc.scalar.activation(vout, ps[0:rows, 2, :], ACT.Copy).then_inc(v_kept, 1)

            with act.Fori(0, NT) as t:
                keep(t, P, qk[:, :, :], VA[:, ds(t, 1), :].rearrange("p o n -> p (o n)"))
            keep(NT, NS, s_aqk[:, :].rearrange("p (g d) -> p g d", d=ADQ), s_av[:, :])


def attention_phase(nc, a, ps, ident, QT, KT, VA, aT, lam):
    with Scope(nc) as ctx, nc.Block() as block:
        def sb(n, shape, dt=F32):
            return ctx.enter_context(nc.sbuf_tensor("at_" + n, shape, dt))

        def sem(n):
            return ctx.sem("at_" + n)

        mask = sb("mask", [P, P])
        pr = sb("probs", [P, 2, 2, SEQ])
        wT = sb("weights_T", [P, 2, SEQ])
        mx = sb("max", [P, 2, 4])
        sm = sb("sums", [P, 2, 4])
        o, sq, on = sb("out", [P, AH, ADV]), sb("squares", [P, AH, ADV]), sb("normed", [P, AH, ADV])
        st = sb("st", [P, 4, AH])
        gain = sb("gain", [P, 1])
        s_tab = sem("tables_loaded")
        scored, maxed, exped, combined = sem("scores_ready"), sem("max_ready"), sem("exp_done"), sem("weights_ready")
        turned, kept, summed = sem("weights_turned"), sem("weights_kept"), sem("values_summed")
        chain, out_kept, mean, root = sem("chain"), sem("out_kept"), sem("mean"), sem("root")
        normed, out_turned, out_stored = sem("normed"), sem("out_turned"), sem("out_columns_kept")
        exp_a = sem("exp_first_map")
        SC = float(ADQ) ** -0.5
        steps = [(t, h) for t in range(NT) for h in range(AH)]
        N = len(steps)

        def score_ps(nk):
            return ps[:, 0:4, :].rearrange("p (c b) n -> p c (b n)", c=2)[:, :, 0:nk]

        @block.sync
        def _(sp):
            sp.dma_start(mask[:, :], a["att_mask"]).then_inc(s_tab, 16)
            sp.dma_start(gain[:, :], a["g_subln"]).then_inc(s_tab, 16)

        @block.tensor
        def _(pe):
            def scores(s):
                t, h = steps[s]
                nk = (t + 1) * P
                if s:
                    pe.wait_ge(exped, s)
                for c in range(2):
                    for b in range(0, nk, BANK):
                        w = min(BANK, nk - b)
                        last = nc.tensor.matmul(ps[:, 2 * c + b // BANK, 0:w],
                                                QT[c * ADQ:(c + 1) * ADQ, h, t * P:(t + 1) * P],
                                                KT[c * ADQ:(c + 1) * ADQ, h, b:b + w], start=True, stop=True)
                last.then_inc(scored, 1)

            def turn_tile(t):
                pe.wait_ge(normed, t + 1)
                if t:
                    pe.wait_ge(out_stored, t)
                for h in range(AH):
                    last = nc.tensor.transpose(ps[:, 7, h * P:(h + 1) * P], on[:, h, :], ident[:, :])
                last.then_inc(out_turned, 1)

            scores(0)
            for s, (t, h) in enumerate(steps):
                if s + 1 < N:
                    scores(s + 1)
                pe.wait_ge(combined, s + 1)
                if s:
                    pe.wait_ge(kept, s)
                for b in range(t + 1):
                    last = nc.tensor.transpose(ps[:, 4 + b // 4, (b % 4) * P:(b % 4 + 1) * P],
                                               pr[:, s % 2, 0, b * P:(b + 1) * P], ident[:, :])
                last.then_inc(turned, 1)
                if t and h == 2:
                    turn_tile(t - 1)
                pe.wait_ge(kept, s + 1)
                if h == 0 and t:
                    pe.wait_ge(out_kept, t)
                for b in range(t + 1):
                    last = nc.tensor.matmul(ps[:, 6, h * P:(h + 1) * P], wT[:, s % 2, b * P:(b + 1) * P],
                                            VA[:, b, h * ADV:(h + 1) * ADV], start=(b == 0), stop=(b == t))
                last.then_inc(summed, 1)
            turn_tile(NT - 1)

        @block.vector
        def _(dve):
            link = Chain(dve, chain)

            def maximum(s):
                t, h = steps[s]
                nk = (t + 1) * P
                dve.wait_ge(scored, s + 1)
                sc = score_ps(nk)
                diag = sc[:, :, t * P:nk]
                link(nc.vector.tensor_tensor(diag, diag, mask[:, :].unsqueeze(1).to_broadcast([P, 2, P]), ALU.add))
                m = mx[:, s % 2, :]
                link(nc.vector.tensor_reduce(m[:, 0:2], sc, AX_X, ALU.max))
                nc.vector.tensor_scalar(m[:, 2:4], m[:, 0:2], -SC, None, ALU.mult).then_inc(maxed, 1)

            def combine(s):
                t, h = steps[s]
                nk = (t + 1) * P
                dve.wait_ge(exped, s + 1)
                w = sm[:, s % 2, :]
                link(nc.vector.reciprocal(w[:, 2:4], w[:, 0:2]))
                p0, p1 = pr[:, s % 2, 0, 0:nk], pr[:, s % 2, 1, 0:nk]
                link(nc.vector.tensor_scalar(p1, p1, w[:, 3:4], lam[:, 0:1], ALU.mult, ALU.mult))
                nc.vector.scalar_tensor_tensor(out=p0, in0=p0, scalar=w[:, 2:3], in1=p1, op0=ALU.mult,
                                               op1=ALU.subtract).then_inc(combined, 1)

            def norm_tile(t):
                dve.wait_ge(out_kept, t + 1)
                link(nc.vector.tensor_tensor(sq[:, :, :], o[:, :, :], o[:, :, :], ALU.mult))
                link(nc.vector.tensor_reduce(st[:, 0, :], sq[:, :, :], AX_X, ALU.add))
                nc.vector.tensor_scalar(st[:, 1, :], st[:, 0, :], 1.0 / ADV, SUB_EPS, ALU.mult,
                                        ALU.add).then_inc(mean, 1)

            def scale_tile(t):
                dve.wait_ge(root, t + 1)
                if t:
                    dve.wait_ge(out_turned, t)
                link(nc.vector.reciprocal(st[:, 3, :], st[:, 2, :]))
                nc.vector.tensor_tensor(on[:, :, :], o[:, :, :],
                                        st[:, 3, :].unsqueeze(2).to_broadcast([P, AH, ADV]),
                                        ALU.mult).then_inc(normed, 1)

            def keep_tile(t):
                dve.wait_ge(out_turned, t + 1)
                nc.vector.tensor_scalar(aT[:, :, t * P:(t + 1) * P], ps[:, 7, :].rearrange("p (h l) -> p h l", h=AH),
                                        gain[:, 0:1], 1.0 - LAM_INIT, ALU.mult, ALU.mult).then_inc(out_stored, 1)

            dve.wait_ge(s_tab, 32)
            maximum(0)
            for s, (t, h) in enumerate(steps):
                if s + 1 < N:
                    maximum(s + 1)
                combine(s)
                if t and h == 0:
                    norm_tile(t - 1)
                if t and h == 1:
                    scale_tile(t - 1)
                if t and h == 3:
                    keep_tile(t - 1)
            norm_tile(NT - 1)
            scale_tile(NT - 1)
            keep_tile(NT - 1)

        @block.scalar
        def _(act):
            def exps(s):
                t, h = steps[s]
                nk = (t + 1) * P
                act.wait_ge(maxed, s + 1)
                if s >= 2:
                    act.wait_ge(turned, s - 1)
                for c in range(2):
                    nc.scalar.activation(pr[:, s % 2, c, 0:nk], score_ps(nk)[:, c, :], ACT.Exp,
                                         bias=mx[:, s % 2, 2 + c:3 + c], scale=SC,
                                         accum_out=sm[:, s % 2, c:c + 1]).then_inc(exped if c else exp_a, 1)

            def keep_out(t):
                act.wait_ge(summed, AH * (t + 1))
                if t:
                    act.wait_ge(normed, t)
                nc.scalar.activation(o[:, :, :].rearrange("p h e -> p (h e)"), ps[:, 6, :],
                                     ACT.Copy).then_inc(out_kept, 1)

            def square_root(t):
                act.wait_ge(mean, t + 1)
                nc.scalar.activation(st[:, 2, :], st[:, 1, :], ACT.Sqrt).then_inc(root, 1)

            exps(0)
            for s, (t, h) in enumerate(steps):
                if s + 1 < N:
                    exps(s + 1)
                if t and h == 0:
                    keep_out(t - 1)
                act.wait_ge(turned, s + 1)
                nk = (t + 1) * P
                if s >= 2:
                    act.wait_ge(summed, s - 1)
                nc.scalar.activation(wT[:, s % 2, 0:nk],
                                     ps[:, 4:6, :].rearrange("p b n -> p (b n)")[:, 0:nk],
                                     ACT.Copy).then_inc(kept, 1)
                if t and h == 0:
                    square_root(t - 1)
            keep_out(NT - 1)
            square_root(NT - 1)


def sample_phase(nc, a, ps, ident, s_rqk, s_rv, s_aqk, s_av, rT, aT, lam):
    J = NS * RH
    R = 2 * J
    with Scope(nc) as ctx, nc.Block() as block:
        def sb(n, shape, dt=F32):
            return ctx.enter_context(nc.sbuf_tensor("sa_" + n, shape, dt))

        def sem(n):
            return ctx.sem("sa_" + n)

        state = sb("state", [P, J, RDV])
        qz = sb("q_padded", [P, J * J])
        km = sb("k_masked", [NS, 2, RH * RDK])
        rn = sb("ret_normed", [J, RDV])
        junk = sb("junk", [R, BANK])
        st = sb("st", [R, 8])
        qb = sb("att_q_padded", [P, J * R])
        kT = sb("att_kT", [P, AH, NS])
        kpg = sb("key_pages", [P, 2, NPAGE, AH, PAGE])
        vpg = sb("value_pages", [P, 2, NPAGE, AH * ADV])
        sc = sb("scores", [R, PAST + 1])
        pr = sb("probs", [R, PAST + 1])
        pz = sb("probs_padded", [P, NPAGE, NS * (R + 8)])
        pn, pnT = sb("probs_self", [R, NS]), sb("probs_self_T", [NS, R])
        sel = sb("selectors", [R, 2 + NS + AH])
        o2, o3 = sb("out_rows", [R, AH, ADV]), sb("out", [NS, AH, ADV])
        on, osq = sb("out_normed", [NS, AH, ADV]), sb("out_squares", [NS, AH, ADV])
        ost = sb("out_st", [NS, 4, AH])
        gain = sb("gain", [P, 1])
        pt = sb("page_table", [1, NS * NPAGE], I32)
        s_tab, s_pt, s_state = sem("tables_loaded"), sem("page_table_loaded"), sem("states_loaded")
        k_in, v_in = [sem(f"key_pages{u}") for u in range(2)], [sem(f"value_pages{u}") for u in range(2)]
        zeroed, q_turned, q_kept = sem("padding_zeroed"), sem("q_turned"), sem("q_kept")
        kv_ready, state_new, stored = sem("outer_products"), sem("state_new"), sem("stored")
        r_out, r_sq, r_mean, r_root, r_norm = (sem("ret_" + n) for n in ("out", "squares", "mean", "root", "normed"))
        r_turned, r_kept = sem("ret_turned"), sem("ret_kept")
        km_ready, scored, s_used, s_evac = sem("k_masked"), sem("scored"), sem("keys_used"), sem("scores_kept")
        maxed, exped, p_turned, p_kept, v_used, summed = (sem(n) for n in (
            "maxed", "exped", "probs_turned", "probs_kept", "values_used", "values_summed"))
        o2_ready, picked, o3_ready, a_mean, a_root, a_norm, a_turned, a_kept = (sem(n) for n in (
            "rows_weighted", "rows_picked", "out_kept", "out_mean", "out_root", "out_normed", "out_turned",
            "out_columns_kept"))
        self_ready, self_turned = sem("self_ready"), sem("self_turned")
        chain = sem("chain")
        SCALE, SC = float(RDK) ** -0.5, float(ADQ) ** -0.5
        gamma = [float(np.exp(np.log(1.0 - 2.0 ** (-5.0 - h)))) for h in range(RH)]

        @block.sync
        def _(sp):
            sp.dma_start(pt[:, :], a["page_table"]).then_inc(s_pt, 16)
            sp.dma_start(sel[:, :], a["sel"]).then_inc(s_tab, 16)
            sp.dma_start(gain[:, :], a["g_subln"]).then_inc(s_tab, 16)
            sp.wait_ge(s_pt, 16)
            for b in range(NS):
                u = b % 2
                for pg in range(NPAGE):
                    n = b * NPAGE + pg
                    pid = sp.value_load(pt[0:1, n:n + 1], min_val=0, max_val=POOL - 1)
                    if b >= 2 and pg == 0:
                        sp.wait_ge(s_used, b - 1)
                    sp.dma_start(kpg[:, u, pg, :, :], a["cache_kT"][ds(pid, 1)].rearrange("o h p n -> p (o h) n")
                                 ).then_inc(k_in[u], 16)

        @block.gpsimd
        def _(pool):
            nc.gpsimd.memset(qz[:, :], 0.0).then_inc(zeroed, 1)
            nc.gpsimd.memset(qb[:, :], 0.0).then_inc(zeroed, 1)
            nc.gpsimd.memset(pz[:, :, :], 0.0).then_inc(zeroed, 1)
            pool.wait_ge(s_pt, 16)
            for b in range(NS):
                u = b % 2
                for pg in range(NPAGE):
                    n = b * NPAGE + pg
                    pid = pool.value_load(pt[0:1, n:n + 1], min_val=0, max_val=POOL - 1)
                    if b >= 2 and pg == 0:
                        pool.wait_ge(v_used, b - 1)
                    pool.dma_start(vpg[:, u, pg, :], a["cache_v"][ds(pid, 1)].rearrange("o p n -> p (o n)")
                                   ).then_inc(v_in[u], 16)

        @block.scalar
        def _(act):
            act.dma_start(state[:, :, :], a["state"].rearrange("b h k v -> k (b h) v")).then_inc(s_state, 16)
            act.wait_ge(r_out, 1)
            nc.scalar.activation(junk[0:J, 0:RDV], ps[0:J, 4, 0:RDV], ACT.Square,
                                 accum_out=st[0:J, 0:1]).then_inc(r_sq, 1)
            act.wait_ge(r_mean, 1)
            nc.scalar.activation(st[0:J, 2:3], st[0:J, 1:2], ACT.Sqrt).then_inc(r_root, 1)
            act.wait_ge(maxed, 1)
            nc.scalar.activation(pr[:, :], sc[:, :], ACT.Exp, bias=st[:, 5:6], scale=SC,
                                 accum_out=st[:, 6:7]).then_inc(exped, 1)
            act.wait_ge(a_mean, 1)
            nc.scalar.activation(ost[:, 2, :], ost[:, 1, :], ACT.Sqrt).then_inc(a_root, 1)
            act.wait_ge(state_new, NS)
            act.dma_start(a["o_ret_s"].rearrange("b h k v -> k (b h) v"), state[:, :, :]).then_inc(stored, 16)
            act.wait_ge(stored, 16)

        @block.tensor
        def _(pe):
            for bank, src, off in ((0, s_rqk, 0), (1, s_aqk, 0), (2, s_aqk, AH * 2 * ADQ)):
                for h in range(RH):
                    last = nc.tensor.transpose(ps[:, bank, h * NS:(h + 1) * NS],
                                               src[:, off + h * P:off + (h + 1) * P], ident[0:NS, 0:NS])
            last.then_inc(q_turned, 1)
            pe.wait_ge(q_kept, 1)
            for b in range(NS):
                pe.wait_ge(km_ready, b + 1)
                if b >= 2:
                    pe.wait_ge(state_new, b - 1)
                for h in range(RH):
                    last = nc.tensor.matmul(ps[:, 2 * (b % 2) + h // 2, (h % 2) * RDV:(h % 2 + 1) * RDV],
                                            km[:, b % 2, h * RDK:(h + 1) * RDK], s_rv[:, h * RDV:(h + 1) * RDV],
                                            start=True, stop=True)
                last.then_inc(kv_ready, 1)
            pe.wait_ge(state_new, NS)
            for j in range(J):
                last = nc.tensor.matmul(ps[0:J, 4, 0:RDV], qz[:, j * J:(j + 1) * J], state[:, j, :],
                                        start=(j == 0), stop=(j == J - 1))
            last.then_inc(r_out, 1)
            for b in range(NS):
                pe.wait_ge(k_in[b % 2], 16 * NPAGE * (b // 2 + 1))
                for h in range(AH):
                    j = b * AH + h
                    last = nc.tensor.matmul(ps[0:R, 5, :], qb[:, j * R:(j + 1) * R], kpg[:, b % 2, :, h, :],
                                            start=(j == 0), stop=(j == J - 1))
                last.then_inc(s_used, 1)
            for b in range(NS):
                for h in range(AH):
                    j = b * AH + h
                    last = nc.tensor.matmul(ps[0:R, 6, 0:1], qb[:, j * R:(j + 1) * R], kT[:, h, b:b + 1],
                                            start=(j == 0), stop=(j == J - 1))
            last.then_inc(scored, 1)
            pe.wait_ge(r_norm, 1)
            for half in range(2):
                last = nc.tensor.transpose(ps[:, 7, half * J:(half + 1) * J], rn[:, half * P:(half + 1) * P],
                                           ident[0:J, 0:J])
            last.then_inc(r_turned, 1)
            pe.wait_ge(exped, 1)
            for pg in range(NPAGE):
                last = nc.tensor.transpose(ps[:, 0, pg * R:(pg + 1) * R], pr[:, pg * PAGE:(pg + 1) * PAGE],
                                           ident[0:R, 0:R])
            last.then_inc(p_turned, 1)
            pe.wait_ge(self_ready, 1)
            nc.tensor.transpose(ps[0:NS, 1, 0:R], pn[:, :], ident[0:R, 0:R]).then_inc(self_turned, 1)
            pe.wait_ge(p_kept, 2)
            for b in range(NS):
                pe.wait_ge(v_in[b % 2], 16 * NPAGE * (b // 2 + 1))
                for pg in range(NPAGE):
                    last = nc.tensor.matmul(ps[0:R, 3, :], pz[:, pg, b * R:(b + 1) * R], vpg[:, b % 2, pg, :],
                                            start=(b == 0 and pg == 0), stop=False)
                last.then_inc(v_used, 1)
            nc.tensor.matmul(ps[0:R, 3, :], pnT[:, :], s_av[:, :], start=False, stop=True).then_inc(summed, 1)
            pe.wait_ge(o2_ready, 1)
            nc.tensor.matmul(ps[0:NS, 2, :], sel[:, 2:2 + NS], o2[:, :, :].rearrange("p h e -> p (h e)"),
                             start=True, stop=True).then_inc(picked, 1)
            pe.wait_ge(a_norm, 1)
            pe.wait_ge(p_kept, 2)
            for h in range(AH):
                last = nc.tensor.transpose(ps[:, 4, h * NS:(h + 1) * NS], on[:, h, :], ident[0:NS, 0:NS])
            last.then_inc(a_turned, 1)

        @block.vector
        def _(dve):
            link = Chain(dve, chain)
            def mask_k(b):
                if b >= 2:
                    dve.wait_ge(kv_ready, b - 1)
                nc.vector.tensor_scalar(km[:, b % 2, :], s_rqk[:, RH * RDK:], ident[0:NS, b:b + 1], SCALE,
                                        ALU.mult, ALU.mult).then_inc(km_ready, 1)

            mask_k(0)
            mask_k(1)
            dve.wait_ge(zeroed, 3)
            dve.wait_ge(q_turned, 1)
            by_head = "p (h b) -> p b h"
            nc.vector.tensor_copy(qz[:, 0:J * J:J + 1].rearrange("p (b h) -> p b h", b=NS),
                                  ps[:, 0, 0:J].rearrange(by_head, b=NS))
            for c in range(2):
                rows = slice(c * ADQ, (c + 1) * ADQ)
                nc.vector.tensor_copy(qb[rows, c:J * R:R + 2].rearrange("p (b h) -> p b h", b=NS),
                                      ps[rows, 1, 0:J].rearrange(by_head, b=NS))
            nc.vector.tensor_copy(kT[:, :, :], ps[:, 2, 0:J].rearrange("p (h b) -> p h b", b=NS)).then_inc(q_kept, 1)
            dve.wait_ge(s_state, 16)
            for b in range(NS):
                dve.wait_ge(kv_ready, b + 1)
                if b + 2 < NS:
                    mask_k(b + 2)
                for h in range(RH):
                    j = b * RH + h
                    last = nc.vector.scalar_tensor_tensor(
                        out=state[:, j, :], in0=state[:, j, :], scalar=gamma[h],
                        in1=ps[:, 2 * (b % 2) + h // 2, (h % 2) * RDV:(h % 2 + 1) * RDV],
                        op0=ALU.mult, op1=ALU.add)
                last.then_inc(state_new, 1)
            dve.wait_ge(r_sq, 1)
            nc.vector.tensor_scalar(st[0:J, 1:2], st[0:J, 0:1], 1.0 / RDV, EPS, ALU.mult, ALU.add).then_inc(r_mean, 1)
            dve.wait_ge(r_root, 1)
            link(nc.vector.reciprocal(st[0:J, 3:4], st[0:J, 2:3]))
            nc.vector.tensor_scalar(rn[:, :], ps[0:J, 4, 0:RDV], st[0:J, 3:4], None, ALU.mult).then_inc(r_norm, 1)
            dve.wait_ge(scored, 1)
            nc.vector.tensor_copy(sc[:, 0:PAST], ps[0:R, 5, :])
            link(nc.vector.tensor_copy(sc[:, PAST:], ps[0:R, 6, 0:1]))
            link(nc.vector.tensor_reduce(st[:, 4:5], sc[:, :], AX_X, ALU.max))
            nc.vector.tensor_scalar(st[:, 5:6], st[:, 4:5], -SC, None, ALU.mult).then_inc(maxed, 1)
            dve.wait_ge(r_turned, 1)
            for half in range(2):
                last = nc.vector.tensor_copy(rT[:, half:KD:2, SEQ:T],
                                             ps[:, 7, half * J:(half + 1) * J].rearrange("p (b h) -> p h b", b=NS))
            last.then_inc(r_kept, 1)
            dve.wait_ge(exped, 1)
            dve.wait_ge(s_tab, 32)
            nc.vector.tensor_scalar(pn[:, :], sel[:, 2:2 + NS], pr[:, PAST:], None, ALU.mult).then_inc(self_ready, 1)
            link(nc.vector.reciprocal(st[:, 7:8], st[:, 6:7]))
            link(nc.vector.scalar_tensor_tensor(out=st[:, 4:5], in0=sel[:, 1:2], scalar=lam[0:R, 0:1],
                                                in1=sel[:, 0:1], op0=ALU.mult, op1=ALU.subtract))
            link(nc.vector.tensor_scalar(st[:, 5:6], st[:, 4:5], st[:, 7:8], -1.0, ALU.mult, ALU.mult))
            dve.wait_ge(p_turned, 1)
            for pg in range(NPAGE):
                last = nc.vector.tensor_copy(
                    pz[:, pg, :].rearrange("p (b w) -> p b w", b=NS)[:, :, 0:8],
                    ps[:, 0, pg * R:(pg + 1) * R].rearrange("p (b w) -> p b w", b=NS))
            last.then_inc(p_kept, 1)
            dve.wait_ge(self_turned, 1)
            nc.vector.tensor_copy(pnT[:, :], ps[0:NS, 1, 0:R]).then_inc(p_kept, 1)
            dve.wait_ge(summed, 1)
            nc.vector.scalar_tensor_tensor(
                out=o2[:, :, :], in0=ps[0:R, 3, :].rearrange("p (h e) -> p h e", h=AH), scalar=st[:, 5:6],
                in1=sel[:, 2 + NS:].unsqueeze(2).to_broadcast([R, AH, ADV]), op0=ALU.mult,
                op1=ALU.mult).then_inc(o2_ready, 1)
            dve.wait_ge(picked, 1)
            link(nc.vector.tensor_copy(o3[:, :, :], ps[0:NS, 2, :].rearrange("p (h e) -> p h e", h=AH)))
            link(nc.vector.tensor_tensor(osq[:, :, :], o3[:, :, :], o3[:, :, :], ALU.mult))
            link(nc.vector.tensor_reduce(ost[:, 0, :], osq[:, :, :], AX_X, ALU.add))
            nc.vector.tensor_scalar(ost[:, 1, :], ost[:, 0, :], 1.0 / ADV, SUB_EPS, ALU.mult, ALU.add).then_inc(a_mean, 1)
            dve.wait_ge(a_root, 1)
            link(nc.vector.reciprocal(ost[:, 3, :], ost[:, 2, :]))
            nc.vector.tensor_tensor(on[:, :, :], o3[:, :, :], ost[:, 3, :].unsqueeze(2).to_broadcast([NS, AH, ADV]),
                                    ALU.mult).then_inc(a_norm, 1)
            dve.wait_ge(a_turned, 1)
            nc.vector.tensor_scalar(aT[:, :, SEQ:T], ps[:, 4, 0:J].rearrange("p (h b) -> p h b", b=NS),
                                    gain[:, 0:1], 1.0 - LAM_INIT, ALU.mult, ALU.mult).then_inc(a_kept, 1)


def merge_phase(nc, a, ps, zT, rT, aT, mT):
    NW = 2 * KD + KD + AH
    with Scope(nc) as ctx, nc.Block() as block:
        w = ctx.enter_context(nc.sbuf_tensor("mg_w", [P, 2, NW, P], F32))
        sg = ctx.enter_context(nc.sbuf_tensor("mg_gates", [P, 2, 2, TB], F32))
        pd = ctx.enter_context(nc.sbuf_tensor("mg_products", [P, 2, 2, TB], F32))

        def sem(n):
            return ctx.sem("mg_" + n)

        w_in, w_used = [sem(f"w_loaded{u}") for u in range(2)], [sem(f"w_used{u}") for u in range(2)]
        ready, gated, mult, merged = ([sem(f"{n}{s}") for s in range(2)] for n in
                                      ("products_ready", "gates_ready", "gated", "merged"))
        steps = [(u, b) for u in range(2) for b in range(3)]

        @block.sync
        def _(sp):
            with sp.Fori(0, KD // 2) as it:
                for u in range(2):
                    sp.wait_ge(w_used[u], it)
                    sp.dma_start(w[:, u, :, :], a["w_merge"][ds(2 * it + u, 1)].rearrange("o p k n -> p (o k) n")
                                 ).then_inc(w_in[u], 16)

        @block.tensor
        def _(pe):
            with pe.Fori(0, KD // 2) as it:
                for k, (u, b) in enumerate(steps):
                    s, lo, hi = k % 2, *BLOCKS[b]
                    if b == 0:
                        pe.wait_ge(w_in[u], 16 * it + 16)
                    pe.wait_ge(merged[s], 3 * it + k // 2)
                    n = 0
                    for bank, x, cnt in ((0, zT, KD), (1, zT, KD), (2, rT, KD), (3, aT, AH)):
                        for c in range(cnt):
                            last = nc.tensor.matmul(ps[:, 4 * s + bank, 0:TB], w[:, u, n, :], x[:, c, lo:hi],
                                                    start=(c == 0), stop=(c == cnt - 1))
                            n += 1
                    last.then_inc(ready[s], 1)
                    if b == 2:
                        pe.wait_ge(ready[s], 3 * it + k // 2 + 1)
                        pe.sem_inc(w_used[u], 1)

        @block.scalar
        def _(act):
            with act.Fori(0, KD // 2) as it:
                for k in range(6):
                    s = k % 2
                    act.wait_ge(ready[s], 3 * it + k // 2 + 1)
                    act.wait_ge(merged[s], 3 * it + k // 2)
                    nc.scalar.activation(sg[:, s, :, :], ps[:, 4 * s:4 * s + 2, 0:TB],
                                         ACT.Sigmoid).then_inc(gated[s], 1)

        @block.vector
        def _(dve):
            with dve.Fori(0, KD // 2) as it:
                for k, (u, b) in enumerate(steps):
                    s, lo, hi = k % 2, *BLOCKS[b]
                    n = 3 * it + k // 2
                    dve.wait_ge(gated[s], n + 1)
                    nc.vector.tensor_tensor(pd[:, s, :, :], sg[:, s, :, :], ps[:, 4 * s + 2:4 * s + 4, 0:TB],
                                            ALU.mult).then_inc(mult[s], 1)
                    dve.wait_ge(mult[s], n + 1)
                    nc.vector.tensor_tensor(mT[:, ds(2 * it + u, 1), lo:hi], pd[:, s, 0:1, :], pd[:, s, 1:2, :],
                                            ALU.add).then_inc(merged[s], 1)


def residual_phase(nc, a, ps, mT, h_dram):
    with Scope(nc) as ctx, nc.Block() as block:
        w = ctx.enter_context(nc.sbuf_tensor("rs_w", [P, KD, D], F32))
        mc = ctx.enter_context(nc.sbuf_tensor("rs_m_tile", [P, 2, KD, P], F32))
        x = ctx.enter_context(nc.sbuf_tensor("rs_x", [P, 2, D], F32))
        h = ctx.enter_context(nc.sbuf_tensor("rs_h", [P, 2, D], F32))

        def sem(n):
            return ctx.sem("rs_" + n)

        s_w = sem("w_loaded")
        m_in, x_in, ready, added, out = ([sem(f"{n}{u}") for u in range(2)] for n in
                                         ("m_tile_ready", "x_loaded", "product_ready", "added", "stored"))

        def over_tiles(eng, step):
            with eng.Fori(0, NT // 2) as it:
                for u in range(2):
                    step(it, u, P)
            step(NT // 2, 0, NS)

        @block.sync
        def _(sp):
            sp.dma_start(w[:, :, :], a["w_out"]).then_inc(s_w, 16)

            def load(it, u, rows):
                sp.wait_ge(added[u], it)
                sp.dma_start(x[0:rows, u, :], a["x"][ds((2 * it + u) * P, rows), :]).then_inc(x_in[u], 16)
            over_tiles(sp, load)

        @block.scalar
        def _(act):
            def store(it, u, rows):
                act.wait_ge(added[u], it + 1)
                act.dma_start(h_dram[ds((2 * it + u) * P, rows), :], h[0:rows, u, :]).then_inc(out[u], 16)
            over_tiles(act, store)
            act.wait_ge(out[0], 16 * (NT // 2 + 1))
            act.wait_ge(out[1], 16 * (NT // 2))

        @block.gpsimd
        def _(pool):
            def copy(it, u, rows):
                pool.wait_ge(ready[u], it)
                nc.gpsimd.tensor_copy(mc[:, u, :, 0:rows], mT[:, :, ds((2 * it + u) * P, rows)]).then_inc(m_in[u], 1)
            over_tiles(pool, copy)

        @block.tensor
        def _(pe):
            pe.wait_ge(s_w, 16)

            def product(it, u, rows):
                pe.wait_ge(m_in[u], it + 1)
                pe.wait_ge(added[u], it)
                for b in range(2):
                    for c in range(KD):
                        last = nc.tensor.matmul(ps[0:rows, 2 * u + b, :], mc[:, u, c, 0:rows],
                                                w[:, c, b * BANK:(b + 1) * BANK], start=(c == 0), stop=(c == KD - 1))
                last.then_inc(ready[u], 1)
            over_tiles(pe, product)

        @block.vector
        def _(dve):
            def add(it, u, rows):
                dve.wait_ge(ready[u], it + 1)
                dve.wait_ge(x_in[u], 16 * it + 16)
                dve.wait_ge(out[u], 16 * it)
                nc.vector.tensor_tensor(h[0:rows, u, :], x[0:rows, u, :],
                                        ps[0:rows, 2 * u:2 * u + 2, :].rearrange("p b n -> p (b n)"),
                                        ALU.add).then_inc(added[u], 1)
            over_tiles(dve, add)


def routing_phase(nc, a, ps, ident, z2T, gT, iT, jT):
    NTT = NT + 1
    with Scope(nc) as ctx, nc.Block() as block:
        def sb(n, shape, dt=F32):
            return ctx.enter_context(nc.sbuf_tensor("rt_" + n, shape, dt))

        def sem(n):
            return ctx.sem("rt_" + n)

        wq = sb("wq", [P, 2, KD, P])
        sk = sb("sub_keys", [P, 2 * PH, NK])
        qT = sb("qT", [P, 2, T])
        sc, sc2 = sb("scores", [P, 2, NTT, NK]), sb("scores_rest", [P, NTT, NK])
        v = sb("best", [P, 2, NTT, TOPK])
        vi = sb("best_index", [P, 2, NTT, TOPK], U32)
        vf = sb("best_index_f", [P, 2, NTT, TOPK])
        cs, cs2 = sb("sums", [P, NTT, TOPK * TOPK]), sb("sums_rest", [P, NTT, TOPK * TOPK])
        pos, pab = sb("pos", [P, NTT, TOPK], U32), sb("pos_ab", [P, 2, NTT, TOPK], U32)
        paf = sb("pos_ab_f", [P, 2, NTT, TOPK])
        it_i, it_f = sb("iota_i", [P, TOPK], I32), sb("iota_f", [P, TOPK])
        best = sb("best_sums", [P, NTT, TOPK])
        top = sb("top", [P, NTT, PH, TOPK])
        ti, tj = sb("top_i", [P, NTT, PH, TOPK]), sb("top_j", [P, NTT, PH, TOPK])
        sub, ex, gt = sb("shifted", [P, NTT, PH, TOPK]), sb("exps", [P, NTT, PH, TOPK]), sb("gates", [P, NTT, PH, TOPK])
        carrier = sb("wait_carrier", [P, 1])
        sm = sb("sums_e", [P, 2, NTT * PH])

        s_sk = sem("sub_keys_loaded")
        w_in = [sem(f"wq_loaded{c}") for c in range(2)]
        q_ready, q_kept = [sem(f"q_ready{c}") for c in range(2)], [sem(f"q_kept{c}") for c in range(2)]
        s_ready, s_kept = sem("scores_ready"), sem("scores_kept")
        s_kept_c = [sem(f"scores_kept{c}") for c in range(2)]
        s_used = [sem(f"scores_used{c}") for c in range(2)]
        chain, zeroed, it_ready = sem("chain"), sem("zeroed"), sem("iota_ready")
        shifted, exped, gates_ready, turned, kept = (sem(n) for n in (
            "shifted", "exped", "gates_ready", "turned", "kept"))
        GROUPS = [(0, 3), (3, 6), (6, 9)]
        NEGBIG = -3.0e38
        NLINK = 2 * 4 + 1 + 5 + 2 + 2 * 3

        @block.sync
        def _(sp):
            sp.dma_start(sk[:, :, :], a["sub_keysT"]).then_inc(s_sk, 16)
            with sp.Fori(0, PH) as h:
                for c in range(2):
                    sp.wait_ge(q_ready[c], h)
                    sp.dma_start(wq[:, c, :, :], a["w_query"][ds(2 * h + c, 1)].rearrange("o p k n -> p (o k) n")
                                 ).then_inc(w_in[c], 16)

        @block.gpsimd
        def _(pool):
            for c in range(2):
                nc.gpsimd.memset(sc[:, c, NT, :], 0.0).then_inc(zeroed, 1)
            nc.gpsimd.iota(it_i[:, :], pattern=[[1, TOPK]], base=0, channel_multiplier=0).then_inc(zeroed, 1)
            pool.wait_ge(zeroed, 3)
            nc.gpsimd.tensor_copy(it_f[:, :], it_i[:, :]).then_inc(it_ready, 1)

        @block.tensor
        def _(pe):
            pe.wait_ge(s_sk, 16)
            with pe.Fori(0, PH) as h:
                for c in range(2):
                    pe.wait_ge(w_in[c], 16 * h + 16)
                    pe.wait_ge(q_kept[c], h)
                    for b, (lo, hi) in enumerate(BLOCKS):
                        for k in range(KD):
                            last = nc.tensor.matmul(ps[:, 3 * c + b, 0:TB], wq[:, c, k, :], z2T[:, k, lo:hi],
                                                    start=(k == 0), stop=(k == KD - 1))
                    last.then_inc(q_ready[c], 1)
                for c in range(2):
                    pe.wait_ge(q_kept[c], h + 1)
                    for n, (lo, hi) in enumerate(GROUPS):
                        m = 3 * c + n
                        if m >= 2:
                            pe.wait_ge(s_kept, 6 * h + m - 1)
                        else:
                            pe.wait_ge(s_kept, 6 * h)
                        for t in range(lo, hi):
                            r = P if t < NT else NS
                            last = nc.tensor.matmul(ps[0:r, 6 + m % 2, (t - lo) * NK:(t - lo + 1) * NK],
                                                    qT[:, c, t * P:t * P + r],
                                                    sk[:, ds(2 * h + c, 1), :].rearrange("p o n -> p (o n)"),
                                                    start=True, stop=True)
                        last.then_inc(s_ready, 1)
            pe.wait_ge(gates_ready, 1)
            pe.wait_ge(s_kept, 6 * PH)
            for n, src in enumerate((gt, ti, tj)):
                for t, lo, r in TILES:
                    last = nc.tensor.transpose(ps[:, t // 4, (t % 4) * P:(t % 4) * P + r],
                                               src[0:r, t, :, :].rearrange("p h k -> p (h k)"), ident[0:r, 0:r])
                last.then_inc(turned, 1)
                pe.wait_ge(kept, n + 1)

        @block.scalar
        def _(act):
            act.wait_ge(zeroed, 3)
            with act.Fori(0, PH) as h:
                for c in range(2):
                    act.wait_ge(q_ready[c], h + 1)
                    act.wait_ge(s_ready, 6 * h)
                    nc.scalar.activation(qT[:, c, :].rearrange("p (b n) -> p b n", b=3), ps[:, 3 * c:3 * c + 3, 0:TB],
                                         ACT.Copy).then_inc(q_kept[c], 1)
                for c in range(2):
                    act.wait_ge(s_used[c], h)
                    for n, (lo, hi) in enumerate(GROUPS):
                        m = 3 * c + n
                        act.wait_ge(s_ready, 6 * h + m + 1)
                        parts = [(lo, hi, P)] if hi <= NT else [(lo, NT, P), (NT, hi, NS)]
                        for x, y, r in parts:
                            last = nc.scalar.activation(
                                sc[0:r, c, x:y, :],
                                ps[0:r, 6 + m % 2, (x - lo) * NK:(y - lo) * NK].rearrange("p (t n) -> p t n", n=NK),
                                ACT.Copy)
                        last.then_inc(s_kept, 1)
            act.wait_ge(shifted, 1)
            nc.scalar.activation(ex[:, :, :, :].rearrange("p t h k -> p (t h k)"),
                                 sub[:, :, :, :].rearrange("p t h k -> p (t h k)"), ACT.Exp).then_inc(exped, 1)
            for n, dst in enumerate((gT, iT, jT)):
                act.wait_ge(turned, n + 1)
                nc.scalar.activation(dst[:, :], ps[:, 0:3, :].rearrange("p b n -> p (b n)")[:, 0:T],
                                     ACT.Copy).then_inc(kept, 1)

        @block.vector
        def _(dve):
            dve.wait_ge(it_ready, 1)
            with dve.Fori(0, PH) as h:
                step = Chain(dve, chain, h * NLINK)

                def carry():
                    nc.vector.memset(carrier[:, :], 0.0)

                def link(ins):
                    step(ins)

                def top16(val, idx, src, rest, last_sem=None):
                    for t in range(NTT):
                        last = nc.vector.max(val(t)[:, 0:8], src(t))
                    link(last)
                    carry()
                    for t in range(NTT):
                        nc.vector.max_index(idx(t)[:, 0:8], val(t)[:, 0:8], src(t))
                        last = nc.vector.match_replace(rest(t), val(t)[:, 0:8], src(t), NEGBIG)
                    link(last)
                    carry()
                    for t in range(NTT):
                        last = nc.vector.max(val(t)[:, 8:16], rest(t))
                    link(last)
                    carry()
                    for t in range(NTT):
                        last = nc.vector.max_index(idx(t)[:, 8:16], val(t)[:, 8:16], rest(t))
                    return last

                for c in range(2):
                    dve.wait_ge(s_kept, 6 * h + 3 * c + 3)
                    carry()
                    last = top16(lambda t: v[:, c, t, :], lambda t: vi[:, c, t, :], lambda t: sc[:, c, t, :],
                                 lambda t: sc2[:, t, :])
                    last.then_inc(s_used[c], 1)
                    dve.wait_ge(s_used[c], h + 1)
                    link(nc.vector.tensor_copy(vf[:, c, :, :], vi[:, c, :, :]))
                link(nc.vector.tensor_tensor(
                    cs[:, :, :].rearrange("p t (i j) -> p t i j", i=TOPK),
                    v[:, 0, :, :].unsqueeze(3).to_broadcast([P, NTT, TOPK, TOPK]),
                    v[:, 1, :, :].unsqueeze(2).to_broadcast([P, NTT, TOPK, TOPK]), ALU.add))
                carry()
                link(top16(lambda t: best[:, t, :], lambda t: pos[:, t, :], lambda t: cs[:, t, :],
                           lambda t: cs2[:, t, :]))
                link(nc.vector.tensor_copy(top[:, :, ds(h, 1), :].rearrange("p t o k -> p t (o k)"), best[:, :, :]))
                nc.vector.tensor_scalar(pab[:, 0, :, :], pos[:, :, :], 4, None, ALU.logical_shift_right)
                link(nc.vector.tensor_scalar(pab[:, 1, :, :], pos[:, :, :], 15, None, ALU.bitwise_and))
                link(nc.vector.tensor_copy(paf[:, :, :, :], pab[:, :, :, :]))
                for c, dst in ((0, ti), (1, tj)):
                    eq = (cs, cs2)[c][:, :, :].rearrange("p t (k r) -> p t k r", k=TOPK)
                    link(nc.vector.tensor_tensor(
                        eq, paf[:, c, :, :].unsqueeze(3).to_broadcast([P, NTT, TOPK, TOPK]),
                        it_f[:, :].unsqueeze(1).unsqueeze(1).to_broadcast([P, NTT, TOPK, TOPK]), ALU.is_equal))
                    link(nc.vector.tensor_tensor(
                        eq, eq, vf[:, c, :, :].unsqueeze(2).to_broadcast([P, NTT, TOPK, TOPK]), ALU.mult))
                    link(nc.vector.tensor_reduce(dst[:, :, ds(h, 1), :].rearrange("p t o k -> p t (o k)"), eq,
                                                 AX_X, ALU.add))
                assert step.n == NLINK, step.n
            link = Chain(dve, chain, PH * NLINK)
            nc.vector.tensor_tensor(sub[:, :, :, :], top[:, :, :, :],
                                    top[:, :, :, 0:1].to_broadcast([P, NTT, PH, TOPK]), ALU.subtract
                                    ).then_inc(shifted, 1)
            dve.wait_ge(exped, 1)
            link(nc.vector.tensor_reduce(sm[:, 0, :].rearrange("p (t h) -> p t h", h=PH), ex[:, :, :, :], AX_X, ALU.add))
            link(nc.vector.reciprocal(sm[:, 1, :], sm[:, 0, :]))
            nc.vector.tensor_tensor(gt[:, :, :, :], ex[:, :, :, :],
                                    sm[:, 1, :].rearrange("p (t h) -> p t h", h=PH).unsqueeze(3)
                                    .to_broadcast([P, NTT, PH, TOPK]), ALU.mult).then_inc(gates_ready, 1)


def gate_phase(nc, a, ps, gT, iT, jT, g_dram, g_sample):
    with Scope(nc) as ctx, nc.Block() as block:
        def sb(n, shape, dt=F32):
            return ctx.enter_context(nc.sbuf_tensor("ga_" + n, shape, dt))

        def sem(n):
            return ctx.sem("ga_" + n)

        GT = 8
        PER = P // GT
        io_i, io = sb("iota_i", [P, NK], I32), sb("iota", [P, NK])
        oi, oj = sb("onehot_i", [P, 2, GT, NK]), sb("onehot_j", [P, 2, GT, NK])
        stage = sb("stage", [P, 2, NK, P])
        io_ready = sem("iota_ready")
        hot, done, kept = ([sem(f"{n}{s}") for s in range(2)] for n in ("onehots_ready", "products_done", "kept"))
        out = [sem(f"stored{u}") for u in range(2)]

        @block.gpsimd
        def _(pool):
            nc.gpsimd.iota(io_i[:, :], pattern=[[1, NK]], base=0, channel_multiplier=0).then_inc(io_ready, 1)
            pool.wait_ge(io_ready, 1)
            nc.gpsimd.tensor_copy(io[:, :], io_i[:, :]).then_inc(io_ready, 1)

        def over_steps(eng, step, tile=None):
            with eng.Fori(0, NT // 2) as tp:
                for u in range(2):
                    if tile:
                        tile(tp, u)
                    with eng.Fori(0, PER // 2) as g:
                        for s in range(2):
                            step((2 * tp + u) * (PER // 2) + g, s, u, (2 * tp + u) * P + (2 * g + s) * GT,
                                 (2 * g + s) * GT)
            step(NT * PER // 2, 0, None, SEQ, 0)

        @block.vector
        def _(dve):
            dve.wait_ge(io_ready, 2)

            def onehots(n, s, u, col, local):
                dve.wait_ge(done[s], n)
                for k in range(GT):
                    nc.vector.tensor_scalar(oj[:, s, k, :], io[:, :], jT[:, ds(col + k, 1)], None, ALU.is_equal)
                    last = nc.vector.tensor_scalar(oi[:, s, k, :], io[:, :], iT[:, ds(col + k, 1)],
                                                   gT[:, ds(col + k, 1)], ALU.is_equal, ALU.mult)
                last.then_inc(hot[s], 1)
            over_steps(dve, onehots)

        @block.tensor
        def _(pe):
            def products(n, s, u, col, local):
                pe.wait_ge(hot[s], n + 1)
                pe.wait_ge(kept[s], n)
                for k in range(GT):
                    last = nc.tensor.matmul(ps[:, 2 * s + k // 4, (k % 4) * NK:(k % 4 + 1) * NK], oj[:, s, k, :],
                                            oi[:, s, k, :], start=True, stop=True)
                last.then_inc(done[s], 1)
            over_steps(pe, products)

        @block.scalar
        def _(act):
            def keep(n, s, u, col, local):
                act.wait_ge(done[s], n + 1)
                dst = g_sample[:, :, :] if u is None else stage[:, u, :, ds(local, GT)]
                nc.scalar.activation(dst.rearrange("p i t -> p t i"),
                                     ps[:, 2 * s:2 * s + 2, :].rearrange("p b (t i) -> p (b t) i", i=NK),
                                     ACT.Copy).then_inc(kept[s], 1)

            def tile(tp, u):
                act.wait_ge(out[u], 16 * tp)
            over_steps(act, keep, tile)

        @block.sync
        def _(sp):
            with sp.Fori(0, NT // 2) as tp:
                for u in range(2):
                    for s in range(2):
                        sp.wait_ge(kept[s], (2 * tp + u + 1) * (PER // 2))
                    sp.dma_start(g_dram[:, :, ds((2 * tp + u) * P, P)].rearrange("i j t -> j i t"),
                                 stage[:, u, :, :]).then_inc(out[u], 16)
            for u in range(2):
                sp.wait_ge(out[u], 16 * (NT // 2))


def expert_phase(nc, a, ps, z2T, g_dram, g_sample, h_dram):
    NG = NK // GC
    with Scope(nc) as ctx:
        def sb(n, shape, dt=F32):
            return ctx.enter_context(nc.sbuf_tensor("ex_" + n, shape, dt))

        def sem(n):
            return ctx.sem("ex_" + n)

        acc = sb("acc", [P, NT + 1, D])
        U = sb("u", [P, GC, KD, P])
        V = sb("v", [P, GC, D])
        G = sb("gates", [P, GC, SEQ])
        A = sb("a", [P, GC, T])
        gl = sb("gelu", [P, 2, T])
        acc_in = sem("h_loaded")
        u_in, g_in, v_in = ([sem(f"{n}{c}") for c in range(GC)] for n in ("u_loaded", "gate_loaded", "v_loaded"))
        h_ready, gelu = [sem(f"hidden_ready{s}") for s in range(2)], [sem(f"gelu_done{s}") for s in range(2)]
        a_ready = [sem(f"a_ready{c}") for c in range(GC)]
        f_ready, f_added = [sem(f"f_ready{b}") for b in range(2)], [sem(f"f_added{b}") for b in range(2)]

        with nc.Block() as block:
            @block.sync
            def _(sp):
                def load_u(g, c):
                    sp.dma_start(U[:, c, :, :], a["expert_uT"][ds(g * GC + c, 1)].rearrange("o p k e -> p (o k) e")
                                 ).then_inc(u_in[c], 16)

                for c in range(GC):
                    load_u(0, c)
                with sp.Fori(1, NG) as g:
                    for c in range(GC):
                        sp.wait_ge(h_ready[c % 2], 2 * g - 1 + c // 2)
                        load_u(g, c)

            @block.gpsimd
            def _(pool):
                pool.dma_start(acc[:, 0:NT, :], h_dram[0:SEQ, :].rearrange("(t p) d -> p t d", p=P)).then_inc(acc_in, 16)
                pool.dma_start(acc[0:NS, NT, :], h_dram[SEQ:T, :]).then_inc(acc_in, 16)
                with pool.Fori(0, NG) as g:
                    for c in range(GC):
                        pool.wait_ge(a_ready[c], g)
                        pool.dma_start(G[:, c, :], g_dram[ds(g * GC + c, 1)].rearrange("o j t -> j (o t)")
                                       ).then_inc(g_in[c], 16)
                    pool.wait_ge(f_ready[1], (NT + 1) * g)
                    for c in range(GC):
                        pool.dma_start(V[:, c, :], a["expert_v"][ds((g * GC + c) * P, P), :]).then_inc(v_in[c], 16)

            @block.tensor
            def _(pe):
                def hidden(g, c):
                    s = c % 2
                    pe.wait_ge(u_in[c], 16 * g + 16)
                    pe.wait_ge(gelu[s], 2 * g + c // 2)
                    for b, (lo, hi) in enumerate(BLOCKS):
                        for k in range(KD):
                            last = nc.tensor.matmul(ps[:, 3 * s + b, 0:TB], U[:, c, k, :], z2T[:, k, lo:hi],
                                                    start=(k == 0), stop=(k == KD - 1))
                    last.then_inc(h_ready[s], 1)

                def values(g):
                    for c in range(GC):
                        pe.wait_ge(a_ready[c], g + 1)
                        pe.wait_ge(v_in[c], 16 * g + 16)
                    for t, lo, r in TILES:
                        for b in range(2):
                            pe.wait_ge(f_added[b], (NT + 1) * g + t)
                            for c in range(GC):
                                last = nc.tensor.matmul(ps[0:r, 6 + b, :], A[:, c, lo:lo + r],
                                                        V[:, c, b * BANK:(b + 1) * BANK],
                                                        start=(c == 0), stop=(c == GC - 1))
                            last.then_inc(f_ready[b], 1)

                for c in range(GC):
                    hidden(0, c)
                with pe.Fori(1, NG) as g:
                    hidden(g, 0)
                    hidden(g, 1)
                    values(g - 1)
                    hidden(g, 2)
                    hidden(g, 3)
                values(NG - 1)

            @block.scalar
            def _(act):
                with act.Fori(0, NG) as g:
                    for c in range(GC):
                        s = c % 2
                        act.wait_ge(h_ready[s], 2 * g + c // 2 + 1)
                        act.wait_ge(a_ready[c - 2 if c >= 2 else c + 2], g + 1 if c >= 2 else g)
                        nc.scalar.activation(gl[:, s, :].rearrange("p (b n) -> p b n", b=3),
                                             ps[:, 3 * s:3 * s + 3, 0:TB], ACT.Gelu).then_inc(gelu[s], 1)

            @block.vector
            def _(dve):
                def add(g):
                    for t, lo, r in TILES:
                        for b in range(2):
                            dve.wait_ge(f_ready[b], (NT + 1) * g + t + 1)
                            dst = acc[0:r, t, b * BANK:(b + 1) * BANK]
                            nc.vector.tensor_tensor(dst, dst, ps[0:r, 6 + b, :], ALU.add).then_inc(f_added[b], 1)

                def weigh(g):
                    dve.wait_ge(f_ready[1], (NT + 1) * g)
                    for c in range(GC):
                        s = c % 2
                        dve.wait_ge(gelu[s], 2 * g + c // 2 + 1)
                        dve.wait_ge(g_in[c], 16 * g + 16)
                        nc.vector.tensor_tensor(A[:, c, SEQ:T], gl[:, s, SEQ:T],
                                                g_sample[:, ds(g * GC + c, 1), :].rearrange("p o t -> p (o t)"), ALU.mult)
                        nc.vector.tensor_tensor(A[:, c, 0:SEQ], gl[:, s, 0:SEQ], G[:, c, :],
                                                ALU.mult).then_inc(a_ready[c], 1)

                dve.wait_ge(acc_in, 32)
                weigh(0)
                with dve.Fori(1, NG) as g:
                    add(g - 1)
                    weigh(g)
                add(NG - 1)

        with nc.Block() as block, ExitStack() as fin:
            gain = fin.enter_context(nc.sbuf_tensor("fn_gain", [P, D], F32))
            junk = fin.enter_context(nc.sbuf_tensor("fn_junk", [P, D], F32))
            st = fin.enter_context(nc.sbuf_tensor("fn_st", [P, 4, NT + 1], F32))
            s_g, s_z, sq, mean, root, ready, out = (fin.enter_context(nc.semaphore("fn_" + n)) for n in (
                "gain_loaded", "zeroed", "squares", "mean", "root", "rows_ready", "stored"))
            inv = fin.enter_context(nc.semaphore("fn_inverse"))

            @block.sync
            def _(sp):
                sp.dma_start(gain[:, :], a["g_final"].partition_broadcast(P)).then_inc(s_g, 16)
                for t, lo, r in TILES:
                    sp.wait_ge(ready, t + 1)
                    dst = a["o_y_p"][lo:lo + r, :] if t < NT else a["o_y_s"]
                    sp.dma_start(dst, acc[0:r, t, :]).then_inc(out, 16)
                sp.wait_ge(out, 16 * (NT + 1))

            @block.scalar
            def _(act):
                act.wait_ge(s_z, 1)
                for t, lo, r in TILES:
                    if t:
                        act.wait_ge(sq, t)
                    nc.scalar.activation(junk[0:r, :], acc[0:r, t, :], ACT.Square,
                                         accum_out=st[0:r, 0, t:t + 1]).then_inc(sq, 1)
                act.wait_ge(mean, 1)
                nc.scalar.activation(st[:, 2, :], st[:, 1, :], ACT.Sqrt).then_inc(root, 1)

            @block.vector
            def _(dve):
                nc.vector.memset(st[:, 0, :], 1.0).then_inc(s_z, 1)
                dve.wait_ge(sq, NT + 1)
                nc.vector.tensor_scalar(st[:, 1, :], st[:, 0, :], 1.0 / D, EPS, ALU.mult, ALU.add).then_inc(mean, 1)
                dve.wait_ge(root, 1)
                nc.vector.reciprocal(st[:, 3, :], st[:, 2, :]).then_inc(inv, 1)
                dve.wait_ge(inv, 1)
                dve.wait_ge(s_g, 16)
                for t, lo, r in TILES:
                    nc.vector.scalar_tensor_tensor(out=acc[0:r, t, :], in0=acc[0:r, t, :], scalar=st[0:r, 3, t:t + 1],
                                                   in1=gain[0:r, :], op0=ALU.mult, op1=ALU.mult).then_inc(ready, 1)



def tables():
    f = np.float32
    pos = np.zeros((NT + 1, P), f)
    pos[0:NT] = np.arange(SEQ, dtype=f).reshape(NT, P)
    pos[NT] = PAST
    base = (f(1.0) / (f(10000.0) ** np.linspace(0.0, 1.0, RDK // 2, dtype=f))).astype(f)
    ang = (pos[:, :, None] * base).astype(f)
    inv = (f(500000.0) ** (-np.arange(0, ROT, 2, dtype=f) / f(ROT))).astype(f)
    ang_a = (pos[:, :, None] * inv).astype(f)
    decay = np.log(1.0 - 2.0 ** (-5.0 - np.arange(RH)))
    m, l = np.arange(P)[:, None], np.arange(P)[None, :]
    maskT = np.where((l >= m)[:, None, :], np.exp(decay[None, :, None] * np.maximum(l - m, 0)[:, None, :]), 0.0)
    qdec = np.broadcast_to(np.exp(decay[:, None] * (np.arange(P) + 1.0)), (P, RH, P))
    kdec = np.exp(decay[None, :] * (P - 1.0 - np.arange(P))[:, None]) * RDK ** -0.5
    q, k = np.arange(P)[:, None], np.arange(P)[None, :]
    row = np.arange(2 * AH * NS)
    sample, head, second = row // (2 * AH), (row // 2) % AH, row % 2
    sel = np.concatenate([(second == 0)[:, None], (second == 1)[:, None],
                          sample[:, None] == np.arange(NS), head[:, None] == np.arange(AH)], axis=1)
    return {
        "ident": np.eye(P), "ret_cos": np.cos(ang), "ret_sin": np.sin(ang), "att_cos": np.cos(ang_a),
        "att_sin": np.sin(ang_a), "ret_maskT": maskT, "ret_qdec": qdec, "ret_kdec": kdec,
        "att_mask": np.where(k <= q, 0.0, NEG), "sel": sel,
    }


OUTS = {
    "o_y_p": (SEQ, D), "o_y_s": (NS, D), "o_ret_p": (RH, RDK, RDV), "o_k_p": (SEQ, AH * 2 * ADQ),
    "o_v_p": (SEQ, AH * ADV), "o_ret_s": (NS, RH, RDK, RDV), "o_k_s": (NS, AH * 2 * ADQ), "o_v_s": (NS, AH * ADV),
}


def lay_out(i):
    c = np.ascontiguousarray
    w_in = np.asarray(i["w_in"])[0]
    cols = np.cumsum([0, 512, 512, 1024, 512, 512, 512, D, D])
    rows = lambda w: w.reshape(-1, P, w.shape[1]).transpose(1, 0, 2)
    blocks = lambda w: w.reshape(-1, P, w.shape[1] // P, P).transpose(2, 1, 0, 3)
    U = np.asarray(i["expert_u"])[0]
    gates = blocks(w_in[:, cols[6]:cols[7]]), blocks(w_in[:, cols[7]:cols[8]])
    return {
        "x": c(np.concatenate([np.asarray(i["x_prompt"])[0], np.asarray(i["x_sample"])[:, 0]])),
        "state": c(np.asarray(i["state_ret"])[0]),
        "cache_kT": c(np.asarray(i["cache_k"])[0].transpose(0, 2, 3, 1)),
        "cache_v": c(np.asarray(i["cache_v"])[0].reshape(POOL, PAGE, AH * ADV)),
        "page_table": c(np.asarray(i["page_table"]).reshape(1, NS * NPAGE)),
        "g_mix": c(np.asarray(i["g_mix"]).reshape(KD, P).T), "g_ffn": c(np.asarray(i["g_ffn"]).reshape(KD, P).T),
        "g_subln": c(np.asarray(i["g_subln"]).reshape(ADV, 1)), "g_final": c(np.asarray(i["g_final"])),
        "lams": c(np.concatenate([np.asarray(i[n]) for n in ("lam_q1", "lam_k1", "lam_q2", "lam_k2")])),
        "w_ret": c(rows(w_in[:, 0:cols[3]])), "w_att": c(rows(w_in[:, cols[3]:cols[6]])),
        "w_merge": c(np.concatenate([*gates, blocks(np.asarray(i["w_br_ret"])[0]),
                                     blocks(np.asarray(i["w_br_att"])[0])], axis=2)),
        "w_out": c(rows(np.asarray(i["w_out"])[0])),
        "w_query": c(blocks(np.asarray(i["w_query"])[0])),
        "sub_keysT": c(np.asarray(i["sub_keys"])[0].reshape(2 * PH, NK, P).transpose(2, 0, 1)),
        "expert_uT": c(U.reshape(NK, P, KD, P).transpose(0, 3, 2, 1)),
        "expert_v": c(np.asarray(i["expert_v"])[0]),
        **{n: c(t.astype(np.float32)) for n, t in tables().items()},
    }


def kernel(**inputs):
    import concourse.bacc as bacc
    from concourse.bass_utils import run_bass_kernel_spmd

    nc = bacc.Bacc("TRN2", target_bir_lowering=False, num_devices=1)
    arrays = lay_out(inputs)
    aps = {n: nc.dram_tensor("in_" + n, x.shape, mybir.dt.from_np(x.dtype), kind="ExternalInput").ap()
           for n, x in arrays.items()}
    for n, shape in OUTS.items():
        aps[n] = nc.dram_tensor(n, shape, F32, kind="ExternalOutput").ap()
    build(nc, aps)
    r = run_bass_kernel_spmd(nc, [{"in_" + n: x for n, x in arrays.items()}], core_ids=[0]).results[0]
    return (r["o_y_p"].reshape(1, SEQ, D), r["o_y_s"].reshape(NS, 1, D),
            r["o_ret_p"].reshape(1, 1, RH, RDK, RDV), r["o_k_p"].reshape(1, 1, SEQ, AH, 2 * ADQ),
            r["o_v_p"].reshape(1, 1, SEQ, AH, ADV), r["o_ret_s"].reshape(1, NS, RH, RDK, RDV),
            r["o_k_s"].reshape(1, NS, 1, AH, 2 * ADQ), r["o_v_s"].reshape(1, NS, 1, AH, ADV))
```

```python
from contextlib import ExitStack

import numpy as np
import concourse.bass as bass
from concourse import mybir
from concourse.alu_op_type import AluOpType as ALU

F32 = mybir.dt.float32
F32R = mybir.dt.float32r
U32 = mybir.dt.uint32
I32 = mybir.dt.int32
ACT = mybir.ActivationFunctionType
AX_X = mybir.AxisListType.X
ds = bass.ds

P = 128
D = 1024
KD = D // P
SEQ = 1024
NS = 8
T = SEQ + NS
NT = SEQ // P
TB = T // 3
BLOCKS = [(b * TB, (b + 1) * TB) for b in range(3)]
BANK = 512
RH, RDK, RDV = 4, 128, 256
AH, ADQ, ADV = 4, 64, 128
ROT = ADQ // 4
PAST, PAGE = 512, 128
NPAGE = PAST // PAGE
POOL = 40
PH, NK, TOPK = 8, 128, 16
WR = 2 * RH * RDK + RH * RDV
WA = 2 * AH * 2 * ADQ + AH * ADV
EPS, SUB_EPS = 1e-6, 1e-5
LAM_INIT = 0.8 - 0.6
NEG = -1e30
ONE = 1
GC = 4
TILES = [(t, t * P, P) for t in range(NT)] + [(NT, SEQ, NS)]


class Chain:

    def __init__(self, eng, sem, base=0):
        self.eng, self.sem, self.base, self.n = eng, sem, base, 0

    def __call__(self, ins):
        ins.then_inc(self.sem, 1)
        self.n += 1
        self.eng.wait_ge(self.sem, ONE + self.base + self.n)


class Scope(ExitStack):

    def __init__(self, nc):
        super().__init__()
        self.nc, self.sems, self.queued = nc, [], []

    def sem(self, name):
        self.sems.append(self.enter_context(self.nc.semaphore(name)))
        return self.sems[-1]

    def queue_sem(self, name):
        self.queued.append(self.enter_context(self.nc.semaphore(name)))
        return self.queued[-1]

    def zero(self):
        for s in self.sems + self.queued:
            self.nc.gpsimd.sem_clear(s)
        self.nc.all_engine_barrier()

    def block(self):
        for s in self.sems:
            self.nc.gpsimd.sem_inc(s, ONE)
        self.nc.all_engine_barrier()
        self.callback(self.zero)
        return self.enter_context(self.nc.Block())


def build(nc, a, stop=99):
    top = ExitStack()
    with top:
        def sb(name, shape, dt=F32, ctx=top):
            return ctx.enter_context(nc.sbuf_tensor(name, shape, dt))

        def sem(name, ctx=top):
            return ctx.enter_context(nc.semaphore(name))

        h_dram = nc.dram_tensor("h_scratch", [T, D], F32, kind="Internal").ap()
        g_dram = nc.dram_tensor("gate_scratch", [NK, P, SEQ], F32, kind="Internal").ap()

        ps = top.enter_context(nc.psum_tensor("ps", [P, 8, BANK], F32))
        ident = sb("ident", [P, P])
        lam = sb("lam", [P, 1])

        with ExitStack() as mid:
            zT = sb("zT", [P, KD, T], ctx=mid)
            rT = sb("rT", [P, KD, T], ctx=mid)
            aT = sb("aT", [P, AH, T], ctx=mid)
            s_rqk = sb("s_rqk", [NS, 2 * RH * RDK], ctx=mid)
            s_rv = sb("s_rv", [NS, RH * RDV], ctx=mid)
            s_aqk = sb("s_aqk", [NS, 2 * AH * 2 * ADQ], ctx=mid)
            s_av = sb("s_av", [NS, AH * ADV], ctx=mid)
            norm_phase(nc, a, ps, ident, zT, lam)
            if stop >= 2:
                retention_phase(nc, a, ps, ident, zT, rT, s_rqk, s_rv)
            with ExitStack() as att:
                QT = sb("QT", [P, AH, SEQ], ctx=att)
                KT = sb("KT", [P, AH, SEQ], ctx=att)
                VA = sb("VA", [P, NT, AH * ADV], ctx=att)
                if stop >= 3:
                    attention_projection(nc, a, ps, ident, zT, QT, KT, VA, s_aqk, s_av)
                if stop >= 4:
                    attention_phase(nc, a, ps, ident, QT, KT, VA, aT, lam)
            if stop >= 5:
                sample_phase(nc, a, ps, ident, s_rqk, s_rv, s_aqk, s_av, rT, aT, lam)
            if stop >= 6:
                mT = sb("mT", [P, KD, T], ctx=mid)
                merge_phase(nc, a, ps, zT, rT, aT, mT)
                residual_phase(nc, a, ps, mT, h_dram)
        if stop >= 7:
            left = ExitStack()
            g_sample = sb("g_sample", [P, NK, NS])
            z2T = sb("z2T", [P, KD, T], ctx=left)
            norm2_phase(nc, a, ps, ident, z2T, h_dram)
            with ExitStack() as route:
                gT = sb("gT", [P, T], ctx=route)
                iT = sb("iT", [P, T], ctx=route)
                jT = sb("jT", [P, T], ctx=route)
                routing_phase(nc, a, ps, ident, z2T, gT, iT, jT)
                gate_phase(nc, a, ps, gT, iT, jT, g_dram, g_sample)
            expert_phase(nc, a, ps, ident, z2T, g_dram, g_sample, h_dram, top, left)


def norm_rows(nc, name, ctx, ps, ident, zT, src, gain_cols, const_ready, consts, extra=None):
    def sb(n, shape):
        return ctx.enter_context(nc.sbuf_tensor(f"{name}_{n}", shape, F32))

    def sem(n):
        return ctx.sem(f"{name}_{n}")

    x = sb("x", [P, 2, D])
    z = sb("z", [P, 2, D])
    junk = sb("junk", [P, D])
    st = sb("st", [P, 2, 4])
    loaded = [sem(f"rows_loaded{u}") for u in range(2)]
    squared = [sem(f"squares_summed{u}") for u in range(2)]
    mean = [sem(f"mean_ready{u}") for u in range(2)]
    root = [sem(f"root_ready{u}") for u in range(2)]
    inverse = [sem(f"inverse_ready{u}") for u in range(2)]
    scaled = [sem(f"rows_scaled{u}") for u in range(2)]
    turned = [sem(f"rows_turned{u}") for u in range(2)]
    kept = [sem(f"columns_kept{u}") for u in range(2)]

    def over_tiles(eng, step):
        with eng.Fori(0, NT // 2) as it:
            for u in range(2):
                step(it, u, P)
        step(NT // 2, 0, NS)

    block = ctx.block()
    if extra:
        extra(block)

    @block.sync
    def _(sp):
        consts(sp)

        def step(it, u, rows):
            sp.wait_ge(scaled[u], ONE + it)
            row = (2 * it + u) * P
            sp.dma_start(x[0:rows, u, :], src[ds(row, rows), :]).then_inc(loaded[u], 16)
        over_tiles(sp, step)

    @block.scalar
    def _(act):
        def step(it, u, rows):
            act.wait_ge(loaded[u], ONE + 16 * it + 16)
            nc.scalar.activation(junk[0:rows, :], x[0:rows, u, :], ACT.Square,
                                 accum_out=st[0:rows, u, 0:1]).then_inc(squared[u], 1)
            act.wait_ge(mean[u], ONE + it + 1)
            nc.scalar.activation(st[0:rows, u, 2:3], st[0:rows, u, 1:2], ACT.Sqrt).then_inc(root[u], 1)
        over_tiles(act, step)

    @block.vector
    def _(dve):
        def step(it, u, rows):
            dve.wait_ge(squared[u], ONE + it + 1)
            nc.vector.tensor_scalar(st[0:rows, u, 1:2], st[0:rows, u, 0:1], 1.0 / D, EPS,
                                    ALU.mult, ALU.add).then_inc(mean[u], 1)
            dve.wait_ge(root[u], ONE + it + 1)
            nc.vector.reciprocal(st[0:rows, u, 3:4], st[0:rows, u, 2:3]).then_inc(inverse[u], 1)
            dve.wait_ge(inverse[u], ONE + it + 1)
            dve.wait_ge(turned[u], ONE + it)
            nc.vector.tensor_scalar(z[0:rows, u, :], x[0:rows, u, :], st[0:rows, u, 3:4], None,
                                    ALU.mult).then_inc(scaled[u], 1)
            dve.wait_ge(turned[u], ONE + it + 1)
            col = (2 * it + u) * P
            nc.vector.tensor_tensor(
                zT[:, :, ds(col, rows)],
                ps[:, 2 * u:2 * u + 2, :].rearrange("p b (c r) -> p (b c) r", r=P)[:, :, 0:rows],
                gain_cols[:, :].unsqueeze(2).to_broadcast([P, KD, rows]), ALU.mult).then_inc(kept[u], 1)
        over_tiles(dve, step)

    @block.tensor
    def _(pe):
        pe.wait_ge(const_ready[0], ONE + const_ready[1])

        def step(it, u, rows):
            pe.wait_ge(scaled[u], ONE + it + 1)
            pe.wait_ge(kept[u], ONE + it)
            for c in range(KD):
                last = nc.tensor.transpose(ps[:, 2 * u + c // 4, (c % 4) * P:(c % 4) * P + rows],
                                           z[0:rows, u, c * P:(c + 1) * P], ident[0:rows, 0:rows])
            last.then_inc(turned[u], 1)
        over_tiles(pe, step)


def norm_phase(nc, a, ps, ident, zT, lam):
    with Scope(nc) as ctx:
        gain = ctx.enter_context(nc.sbuf_tensor("gain_mix", [P, KD], F32))
        lv = ctx.enter_context(nc.sbuf_tensor("lam_vectors", [P, 4, ADQ], F32))
        lp = ctx.enter_context(nc.sbuf_tensor("lam_products", [P, 2, ADQ], F32))
        le = ctx.enter_context(nc.sbuf_tensor("lam_parts", [P, 4], F32))
        s_const = ctx.sem("consts_loaded")
        s_step = ctx.sem("lam_step")
        s_sum = ctx.sem("lam_sums")
        s_exp = ctx.sem("lam_exps")
        n = 16 * 3
        def consts(sp):
            sp.dma_start(ident[:, :], a["ident"]).then_inc(s_const, 16)
            sp.dma_start(gain[:, :], a["g_mix"]).then_inc(s_const, 16)
            sp.dma_start(lv[:, :, :], a["lams"].partition_broadcast(P)).then_inc(s_const, 16)

        def find_lambda(block):
            @block.vector
            def _(dve):
                link = Chain(dve, s_step)
                dve.wait_ge(s_const, ONE + n)
                link(nc.vector.tensor_tensor(lp[:, :, :], lv[:, 0:4:2, :], lv[:, 1:4:2, :], ALU.mult))
                nc.vector.tensor_reduce(le[:, 0:2], lp[:, :, :], AX_X, ALU.add).then_inc(s_sum, 1)

            @block.scalar
            def _(act):
                act.wait_ge(s_sum, ONE + 1)
                nc.scalar.activation(le[:, 2:4], le[:, 0:2], ACT.Exp).then_inc(s_exp, 1)

            @block.gpsimd
            def _(pool):
                pool.wait_ge(s_exp, ONE + 1)
                nc.gpsimd.tensor_tensor(le[:, 0:1], le[:, 2:3], le[:, 3:4], ALU.subtract).then_inc(s_exp, 1)
                pool.wait_ge(s_exp, ONE + 2)
                nc.gpsimd.tensor_scalar(lam[:, :], le[:, 0:1], LAM_INIT, None, ALU.add).then_inc(s_exp, 1)

        norm_rows(nc, "mix", ctx, ps, ident, zT, a["x"], gain, (s_const, n), consts, find_lambda)


def norm2_phase(nc, a, ps, ident, z2T, h_dram):
    with Scope(nc) as ctx:
        gain = ctx.enter_context(nc.sbuf_tensor("gain_ffn", [P, KD], F32))
        s_gain = ctx.sem("gain_ffn_loaded")
        def consts(sp):
            sp.dma_start(gain[:, :], a["g_ffn"]).then_inc(s_gain, 16)

        norm_rows(nc, "ffn", ctx, ps, ident, z2T, h_dram, gain, (s_gain, 16), consts)


def retention_phase(nc, a, ps, ident, zT, rT, s_rqk, s_rv):
    with Scope(nc) as ctx:
        def sb(n, shape, dt=F32):
            return ctx.enter_context(nc.sbuf_tensor("ret_" + n, shape, dt))

        def sem(n):
            return ctx.sem("ret_" + n)

        W = sb("w", [P, KD, WR])
        zc = sb("z_tile", [P, KD, P])
        cosr, sinr = sb("cos", [P, NT + 1, 64]), sb("sin", [P, NT + 1, 64])
        maskT = sb("maskT", [P, RH, P])
        qdec = sb("q_decay", [P, RH, P])
        kdec = sb("k_decay", [P, RH])
        rot = sb("rotated", [P, 2 * RH, 64, 2])
        t1, t2 = sb("t1", [P, 2 * RH, 64]), sb("t2", [P, 2 * RH, 64])
        kd = sb("k_decayed", [P, RH, P])
        v = sb("v", [P, RH * RDV])
        qT, qdT, kT, sT = (sb(n, [P, RH, P]) for n in ("qT", "qdT", "kT", "sT"))
        state = sb("state", [P, RH, RDV])
        rn = sb("normed", [P, RH, RDV])
        junk = sb("junk", [P, RDV])
        st = sb("st", [P, 4, RH])

        s_w, s_tab = [sem("w_loaded_qk"), sem("w_loaded_v")], sem("tables_loaded")
        state_zero, inv, sq_step = sem("state_zero"), sem("inverse"), sem("square_step")
        z_ready, qk_ready, v_ready = sem("z_tile_ready"), sem("qk_projected"), sem("v_projected")
        v_kept = sem("v_kept")
        chain, rotated, k_dec_ready = sem("chain"), sem("rotated_ready"), sem("kd_ready")
        qk_turned, qk_kept = sem("qk_turned"), sem("qk_kept")
        s_ready, s_kept = sem("scores_ready"), sem("scores_kept")
        out_ready, state_ready, state_kept = sem("out_ready"), sem("state_update_ready"), sem("state_kept")
        squares, mean, root, normed = sem("squares"), sem("mean"), sem("root"), sem("normed_ready")
        turned, kept, stored = sem("out_turned"), sem("out_kept"), sem("stored")
        ACT_V, PROJ = 3, WR // BANK
        SCALE = float(RDK) ** -0.5
        log_decay = np.log(1.0 - 2.0 ** (-5.0 - np.arange(RH)))
        g_chunk = [float(np.exp(x * P)) for x in log_decay]
        NLINK = 5

        block = ctx.block()

        @block.sync
        def _(sp):
            sp.dma_start(W[:, :, 0:2 * BANK], a["w_ret"][:, :, 0:2 * BANK]).then_inc(s_w[0], 16)
            for d_, s_ in ((cosr, "ret_cos"), (sinr, "ret_sin")):
                sp.dma_start(d_[:, :, :], a[s_].rearrange("t p f -> p t f")).then_inc(s_tab, 16)
            for d_, s_ in ((maskT, "ret_maskT"), (qdec, "ret_qdec")):
                sp.dma_start(d_[:, :, :], a[s_]).then_inc(s_tab, 16)
            sp.dma_start(kdec[:, :], a["ret_kdec"]).then_inc(s_tab, 16)
            sp.dma_start(W[:, :, 2 * BANK:WR], a["w_ret"][:, :, 2 * BANK:WR]).then_inc(s_w[1], 16)
            sp.wait_ge(state_kept, ONE + NT)
            sp.dma_start(a["o_ret_p"].rearrange("h k v -> k h v"), state[:, :, :]).then_inc(stored, 16)
            sp.wait_ge(stored, ONE + 16)

        @block.gpsimd
        def _(pool):
            def copy_tile(t):
                pool.wait_ge(v_ready, ONE + t)
                nc.gpsimd.tensor_copy(zc[:, :, :], zT[:, :, ds(t * P, P)]).then_inc(z_ready, 1)
            nc.gpsimd.memset(state[:, :, :], 0.0).then_inc(state_zero, 1)
            with pool.Fori(0, NT) as t:
                copy_tile(t)

        @block.tensor
        def _(pe):
            def project(t, rows, lhs):
                pe.wait_ge(rotated, ONE + t)
                for b in range(PROJ):
                    if b == 2:
                        pe.wait_ge(v_kept, ONE + t)
                    for c in range(KD):
                        last = nc.tensor.matmul(ps[0:rows, b, :], lhs(c), W[:, c, b * BANK:(b + 1) * BANK],
                                                start=(c == 0), stop=(c == KD - 1))
                    if b == 1:
                        last.then_inc(qk_ready, 1)
                last.then_inc(v_ready, 1)

            def tile_project(t):
                pe.wait_ge(z_ready, ONE + t + 1)
                project(t, P, lambda c: zc[:, c, :])

            def chunk(t):
                pe.wait_ge(rotated, ONE + t + 1)
                pe.wait_ge(normed, ONE + t)
                for i in range(2 * RH):
                    last = nc.tensor.transpose(ps[:, 4 + i // RH, (i % RH) * P:(i % RH + 1) * P],
                                               rot[:, i, :, :].rearrange("p f two -> p (f two)"), ident[:, :])
                last.then_inc(qk_turned, 1)
                pe.wait_ge(qk_kept, ONE + t + 1)
                pe.wait_ge(kept, ONE + t)
                for h in range(RH):
                    last = nc.tensor.matmul(ps[:, 6, h * P:(h + 1) * P], kT[:, h, :], qT[:, h, :],
                                            start=True, stop=True)
                last.then_inc(s_ready, 1)
                pe.wait_ge(s_kept, ONE + t + 1)
                pe.wait_ge(v_kept, ONE + t + 1)
                pe.wait_ge(state_kept, ONE + t)
                for h in range(RH):
                    o = ps[:, 4 + h // 2, (h % 2) * RDV:(h % 2 + 1) * RDV]
                    vh = v[:, h * RDV:(h + 1) * RDV]
                    nc.tensor.matmul(o, sT[:, h, :], vh, start=True, stop=False)
                    last = nc.tensor.matmul(o, qdT[:, h, :], state[:, h, :], start=False, stop=True)
                last.then_inc(out_ready, 1)
                pe.wait_ge(k_dec_ready, ONE + t + 1)
                for h in range(RH):
                    last = nc.tensor.matmul(ps[:, 6 + h // 2, (h % 2) * RDV:(h % 2 + 1) * RDV], kd[:, h, :],
                                            v[:, h * RDV:(h + 1) * RDV], start=True, stop=True)
                last.then_inc(state_ready, 1)

            def turn_out(t):
                pe.wait_ge(normed, ONE + t + 1)
                pe.wait_ge(state_kept, ONE + t + 1)
                for c in range(KD):
                    last = nc.tensor.transpose(ps[:, 6 + c // 4, (c % 4) * P:(c % 4 + 1) * P],
                                               rn[:, :, :].rearrange("p h e -> p (h e)")[:, c * P:(c + 1) * P],
                                               ident[:, :])
                last.then_inc(turned, 1)

            pe.wait_ge(s_w[0], ONE + 16)
            pe.wait_ge(s_w[1], ONE + 16)
            pe.wait_ge(state_zero, ONE + 1)
            tile_project(0)
            with pe.Fori(0, NT - 1) as t:
                chunk(t)
                tile_project(t + 1)
                turn_out(t)
            chunk(NT - 1)
            project(NT, NS, lambda c: zT[:, c, SEQ:T])
            turn_out(NT - 1)

        @block.vector
        def _(dve):
            def rotate(t, rows, out, base):
                dve.wait_ge(qk_ready, ONE + t + 1)
                dve.wait_ge(state_ready, ONE + t)
                x = ps[0:rows, 0:2, :].rearrange("p b (h f two) -> p (b h) f two", h=RH, two=2)
                cb = cosr[0:rows, ds(t, 1), :].to_broadcast([rows, 2 * RH, 64])
                sb_ = sinr[0:rows, ds(t, 1), :].to_broadcast([rows, 2 * RH, 64])
                link = Chain(dve, chain, base)
                u1, u2 = t1[0:rows], t2[0:rows]
                link(nc.vector.tensor_tensor(u1, x[:, :, :, 0], cb, ALU.mult))
                link(nc.vector.tensor_tensor(u2, x[:, :, :, 1], sb_, ALU.mult))
                link(nc.vector.tensor_tensor(out[:, :, :, 0], u1, u2, ALU.subtract))
                link(nc.vector.tensor_tensor(u1, x[:, :, :, 1], cb, ALU.mult))
                link(nc.vector.tensor_tensor(u2, x[:, :, :, 0], sb_, ALU.mult))
                nc.vector.tensor_tensor(out[:, :, :, 1], u1, u2, ALU.add).then_inc(rotated, 1)

            def tile_rotate(t):
                rotate(t, P, rot[:, :, :, :], t * NLINK)
                dve.wait_ge(rotated, ONE + t + 1)
                nc.vector.tensor_tensor(kd[:, :, :], rot[:, RH:, :, :].rearrange("p h f two -> p h (f two)"),
                                        kdec[:, :].unsqueeze(2).to_broadcast([P, RH, P]),
                                        ALU.mult).then_inc(k_dec_ready, 1)

            def chunk(t):
                dve.wait_ge(qk_turned, ONE + t + 1)
                q_ps = ps[:, 4, :].rearrange("p (h l) -> p h l", h=RH)
                nc.vector.tensor_copy(qT[:, :, :], q_ps)
                nc.vector.tensor_tensor(qdT[:, :, :], q_ps, qdec[:, :, :], ALU.mult)
                nc.vector.tensor_scalar(kT[:, :, :], ps[:, 5, :].rearrange("p (h l) -> p h l", h=RH), SCALE,
                                        None, ALU.mult).then_inc(qk_kept, 1)
                dve.wait_ge(s_ready, ONE + t + 1)
                nc.vector.tensor_tensor(sT[:, :, :], ps[:, 6, :].rearrange("p (h l) -> p h l", h=RH),
                                        maskT[:, :, :], ALU.mult).then_inc(s_kept, 1)
                dve.wait_ge(squares, ONE + t + 1)
                nc.vector.tensor_scalar(st[:, 1, :], st[:, 0, :], 1.0 / RDV, EPS, ALU.mult,
                                        ALU.add).then_inc(mean, 1)
                dve.wait_ge(root, ONE + t + 1)
                nc.vector.reciprocal(st[:, 3, :], st[:, 2, :]).then_inc(inv, 1)
                dve.wait_ge(state_ready, ONE + t + 1)
                for h in range(RH):
                    last = nc.vector.scalar_tensor_tensor(
                        out=state[:, h, :], in0=state[:, h, :], scalar=g_chunk[h],
                        in1=ps[:, 6 + h // 2, (h % 2) * RDV:(h % 2 + 1) * RDV], op0=ALU.mult, op1=ALU.add)
                last.then_inc(state_kept, 1)
                dve.wait_ge(inv, ONE + t + 1)
                dve.wait_ge(turned, ONE + t)
                nc.vector.tensor_tensor(rn[:, :, :], ps[:, 4:6, :].rearrange("p b (h e) -> p (b h) e", h=2),
                                        st[:, 3, :].unsqueeze(2).to_broadcast([P, RH, RDV]),
                                        ALU.mult).then_inc(normed, 1)

            dve.wait_ge(s_tab, ONE + 16 * 5)
            tile_rotate(0)
            with dve.Fori(0, NT - 1) as t:
                chunk(t)
                tile_rotate(t + 1)
            chunk(NT - 1)
            rotate(NT, NS, s_rqk[:, :].rearrange("p (h f two) -> p h f two", f=64, two=2), NT * NLINK)

        @block.scalar
        def _(act):
            def keep_v(t, rows, out):
                act.wait_ge(v_ready, ONE + t + 1)
                nc.scalar.activation(out, ps[0:rows, 2:4, :].rearrange("p b n -> p (b n)"),
                                     ACT.Copy).then_inc(v_kept, 1)

            def chunk(t):
                act.wait_ge(out_ready, ONE + t + 1)
                for h in range(RH):
                    if h:
                        act.wait_ge(sq_step, ONE + (RH - 1) * t + h)
                    ins = nc.scalar.activation(junk[:, :], ps[:, 4 + h // 2, (h % 2) * RDV:(h % 2 + 1) * RDV],
                                               ACT.Square, accum_out=st[:, 0, h:h + 1])
                    ins.then_inc(sq_step if h < RH - 1 else squares, 1)
                act.wait_ge(mean, ONE + t + 1)
                nc.scalar.activation(st[:, 2, :], st[:, 1, :], ACT.Sqrt).then_inc(root, 1)

            def keep_out(t):
                act.wait_ge(turned, ONE + t + 1)
                nc.scalar.activation(rT[:, :, ds(t * P, P)],
                                     ps[:, 6:8, :].rearrange("p b (c r) -> p (b c) r", r=P),
                                     ACT.Copy).then_inc(kept, 1)

            keep_v(0, P, v[:, :])
            with act.Fori(0, NT - 1) as t:
                chunk(t)
                act.wait_ge(state_ready, ONE + t + 1)
                keep_v(t + 1, P, v[:, :])
                keep_out(t)
            chunk(NT - 1)
            keep_v(NT, NS, s_rv[:, :])
            keep_out(NT - 1)


def attention_projection(nc, a, ps, ident, zT, QT, KT, VA, s_aqk, s_av):
    with Scope(nc) as ctx:
        def sb(n, shape, dt=F32):
            return ctx.enter_context(nc.sbuf_tensor("ap_" + n, shape, dt))

        def sem(n):
            return ctx.sem("ap_" + n)

        W = sb("w", [P, KD, WA])
        zc = sb("z_tile", [P, KD, P])
        cosa, sina = sb("cos", [P, NT + 1, 8]), sb("sin", [P, NT + 1, 8])
        NG = 4 * AH
        qk = sb("qk", [P, NG, ADQ])
        u = sb("u", [P, 4, NG, 8])
        s_w, s_tab, z_ready = sem("w_loaded"), sem("tables_loaded"), sem("z_tile_ready")
        projected, copied, rotated = sem("projected"), sem("straight_part_kept"), sem("rotated")
        prods, v_kept, turned, kept = sem("products"), sem("v_kept"), sem("qk_turned"), sem("qk_kept")
        k_stored, v_stored = sem("k_rows_stored"), sem("v_rows_stored")

        block = ctx.block()

        @block.sync
        def _(sp):
            sp.dma_start(W[:, :, :], a["w_att"]).then_inc(s_w, 16)
            for d_, s_ in ((cosa, "att_cos"), (sina, "att_sin")):
                sp.dma_start(d_[:, :, :], a[s_].rearrange("t p f -> p t f")).then_inc(s_tab, 16)
            with sp.Fori(0, NT) as t:
                sp.wait_ge(rotated, ONE + t + 1)
                sp.dma_start(a["o_k_p"][ds(t * P, P), :], qk[:, NG // 2:, :]).then_inc(k_stored, 16)
            sp.wait_ge(rotated, ONE + NT + 1)
            sp.dma_start(a["o_k_s"], s_aqk[:, 512:1024]).then_inc(k_stored, 16)
            sp.wait_ge(v_kept, ONE + NT + 1)
            sp.dma_start(a["o_v_p"].rearrange("(t p) n -> p t n", p=P), VA[:, :, :]).then_inc(v_stored, 16)
            sp.dma_start(a["o_v_s"], s_av[:, :]).then_inc(v_stored, 16)
            sp.wait_ge(k_stored, ONE + 16 * (NT + 1))
            sp.wait_ge(v_stored, ONE + 32)

        @block.gpsimd
        def _(pool):
            with pool.Fori(0, NT) as t:
                pool.wait_ge(projected, ONE + t)
                nc.gpsimd.tensor_copy(zc[:, :, :], zT[:, :, ds(t * P, P)]).then_inc(z_ready, 1)

        @block.tensor
        def _(pe):
            def project(t, rows, lhs):
                pe.wait_ge(rotated, ONE + t)
                pe.wait_ge(v_kept, ONE + t)
                for b in range(3):
                    for c in range(KD):
                        last = nc.tensor.matmul(ps[0:rows, b, :], lhs(c), W[:, c, b * BANK:(b + 1) * BANK],
                                                start=(c == 0), stop=(c == KD - 1))
                last.then_inc(projected, 1)

            pe.wait_ge(s_w, ONE + 16)
            with pe.Fori(0, NT) as t:
                pe.wait_ge(z_ready, ONE + t + 1)
                project(t, P, lambda c: zc[:, c, :])
                pe.wait_ge(rotated, ONE + t + 1)
                pe.wait_ge(kept, ONE + t)
                for i in range(2 * AH):
                    last = nc.tensor.transpose(ps[:, 4 + i // AH, (i % AH) * P:(i % AH + 1) * P],
                                               qk[:, 2 * i:2 * i + 2, :].rearrange("p c d -> p (c d)"), ident[:, :])
                last.then_inc(turned, 1)
            project(NT, NS, lambda c: zT[:, c, SEQ:T])

        @block.vector
        def _(dve):
            def rotate(t, rows, out, x):
                dve.wait_ge(projected, ONE + t + 1)
                dve.wait_ge(copied, ONE + t + 1)
                cb = cosa[0:rows, ds(t, 1), :].to_broadcast([rows, NG, 8])
                sb_ = sina[0:rows, ds(t, 1), :].to_broadcast([rows, NG, 8])
                x1, x2 = x[:, :, 0:8], x[:, :, 8:16]
                w = u[0:rows]
                nc.vector.tensor_tensor(w[:, 0], x1, cb, ALU.mult)
                nc.vector.tensor_tensor(w[:, 1], x2, sb_, ALU.mult)
                nc.vector.tensor_tensor(w[:, 2], x2, cb, ALU.mult)
                nc.vector.tensor_tensor(w[:, 3], x1, sb_, ALU.mult).then_inc(prods, 1)
                dve.wait_ge(prods, ONE + t + 1)
                nc.vector.tensor_tensor(out[:, :, 0:8], w[:, 0], w[:, 1], ALU.subtract)
                nc.vector.tensor_tensor(out[:, :, 8:16], w[:, 2], w[:, 3], ALU.add).then_inc(rotated, 1)

            dve.wait_ge(s_tab, ONE + 32)
            with dve.Fori(0, NT) as t:
                rotate(t, P, qk[:, :, :], ps[:, 0:2, :].rearrange("p b (g d) -> p (b g) d", d=ADQ))
                dve.wait_ge(turned, ONE + t + 1)
                nc.vector.tensor_copy(QT[:, :, ds(t * P, P)], ps[:, 4, :].rearrange("p (h l) -> p h l", h=AH))
                nc.vector.tensor_copy(KT[:, :, ds(t * P, P)],
                                      ps[:, 5, :].rearrange("p (h l) -> p h l", h=AH)).then_inc(kept, 1)
            rotate(NT, NS, s_aqk[:, :].rearrange("p (g d) -> p g d", d=ADQ),
                   ps[0:NS, 0:2, :].rearrange("p b (g d) -> p (b g) d", d=ADQ))

        @block.scalar
        def _(act):
            def keep(t, rows, out, vout):
                act.wait_ge(projected, ONE + t + 1)
                act.wait_ge(turned, ONE + t)
                act.wait_ge(k_stored, ONE + 16 * t)
                x = ps[0:rows, 0:2, :].rearrange("p b (g d) -> p (b g) d", d=ADQ)
                nc.scalar.activation(out[:, :, ROT:ADQ], x[:, :, ROT:ADQ], ACT.Copy).then_inc(copied, 1)
                nc.scalar.activation(vout, ps[0:rows, 2, :], ACT.Copy).then_inc(v_kept, 1)

            with act.Fori(0, NT) as t:
                keep(t, P, qk[:, :, :], VA[:, ds(t, 1), :].rearrange("p o n -> p (o n)"))
            keep(NT, NS, s_aqk[:, :].rearrange("p (g d) -> p g d", d=ADQ), s_av[:, :])


def attention_phase(nc, a, ps, ident, QT, KT, VA, aT, lam):
    with Scope(nc) as ctx:
        def sb(n, shape, dt=F32):
            return ctx.enter_context(nc.sbuf_tensor("at_" + n, shape, dt))

        def sem(n):
            return ctx.sem("at_" + n)

        mask = sb("mask", [P, P])
        pr = sb("probs", [P, 2, 2, SEQ])
        wT = sb("weights_T", [P, 2, SEQ])
        mx = sb("max", [P, 2, 4])
        sm = sb("sums", [P, 2, 4])
        o, sq = sb("out", [P, NT, AH, ADV]), sb("squares", [P, AH, ADV])
        st = sb("st", [P, 4, NT, AH])
        gain = sb("gain", [P, 1])
        s_tab = sem("tables_loaded")
        scored, maxed, exped = sem("scores_ready"), sem("max_ready"), sem("exp_done")
        combined = sem("weights_ready")
        turned, kept, summed = sem("weights_turned"), sem("weights_kept"), sem("values_summed")
        chain, squares = sem("chain"), sem("squares")
        out_kept, mean, root = sem("out_kept"), sem("mean"), sem("root")
        normed, out_turned, out_stored = sem("normed"), sem("out_turned"), sem("out_columns_kept")
        SC = float(ADQ) ** -0.5
        steps = [(t, h) for t in range(NT) for h in range(AH)]
        N = len(steps)

        def score_ps(c, nk):
            return ps[:, 2 * c:2 * c + 2, :].rearrange("p b n -> p (b n)")[:, 0:nk]

        block = ctx.block()

        @block.sync
        def _(sp):
            sp.dma_start(mask[:, :], a["att_mask"]).then_inc(s_tab, 16)
            sp.dma_start(gain[:, :], a["g_subln"]).then_inc(s_tab, 16)

        @block.tensor
        def _(pe):
            def scores(s, c):
                t, h = steps[s]
                nk = (t + 1) * P
                if s:
                    pe.wait_ge(exped, ONE + 2 * (s - 1) + c + 1)
                for b in range(0, nk, BANK):
                    w = min(BANK, nk - b)
                    last = nc.tensor.matmul(ps[:, 2 * c + b // BANK, 0:w],
                                            QT[c * ADQ:(c + 1) * ADQ, h, t * P:(t + 1) * P],
                                            KT[c * ADQ:(c + 1) * ADQ, h, b:b + w], start=True, stop=True)
                last.then_inc(scored, 1)

            def turn_weights(s):
                t, h = steps[s]
                pe.wait_ge(combined, ONE + s + 1)
                if s:
                    pe.wait_ge(kept, ONE + s)
                for b in range(t + 1):
                    last = nc.tensor.transpose(ps[:, 4 + b // 4, (b % 4) * P:(b % 4 + 1) * P],
                                               pr[:, s % 2, 0, b * P:(b + 1) * P], ident[:, :])
                last.then_inc(turned, 1)

            def values(s):
                t, h = steps[s]
                pe.wait_ge(kept, ONE + s + 1)
                if h == 0 and t >= 2:
                    pe.wait_ge(out_kept, ONE + t - 1)
                for b in range(t + 1):
                    last = nc.tensor.matmul(ps[:, 6 + t % 2, h * P:(h + 1) * P], wT[:, s % 2, b * P:(b + 1) * P],
                                            VA[:, b, h * ADV:(h + 1) * ADV], start=(b == 0), stop=(b == t))
                last.then_inc(summed, 1)

            scores(0, 0)
            scores(0, 1)
            for s in range(N):
                if s + 1 < N:
                    scores(s + 1, 0)
                if s:
                    values(s - 1)
                if s + 1 < N:
                    scores(s + 1, 1)
                turn_weights(s)
            values(N - 1)
            for t in range(NT):
                pe.wait_ge(normed, ONE + t + 1)
                for h in range(AH):
                    last = nc.tensor.transpose(ps[:, t, h * P:(h + 1) * P], o[:, t, h, :], ident[:, :])
                last.then_inc(out_turned, 1)

        @block.vector
        def _(dve):
            link = Chain(dve, chain)

            def maximum(s, c):
                t, h = steps[s]
                nk = (t + 1) * P
                dve.wait_ge(scored, ONE + 2 * s + c + 1)
                sc = score_ps(c, nk)
                diag = sc[:, t * P:nk]
                link(nc.vector.tensor_tensor(diag, diag, mask[:, :], ALU.add))
                m = mx[:, s % 2, :]
                link(nc.vector.tensor_reduce(m[:, c:c + 1], sc, AX_X, ALU.max))
                nc.vector.tensor_scalar(m[:, 2 + c:3 + c], m[:, c:c + 1], -SC, None, ALU.mult).then_inc(maxed, 1)

            def combine(s):
                t, h = steps[s]
                nk = (t + 1) * P
                dve.wait_ge(exped, ONE + 2 * s + 2)
                w = sm[:, s % 2, :]
                link(nc.vector.reciprocal(w[:, 2:4], w[:, 0:2]))
                p0, p1 = pr[:, s % 2, 0, 0:nk], pr[:, s % 2, 1, 0:nk]
                link(nc.vector.tensor_scalar(p1, p1, w[:, 3:4], lam[:, 0:1], ALU.mult, ALU.mult))
                nc.vector.scalar_tensor_tensor(out=p0, in0=p0, scalar=w[:, 2:3], in1=p1, op0=ALU.mult,
                                               op1=ALU.subtract).then_inc(combined, 1)

            def square_tile(t):
                dve.wait_ge(out_kept, ONE + t + 1)
                if t:
                    dve.wait_ge(squares, ONE + 2 * t)
                nc.vector.tensor_tensor(sq[:, :, :], o[:, t, :, :], o[:, t, :, :], ALU.mult).then_inc(squares, 1)
                dve.wait_ge(squares, ONE + 2 * t + 1)
                nc.vector.tensor_reduce(st[:, 0, t, :], sq[:, :, :], AX_X, ALU.add).then_inc(squares, 1)

            dve.wait_ge(s_tab, ONE + 32)
            for c in range(2):
                maximum(0, c)
            for s, (t, h) in enumerate(steps):
                if s + 1 < N:
                    maximum(s + 1, 0)
                combine(s)
                if s + 1 < N:
                    maximum(s + 1, 1)
                if t and h == 2:
                    square_tile(t - 1)
            square_tile(NT - 1)
            dve.wait_ge(squares, ONE + 2 * NT)
            nc.vector.tensor_scalar(st[:, 1, :, :], st[:, 0, :, :], 1.0 / ADV, SUB_EPS, ALU.mult,
                                    ALU.add).then_inc(mean, 1)
            dve.wait_ge(root, ONE + 1)
            link(nc.vector.reciprocal(st[:, 3, :, :], st[:, 2, :, :]))
            flat = o[:, :, :, :].rearrange("p t h e -> p (t h) e")
            inv = st[:, 3, :, :].rearrange("p t h -> p (t h)").unsqueeze(2)
            for t in range(NT):
                q = slice(t * AH, (t + 1) * AH)
                nc.vector.tensor_tensor(flat[:, q, :], flat[:, q, :], inv[:, q, :].to_broadcast([P, AH, ADV]),
                                        ALU.mult).then_inc(normed, 1)
            for t in range(NT):
                dve.wait_ge(out_turned, ONE + t + 1)
                nc.vector.tensor_scalar(aT[:, :, t * P:(t + 1) * P], ps[:, t, :].rearrange("p (h l) -> p h l", h=AH),
                                        gain[:, 0:1], 1.0 - LAM_INIT, ALU.mult, ALU.mult).then_inc(out_stored, 1)

        @block.scalar
        def _(act):
            def exps(s, c):
                t, h = steps[s]
                nk = (t + 1) * P
                act.wait_ge(maxed, ONE + 2 * s + c + 1)
                if s >= 2 and c == 0:
                    act.wait_ge(turned, ONE + s - 1)
                nc.scalar.activation(pr[:, s % 2, c, 0:nk], score_ps(c, nk), ACT.Exp,
                                     bias=mx[:, s % 2, 2 + c:3 + c], scale=SC,
                                     accum_out=sm[:, s % 2, c:c + 1]).then_inc(exped, 1)

            def keep_out(t):
                act.wait_ge(summed, ONE + AH * (t + 1))
                nc.scalar.activation(o[:, t, :, :].rearrange("p h e -> p (h e)"), ps[:, 6 + t % 2, :],
                                     ACT.Copy).then_inc(out_kept, 1)

            def keep_weights(s):
                t, h = steps[s]
                nk = (t + 1) * P
                act.wait_ge(turned, ONE + s + 1)
                if s >= 2:
                    act.wait_ge(summed, ONE + s - 1)
                nc.scalar.activation(wT[:, s % 2, 0:nk],
                                     ps[:, 4:6, :].rearrange("p b n -> p (b n)")[:, 0:nk],
                                     ACT.Copy).then_inc(kept, 1)

            exps(0, 0)
            exps(0, 1)
            for s, (t, h) in enumerate(steps):
                if s + 1 < N:
                    exps(s + 1, 0)
                keep_weights(s)
                if s + 1 < N:
                    exps(s + 1, 1)
                if t and h == 1:
                    keep_out(t - 1)
            keep_out(NT - 1)
            act.wait_ge(mean, ONE + 1)
            nc.scalar.activation(st[:, 2, :, :], st[:, 1, :, :], ACT.Sqrt).then_inc(root, 1)


def sample_phase(nc, a, ps, ident, s_rqk, s_rv, s_aqk, s_av, rT, aT, lam):
    J = NS * RH
    R = 2 * J
    with Scope(nc) as ctx:
        def sb(n, shape, dt=F32):
            return ctx.enter_context(nc.sbuf_tensor("sa_" + n, shape, dt))

        def sem(n):
            return ctx.sem("sa_" + n)

        state = sb("state", [P, J, RDV])
        qz = sb("q_padded", [P, J * J])
        km = sb("k_masked", [NS, 2, RH * RDK])
        rn = sb("ret_normed", [J, RDV])
        junk = sb("junk", [R, BANK])
        st = sb("st", [R, 8])
        qb = sb("att_q_padded", [P, J * R])
        kT = sb("att_kT", [P, AH, NS])
        kpg = sb("key_pages", [P, 2, NPAGE, AH, PAGE])
        vpg = sb("value_pages", [P, 2, NPAGE, AH * ADV])
        sc = sb("scores", [R, PAST + 1])
        pr = sb("probs", [R, PAST + 1])
        pz = sb("probs_padded", [P, NPAGE, NS * (R + 8)])
        pn, pnT = sb("probs_self", [R, NS]), sb("probs_self_T", [NS, R])
        sel = sb("selectors", [R, 2 + NS + AH])
        o2, o3 = sb("out_rows", [R, AH, ADV]), sb("out", [NS, AH, ADV])
        on, osq = sb("out_normed", [NS, AH, ADV]), sb("out_squares", [NS, AH, ADV])
        ost = sb("out_st", [NS, 4, AH])
        gain = sb("gain", [P, 1])
        pt = sb("page_table", [1, NS * NPAGE], I32)
        s_tab, s_pt, s_state = sem("tables_loaded"), sem("page_table_loaded"), sem("states_loaded")
        k_in = [sem(f"key_pages{u}") for u in range(2)]
        v_in = [ctx.queue_sem(f"sa_value_pages{u}") for u in range(2)]
        zeroed, q_turned, q_kept = sem("padding_zeroed"), sem("q_turned"), sem("q_kept")
        kv_ready, state_new, stored = sem("outer_products"), sem("state_new"), sem("stored")
        r_out, r_sq, r_mean, r_root, r_norm = (sem("ret_" + n) for n in ("out", "squares", "mean", "root", "normed"))
        r_turned, r_kept = sem("ret_turned"), sem("ret_kept")
        km_ready, scored, s_used, s_evac = sem("k_masked"), sem("scored"), sem("keys_used"), sem("scores_kept")
        maxed, exped, p_turned, p_kept, v_used, summed = (sem(n) for n in (
            "maxed", "exped", "probs_turned", "probs_kept", "values_used", "values_summed"))
        o2_ready, picked, o3_ready, a_mean, a_root, a_norm, a_turned, a_kept = (sem(n) for n in (
            "rows_weighted", "rows_picked", "out_kept", "out_mean", "out_root", "out_normed", "out_turned",
            "out_columns_kept"))
        self_ready, self_turned = sem("self_ready"), sem("self_turned")
        chain = sem("chain")
        SCALE, SC = float(RDK) ** -0.5, float(ADQ) ** -0.5
        gamma = [float(np.exp(np.log(1.0 - 2.0 ** (-5.0 - h)))) for h in range(RH)]

        block = ctx.block()

        @block.sync
        def _(sp):
            sp.dma_start(pt[:, :], a["page_table"]).then_inc(s_pt, 16)
            sp.dma_start(sel[:, :], a["sel"]).then_inc(s_tab, 16)
            sp.dma_start(gain[:, :], a["g_subln"]).then_inc(s_tab, 16)
            sp.wait_ge(s_pt, ONE + 16)
            for b in range(NS):
                u = b % 2
                for pg in range(NPAGE):
                    n = b * NPAGE + pg
                    pid = sp.value_load(pt[0:1, n:n + 1], min_val=0, max_val=POOL - 1)
                    if b >= 2 and pg == 0:
                        sp.wait_ge(s_used, ONE + b - 1)
                    sp.dma_start(kpg[:, u, pg, :, :], a["cache_kT"][ds(pid, 1)].rearrange("o h p n -> p (o h) n")
                                 ).then_inc(k_in[u], 16)

        @block.gpsimd
        def _(pool):
            nc.gpsimd.memset(qz[:, :], 0.0).then_inc(zeroed, 1)
            nc.gpsimd.memset(qb[:, :], 0.0).then_inc(zeroed, 1)
            nc.gpsimd.memset(pz[:, :, :], 0.0).then_inc(zeroed, 1)
            pool.wait_ge(s_pt, ONE + 16)
            for b in range(NS):
                u = b % 2
                for pg in range(NPAGE):
                    n = b * NPAGE + pg
                    pid = pool.value_load(pt[0:1, n:n + 1], min_val=0, max_val=POOL - 1)
                    if b >= 2 and pg == 0:
                        pool.wait_ge(v_used, ONE + b - 1)
                    pool.dma_start(vpg[:, u, pg, :], a["cache_v"][ds(pid, 1)].rearrange("o p n -> p (o n)")
                                   ).then_inc(v_in[u], 16)

        @block.scalar
        def _(act):
            act.dma_start(state[:, :, :], a["state"].rearrange("b h k v -> k (b h) v")).then_inc(s_state, 16)
            act.wait_ge(r_out, ONE + 1)
            nc.scalar.activation(junk[0:J, 0:RDV], ps[0:J, 4, 0:RDV], ACT.Square,
                                 accum_out=st[0:J, 0:1]).then_inc(r_sq, 1)
            act.wait_ge(r_mean, ONE + 1)
            nc.scalar.activation(st[0:J, 2:3], st[0:J, 1:2], ACT.Sqrt).then_inc(r_root, 1)
            act.wait_ge(maxed, ONE + 1)
            nc.scalar.activation(pr[:, :], sc[:, :], ACT.Exp, bias=st[:, 5:6], scale=SC,
                                 accum_out=st[:, 6:7]).then_inc(exped, 1)
            act.wait_ge(a_mean, ONE + 1)
            nc.scalar.activation(ost[:, 2, :], ost[:, 1, :], ACT.Sqrt).then_inc(a_root, 1)
            act.wait_ge(state_new, ONE + NS)
            act.dma_start(a["o_ret_s"].rearrange("b h k v -> k (b h) v"), state[:, :, :]).then_inc(stored, 16)
            act.wait_ge(stored, ONE + 16)

        @block.tensor
        def _(pe):
            for bank, src, off in ((0, s_rqk, 0), (1, s_aqk, 0), (2, s_aqk, AH * 2 * ADQ)):
                for h in range(RH):
                    last = nc.tensor.transpose(ps[:, bank, h * NS:(h + 1) * NS],
                                               src[:, off + h * P:off + (h + 1) * P], ident[0:NS, 0:NS])
            last.then_inc(q_turned, 1)
            pe.wait_ge(q_kept, ONE + 1)
            for b in range(NS):
                pe.wait_ge(km_ready, ONE + b + 1)
                if b >= 2:
                    pe.wait_ge(state_new, ONE + b - 1)
                for h in range(RH):
                    last = nc.tensor.matmul(ps[:, 2 * (b % 2) + h // 2, (h % 2) * RDV:(h % 2 + 1) * RDV],
                                            km[:, b % 2, h * RDK:(h + 1) * RDK], s_rv[:, h * RDV:(h + 1) * RDV],
                                            start=True, stop=True)
                last.then_inc(kv_ready, 1)
            pe.wait_ge(state_new, ONE + NS)
            for j in range(J):
                last = nc.tensor.matmul(ps[0:J, 4, 0:RDV], qz[:, j * J:(j + 1) * J], state[:, j, :],
                                        start=(j == 0), stop=(j == J - 1))
            last.then_inc(r_out, 1)
            for b in range(NS):
                pe.wait_ge(k_in[b % 2], ONE + 16 * NPAGE * (b // 2 + 1))
                for h in range(AH):
                    j = b * AH + h
                    last = nc.tensor.matmul(ps[0:R, 5, :], qb[:, j * R:(j + 1) * R], kpg[:, b % 2, :, h, :],
                                            start=(j == 0), stop=(j == J - 1))
                last.then_inc(s_used, 1)
            for b in range(NS):
                for h in range(AH):
                    j = b * AH + h
                    last = nc.tensor.matmul(ps[0:R, 6, 0:1], qb[:, j * R:(j + 1) * R], kT[:, h, b:b + 1],
                                            start=(j == 0), stop=(j == J - 1))
            last.then_inc(scored, 1)
            pe.wait_ge(r_norm, ONE + 1)
            for half in range(2):
                last = nc.tensor.transpose(ps[:, 7, half * J:(half + 1) * J], rn[:, half * P:(half + 1) * P],
                                           ident[0:J, 0:J])
            last.then_inc(r_turned, 1)
            pe.wait_ge(exped, ONE + 1)
            for pg in range(NPAGE):
                last = nc.tensor.transpose(ps[:, 0, pg * R:(pg + 1) * R], pr[:, pg * PAGE:(pg + 1) * PAGE],
                                           ident[0:R, 0:R])
            last.then_inc(p_turned, 1)
            pe.wait_ge(self_ready, ONE + 1)
            nc.tensor.transpose(ps[0:NS, 1, 0:R], pn[:, :], ident[0:R, 0:R]).then_inc(self_turned, 1)
            pe.wait_ge(p_kept, ONE + 2)
            for b in range(NS):
                pe.wait_ge(v_in[b % 2], 16 * NPAGE * (b // 2 + 1))
                for pg in range(NPAGE):
                    last = nc.tensor.matmul(ps[0:R, 3, :], pz[:, pg, b * R:(b + 1) * R], vpg[:, b % 2, pg, :],
                                            start=(b == 0 and pg == 0), stop=False)
                last.then_inc(v_used, 1)
            nc.tensor.matmul(ps[0:R, 3, :], pnT[:, :], s_av[:, :], start=False, stop=True).then_inc(summed, 1)
            pe.wait_ge(o2_ready, ONE + 1)
            nc.tensor.matmul(ps[0:NS, 2, :], sel[:, 2:2 + NS], o2[:, :, :].rearrange("p h e -> p (h e)"),
                             start=True, stop=True).then_inc(picked, 1)
            pe.wait_ge(a_norm, ONE + 1)
            pe.wait_ge(p_kept, ONE + 2)
            for h in range(AH):
                last = nc.tensor.transpose(ps[:, 4, h * NS:(h + 1) * NS], on[:, h, :], ident[0:NS, 0:NS])
            last.then_inc(a_turned, 1)

        @block.vector
        def _(dve):
            link = Chain(dve, chain)
            def mask_k(b):
                if b >= 2:
                    dve.wait_ge(kv_ready, ONE + b - 1)
                nc.vector.tensor_scalar(km[:, b % 2, :], s_rqk[:, RH * RDK:], ident[0:NS, b:b + 1], SCALE,
                                        ALU.mult, ALU.mult).then_inc(km_ready, 1)

            mask_k(0)
            mask_k(1)
            dve.wait_ge(zeroed, ONE + 3)
            dve.wait_ge(q_turned, ONE + 1)
            by_head = "p (h b) -> p b h"
            nc.vector.tensor_copy(qz[:, 0:J * J:J + 1].rearrange("p (b h) -> p b h", b=NS),
                                  ps[:, 0, 0:J].rearrange(by_head, b=NS))
            for c in range(2):
                rows = slice(c * ADQ, (c + 1) * ADQ)
                nc.vector.tensor_copy(qb[rows, c:J * R:R + 2].rearrange("p (b h) -> p b h", b=NS),
                                      ps[rows, 1, 0:J].rearrange(by_head, b=NS))
            nc.vector.tensor_copy(kT[:, :, :], ps[:, 2, 0:J].rearrange("p (h b) -> p h b", b=NS)).then_inc(q_kept, 1)
            dve.wait_ge(s_state, ONE + 16)
            for b in range(NS):
                dve.wait_ge(kv_ready, ONE + b + 1)
                if b + 2 < NS:
                    mask_k(b + 2)
                for h in range(RH):
                    j = b * RH + h
                    last = nc.vector.scalar_tensor_tensor(
                        out=state[:, j, :], in0=state[:, j, :], scalar=gamma[h],
                        in1=ps[:, 2 * (b % 2) + h // 2, (h % 2) * RDV:(h % 2 + 1) * RDV],
                        op0=ALU.mult, op1=ALU.add)
                last.then_inc(state_new, 1)
            dve.wait_ge(r_sq, ONE + 1)
            nc.vector.tensor_scalar(st[0:J, 1:2], st[0:J, 0:1], 1.0 / RDV, EPS, ALU.mult, ALU.add).then_inc(r_mean, 1)
            dve.wait_ge(r_root, ONE + 1)
            link(nc.vector.reciprocal(st[0:J, 3:4], st[0:J, 2:3]))
            nc.vector.tensor_scalar(rn[:, :], ps[0:J, 4, 0:RDV], st[0:J, 3:4], None, ALU.mult).then_inc(r_norm, 1)
            dve.wait_ge(scored, ONE + 1)
            nc.vector.tensor_copy(sc[:, 0:PAST], ps[0:R, 5, :])
            link(nc.vector.tensor_copy(sc[:, PAST:], ps[0:R, 6, 0:1]))
            link(nc.vector.tensor_reduce(st[:, 4:5], sc[:, :], AX_X, ALU.max))
            nc.vector.tensor_scalar(st[:, 5:6], st[:, 4:5], -SC, None, ALU.mult).then_inc(maxed, 1)
            dve.wait_ge(r_turned, ONE + 1)
            for half in range(2):
                last = nc.vector.tensor_copy(rT[:, half:KD:2, SEQ:T],
                                             ps[:, 7, half * J:(half + 1) * J].rearrange("p (b h) -> p h b", b=NS))
            last.then_inc(r_kept, 1)
            dve.wait_ge(exped, ONE + 1)
            dve.wait_ge(s_tab, ONE + 32)
            nc.vector.tensor_scalar(pn[:, :], sel[:, 2:2 + NS], pr[:, PAST:], None, ALU.mult).then_inc(self_ready, 1)
            link(nc.vector.reciprocal(st[:, 7:8], st[:, 6:7]))
            link(nc.vector.scalar_tensor_tensor(out=st[:, 4:5], in0=sel[:, 1:2], scalar=lam[0:R, 0:1],
                                                in1=sel[:, 0:1], op0=ALU.mult, op1=ALU.subtract))
            link(nc.vector.tensor_scalar(st[:, 5:6], st[:, 4:5], st[:, 7:8], -1.0, ALU.mult, ALU.mult))
            dve.wait_ge(p_turned, ONE + 1)
            for pg in range(NPAGE):
                last = nc.vector.tensor_copy(
                    pz[:, pg, :].rearrange("p (b w) -> p b w", b=NS)[:, :, 0:8],
                    ps[:, 0, pg * R:(pg + 1) * R].rearrange("p (b w) -> p b w", b=NS))
            last.then_inc(p_kept, 1)
            dve.wait_ge(self_turned, ONE + 1)
            nc.vector.tensor_copy(pnT[:, :], ps[0:NS, 1, 0:R]).then_inc(p_kept, 1)
            dve.wait_ge(summed, ONE + 1)
            nc.vector.scalar_tensor_tensor(
                out=o2[:, :, :], in0=ps[0:R, 3, :].rearrange("p (h e) -> p h e", h=AH), scalar=st[:, 5:6],
                in1=sel[:, 2 + NS:].unsqueeze(2).to_broadcast([R, AH, ADV]), op0=ALU.mult,
                op1=ALU.mult).then_inc(o2_ready, 1)
            dve.wait_ge(picked, ONE + 1)
            link(nc.vector.tensor_copy(o3[:, :, :], ps[0:NS, 2, :].rearrange("p (h e) -> p h e", h=AH)))
            link(nc.vector.tensor_tensor(osq[:, :, :], o3[:, :, :], o3[:, :, :], ALU.mult))
            link(nc.vector.tensor_reduce(ost[:, 0, :], osq[:, :, :], AX_X, ALU.add))
            nc.vector.tensor_scalar(ost[:, 1, :], ost[:, 0, :], 1.0 / ADV, SUB_EPS, ALU.mult, ALU.add).then_inc(a_mean, 1)
            dve.wait_ge(a_root, ONE + 1)
            link(nc.vector.reciprocal(ost[:, 3, :], ost[:, 2, :]))
            nc.vector.tensor_tensor(on[:, :, :], o3[:, :, :], ost[:, 3, :].unsqueeze(2).to_broadcast([NS, AH, ADV]),
                                    ALU.mult).then_inc(a_norm, 1)
            dve.wait_ge(a_turned, ONE + 1)
            nc.vector.tensor_scalar(aT[:, :, SEQ:T], ps[:, 4, 0:J].rearrange("p (h b) -> p h b", b=NS),
                                    gain[:, 0:1], 1.0 - LAM_INIT, ALU.mult, ALU.mult).then_inc(a_kept, 1)


def merge_phase(nc, a, ps, zT, rT, aT, mT):
    NW = 2 * KD + KD + AH
    with Scope(nc) as ctx:
        w = ctx.enter_context(nc.sbuf_tensor("mg_w", [P, 2, NW, P], F32))
        sg = ctx.enter_context(nc.sbuf_tensor("mg_gates", [P, 2, 2, TB], F32))
        pd = ctx.enter_context(nc.sbuf_tensor("mg_products", [P, 2, 2, TB], F32))

        def sem(n):
            return ctx.sem("mg_" + n)

        w_in = [sem(f"w_loaded{u}") for u in range(2)]
        ready, gated, mult, merged = ([sem(f"{n}{s}") for s in range(2)] for n in
                                      ("products_ready", "gates_ready", "gated", "merged"))
        steps = [(u, b) for u in range(2) for b in range(3)]

        block = ctx.block()

        @block.sync
        def _(sp):
            def load(it, u):
                sp.dma_start(w[:, u, :, :], a["w_merge"][ds(2 * it + u, 1)].rearrange("o p k n -> p (o k) n")
                             ).then_inc(w_in[u], 16)

            load(0, 0)
            load(0, 1)
            with sp.Fori(1, KD // 2) as it:
                sp.wait_ge(ready[0], ONE + 3 * it - 1)
                load(it, 0)
                sp.wait_ge(ready[1], ONE + 3 * it)
                load(it, 1)

        @block.tensor
        def _(pe):
            with pe.Fori(0, KD // 2) as it:
                for k, (u, b) in enumerate(steps):
                    s, lo, hi = k % 2, *BLOCKS[b]
                    if b == 0:
                        pe.wait_ge(w_in[u], ONE + 16 * it + 16)
                    pe.wait_ge(merged[s], ONE + 3 * it + k // 2)
                    n = 0
                    for bank, x, cnt in ((0, zT, KD), (1, zT, KD), (2, rT, KD), (3, aT, AH)):
                        for c in range(cnt):
                            last = nc.tensor.matmul(ps[:, 4 * s + bank, 0:TB], w[:, u, n, :], x[:, c, lo:hi],
                                                    start=(c == 0), stop=(c == cnt - 1))
                            n += 1
                    last.then_inc(ready[s], 1)

        @block.scalar
        def _(act):
            with act.Fori(0, KD // 2) as it:
                for k in range(6):
                    s = k % 2
                    act.wait_ge(ready[s], ONE + 3 * it + k // 2 + 1)
                    act.wait_ge(merged[s], ONE + 3 * it + k // 2)
                    nc.scalar.activation(sg[:, s, :, :], ps[:, 4 * s:4 * s + 2, 0:TB],
                                         ACT.Sigmoid).then_inc(gated[s], 1)

        @block.vector
        def _(dve):
            with dve.Fori(0, KD // 2) as it:
                for k, (u, b) in enumerate(steps):
                    s, lo, hi = k % 2, *BLOCKS[b]
                    n = 3 * it + k // 2
                    dve.wait_ge(gated[s], ONE + n + 1)
                    nc.vector.tensor_tensor(pd[:, s, :, :], sg[:, s, :, :], ps[:, 4 * s + 2:4 * s + 4, 0:TB],
                                            ALU.mult).then_inc(mult[s], 1)
                    dve.wait_ge(mult[s], ONE + n + 1)
                    nc.vector.tensor_tensor(mT[:, ds(2 * it + u, 1), lo:hi], pd[:, s, 0:1, :], pd[:, s, 1:2, :],
                                            ALU.add).then_inc(merged[s], 1)


def residual_phase(nc, a, ps, mT, h_dram):
    with Scope(nc) as ctx:
        w = ctx.enter_context(nc.sbuf_tensor("rs_w", [P, KD, D], F32))
        mc = ctx.enter_context(nc.sbuf_tensor("rs_m_tile", [P, 2, KD, P], F32))
        x = ctx.enter_context(nc.sbuf_tensor("rs_x", [P, 2, D], F32))
        h = ctx.enter_context(nc.sbuf_tensor("rs_h", [P, 2, D], F32))

        def sem(n):
            return ctx.sem("rs_" + n)

        s_w = sem("w_loaded")
        m_in, x_in, ready, added, out = ([sem(f"{n}{u}") for u in range(2)] for n in
                                         ("m_tile_ready", "x_loaded", "product_ready", "added", "stored"))

        def over_tiles(eng, step):
            with eng.Fori(0, NT // 2) as it:
                for u in range(2):
                    step(it, u, P)
            step(NT // 2, 0, NS)

        block = ctx.block()

        @block.sync
        def _(sp):
            sp.dma_start(w[:, :, :], a["w_out"]).then_inc(s_w, 16)

            def load(it, u, rows):
                sp.wait_ge(added[u], ONE + it)
                sp.dma_start(x[0:rows, u, :], a["x"][ds((2 * it + u) * P, rows), :]).then_inc(x_in[u], 16)
            over_tiles(sp, load)

        @block.scalar
        def _(act):
            def store(it, u, rows):
                act.wait_ge(added[u], ONE + it + 1)
                act.dma_start(h_dram[ds((2 * it + u) * P, rows), :], h[0:rows, u, :]).then_inc(out[u], 16)
            over_tiles(act, store)
            act.wait_ge(out[0], ONE + 16 * (NT // 2 + 1))
            act.wait_ge(out[1], ONE + 16 * (NT // 2))

        @block.gpsimd
        def _(pool):
            def copy(it, u, rows):
                pool.wait_ge(ready[u], ONE + it)
                nc.gpsimd.tensor_copy(mc[:, u, :, 0:rows], mT[:, :, ds((2 * it + u) * P, rows)]).then_inc(m_in[u], 1)
            over_tiles(pool, copy)

        @block.tensor
        def _(pe):
            pe.wait_ge(s_w, ONE + 16)

            def product(it, u, rows):
                pe.wait_ge(m_in[u], ONE + it + 1)
                pe.wait_ge(added[u], ONE + it)
                for b in range(2):
                    for c in range(KD):
                        last = nc.tensor.matmul(ps[0:rows, 2 * u + b, :], mc[:, u, c, 0:rows],
                                                w[:, c, b * BANK:(b + 1) * BANK], start=(c == 0), stop=(c == KD - 1))
                last.then_inc(ready[u], 1)
            over_tiles(pe, product)

        @block.vector
        def _(dve):
            def add(it, u, rows):
                dve.wait_ge(ready[u], ONE + it + 1)
                dve.wait_ge(x_in[u], ONE + 16 * it + 16)
                dve.wait_ge(out[u], ONE + 16 * it)
                nc.vector.tensor_tensor(h[0:rows, u, :], x[0:rows, u, :],
                                        ps[0:rows, 2 * u:2 * u + 2, :].rearrange("p b n -> p (b n)"),
                                        ALU.add).then_inc(added[u], 1)
            over_tiles(dve, add)


def routing_phase(nc, a, ps, ident, z2T, gT, iT, jT):
    NTT = NT + 1
    with Scope(nc) as ctx:
        def sb(n, shape, dt=F32):
            return ctx.enter_context(nc.sbuf_tensor("rt_" + n, shape, dt))

        def sem(n):
            return ctx.sem("rt_" + n)

        wq = sb("wq", [P, 2, KD, P])
        sk = sb("sub_keys", [P, 2 * PH, NK])
        qT = sb("qT", [P, 2, T])
        sc, sc2 = sb("scores", [P, 2, NTT, NK]), sb("scores_rest", [P, NTT, NK])
        v = sb("best", [P, 2, NTT, TOPK])
        vi = sb("best_index", [P, 2, NTT, TOPK], U32)
        vf = sb("best_index_f", [P, 2, NTT, TOPK])
        R = TOPK // 2
        LASTROW = R + 1
        NSUM = (LASTROW + 1) * R
        cs, cs2 = sb("sums", [P, NTT, NSUM]), sb("sums_rest", [P, NTT, NSUM])
        pos, prc = sb("pos", [P, NTT, TOPK], U32), sb("pos_row_column", [P, 2, NTT, TOPK], U32)
        prcf, ranks = sb("pos_row_column_f", [P, 2, NTT, TOPK]), sb("ranks", [P, 2, NTT, TOPK])
        index = sb("index_by_rank", [P, 2, NTT, TOPK])
        flag = sb("flag", [P, 2, NTT, TOPK])
        hot = sb("rank_onehots", [P, 2 * NTT, TOPK, TOPK])
        it_i, it_f = sb("iota_i", [P, TOPK], I32), sb("iota_f", [P, TOPK])
        best = sb("best_sums", [P, NTT, TOPK])
        top = sb("top", [P, NTT, PH, TOPK])
        tij = sb("top_ij", [P, 2 * NTT, PH, TOPK])
        sub, ex, gt = sb("shifted", [P, NTT, PH, TOPK]), sb("exps", [P, NTT, PH, TOPK]), sb("gates", [P, NTT, PH, TOPK])
        carrier, pool_carrier = sb("wait_carrier", [P, 1]), sb("pool_wait_carrier", [P, 1])
        sm = sb("sums_e", [P, 2, NTT * PH])

        s_sk = sem("sub_keys_loaded")
        w_in = [sem(f"wq_loaded{c}") for c in range(2)]
        q_ready, q_kept = [sem(f"q_ready{c}") for c in range(2)], [sem(f"q_kept{c}") for c in range(2)]
        s_ready, s_kept = sem("scores_ready"), sem("scores_kept")
        s_kept_c = [sem(f"scores_kept{c}") for c in range(2)]
        s_used = [sem(f"scores_used{c}") for c in range(2)]
        chain, zeroed, it_ready = sem("chain"), sem("zeroed"), sem("iota_ready")
        pos_ready, decoded, pool_chain = sem("pos_ready"), sem("ranks_ready"), sem("pool_chain")
        hots_ready, picked, looked_up = sem("onehots_ready"), sem("onehots_times_index"), sem("looked_up")
        shifted, exped, gates_ready, turned, kept = (sem(n) for n in (
            "shifted", "exped", "gates_ready", "turned", "kept"))
        GROUPS = [(0, 3), (3, 6), (6, 9)]
        NEGBIG = -3.0e38
        NLINK = 2 * 4 + 1 + 5
        NDECODE = 4

        block = ctx.block()

        @block.sync
        def _(sp):
            sp.dma_start(sk[:, :, :], a["sub_keysT"]).then_inc(s_sk, 16)
            with sp.Fori(0, PH) as h:
                for c in range(2):
                    sp.wait_ge(q_ready[c], ONE + h)
                    sp.dma_start(wq[:, c, :, :], a["w_query"][ds(2 * h + c, 1)].rearrange("o p k n -> p (o k) n")
                                 ).then_inc(w_in[c], 16)

        @block.gpsimd
        def _(pool):
            for c in range(2):
                nc.gpsimd.memset(sc[:, c, NT, :], 0.0).then_inc(zeroed, 1)
            nc.gpsimd.iota(it_i[:, :], pattern=[[1, TOPK]], base=0, channel_multiplier=0).then_inc(zeroed, 1)
            pool.wait_ge(zeroed, ONE + 3)
            nc.gpsimd.tensor_copy(it_f[:, :], it_i[:, :]).then_inc(it_ready, 1)

            pool.wait_ge(it_ready, ONE + 1)

            def carry():
                nc.gpsimd.tensor_tensor(pool_carrier[:, :], it_f[:, 0:1], it_f[:, 0:1], ALU.mult)

            with pool.Fori(0, PH) as h:
                step = Chain(pool, pool_chain, h * NDECODE)
                pool.wait_ge(pos_ready, ONE + h + 1)
                pool.wait_ge(picked, ONE + h)
                row, col = prcf[:, 0, :, :], prcf[:, 1, :, :]
                carry()
                nc.gpsimd.tensor_copy(index[:, :, :, :], vf[:, :, :, :])
                step(nc.gpsimd.tensor_copy(prcf[:, :, :, :], prc[:, :, :, :]))
                carry()
                nc.gpsimd.tensor_scalar(flag[:, 0, :, :], row, float(LASTROW), None, ALU.is_equal)
                nc.gpsimd.tensor_scalar(flag[:, 1, :, :], row, 1.0, float(R), ALU.is_equal, ALU.mult)
                step(nc.gpsimd.tensor_scalar(ranks[:, 0, :, :], row, -1.0, 0.0, ALU.add, ALU.max))
                step(nc.gpsimd.tensor_tensor(flag[:, 0, :, :], flag[:, 0, :, :], col, ALU.mult))
                nc.gpsimd.tensor_tensor(ranks[:, 0, :, :], ranks[:, 0, :, :], flag[:, 0, :, :], ALU.add)
                step(nc.gpsimd.tensor_tensor(ranks[:, 1, :, :], col, flag[:, 0, :, :], ALU.subtract))
                nc.gpsimd.tensor_tensor(ranks[:, 1, :, :], ranks[:, 1, :, :], flag[:, 1, :, :], ALU.add
                                        ).then_inc(decoded, 1)
                assert step.n == NDECODE, step.n
                pool.wait_ge(hots_ready, ONE + h + 1)
                nc.gpsimd.tensor_tensor(hot[:, :, :, :], hot[:, :, :, :],
                                        index[:, :, :, :].rearrange("p c t r -> p (c t) r").unsqueeze(2)
                                        .to_broadcast([P, 2 * NTT, TOPK, TOPK]), ALU.mult).then_inc(picked, 1)

        @block.tensor
        def _(pe):
            pe.wait_ge(s_sk, ONE + 16)
            with pe.Fori(0, PH) as h:
                for c in range(2):
                    pe.wait_ge(w_in[c], ONE + 16 * h + 16)
                    pe.wait_ge(q_kept[c], ONE + h)
                    for b, (lo, hi) in enumerate(BLOCKS):
                        for k in range(KD):
                            last = nc.tensor.matmul(ps[:, 3 * c + b, 0:TB], wq[:, c, k, :], z2T[:, k, lo:hi],
                                                    start=(k == 0), stop=(k == KD - 1))
                    last.then_inc(q_ready[c], 1)
                for c in range(2):
                    pe.wait_ge(q_kept[c], ONE + h + 1)
                    for n, (lo, hi) in enumerate(GROUPS):
                        m = 3 * c + n
                        if m >= 2:
                            pe.wait_ge(s_kept, ONE + 6 * h + m - 1)
                        else:
                            pe.wait_ge(s_kept, ONE + 6 * h)
                        for t in range(lo, hi):
                            r = P if t < NT else NS
                            last = nc.tensor.matmul(ps[0:r, 6 + m % 2, (t - lo) * NK:(t - lo + 1) * NK],
                                                    qT[:, c, t * P:t * P + r],
                                                    sk[:, ds(2 * h + c, 1), :].rearrange("p o n -> p (o n)"),
                                                    start=True, stop=True)
                        last.then_inc(s_ready, 1)
            pe.wait_ge(gates_ready, ONE + 1)
            pe.wait_ge(s_kept, ONE + 6 * PH)
            for n, src in enumerate((gt, tij[:, 0:NTT], tij[:, NTT:2 * NTT])):
                for t, lo, r in TILES:
                    last = nc.tensor.transpose(ps[:, t // 4, (t % 4) * P:(t % 4) * P + r],
                                               src[0:r, t, :, :].rearrange("p h k -> p (h k)"), ident[0:r, 0:r])
                last.then_inc(turned, 1)
                pe.wait_ge(kept, ONE + n + 1)

        @block.scalar
        def _(act):
            act.wait_ge(zeroed, ONE + 3)
            with act.Fori(0, PH) as h:
                for c in range(2):
                    act.wait_ge(q_ready[c], ONE + h + 1)
                    act.wait_ge(s_ready, ONE + 6 * h)
                    nc.scalar.activation(qT[:, c, :].rearrange("p (b n) -> p b n", b=3), ps[:, 3 * c:3 * c + 3, 0:TB],
                                         ACT.Copy).then_inc(q_kept[c], 1)
                for c in range(2):
                    act.wait_ge(s_used[c], ONE + h)
                    for n, (lo, hi) in enumerate(GROUPS):
                        m = 3 * c + n
                        act.wait_ge(s_ready, ONE + 6 * h + m + 1)
                        parts = [(lo, hi, P)] if hi <= NT else [(lo, NT, P), (NT, hi, NS)]
                        for x, y, r in parts:
                            last = nc.scalar.activation(
                                sc[0:r, c, x:y, :],
                                ps[0:r, 6 + m % 2, (x - lo) * NK:(y - lo) * NK].rearrange("p (t n) -> p t n", n=NK),
                                ACT.Copy)
                        last.then_inc(s_kept, 1)
            act.wait_ge(shifted, ONE + 1)
            nc.scalar.activation(ex[:, :, :, :].rearrange("p t h k -> p (t h k)"),
                                 sub[:, :, :, :].rearrange("p t h k -> p (t h k)"), ACT.Exp).then_inc(exped, 1)
            for n, dst in enumerate((gT, iT, jT)):
                act.wait_ge(turned, ONE + n + 1)
                nc.scalar.activation(dst[:, :], ps[:, 0:3, :].rearrange("p b n -> p (b n)")[:, 0:T],
                                     ACT.Copy).then_inc(kept, 1)

        @block.vector
        def _(dve):
            dve.wait_ge(it_ready, ONE + 1)

            def onehots(h):
                dve.wait_ge(decoded, ONE + h + 1)
                dve.wait_ge(looked_up, ONE + h)
                nc.vector.tensor_tensor(
                    hot[:, :, :, :],
                    ranks[:, :, :, :].rearrange("p c t k -> p (c t) k").unsqueeze(3)
                    .to_broadcast([P, 2 * NTT, TOPK, TOPK]),
                    it_f[:, :].unsqueeze(1).unsqueeze(1).to_broadcast([P, 2 * NTT, TOPK, TOPK]), ALU.is_equal
                    ).then_inc(hots_ready, 1)

            def look_up(h):
                dve.wait_ge(picked, ONE + h + 1)
                nc.vector.tensor_reduce(tij[:, :, ds(h, 1), :].rearrange("p t o k -> p t (o k)"),
                                        hot[:, :, :, :], AX_X, ALU.add).then_inc(looked_up, 1)

            def head(h, first):
                link = Chain(dve, chain, h * NLINK)

                def carry():
                    nc.vector.memset(carrier[:, :], 0.0)

                def top16(val, idx, src, rest):
                    for t in range(NTT):
                        last = nc.vector.max(val(t)[:, 0:8], src(t))
                    link(last)
                    carry()
                    for t in range(NTT):
                        nc.vector.max_index(idx(t)[:, 0:8], val(t)[:, 0:8], src(t))
                        last = nc.vector.match_replace(rest(t), val(t)[:, 0:8], src(t), NEGBIG)
                    link(last)
                    carry()
                    for t in range(NTT):
                        last = nc.vector.max(val(t)[:, 8:16], rest(t))
                    link(last)
                    carry()
                    for t in range(NTT):
                        last = nc.vector.max_index(idx(t)[:, 8:16], val(t)[:, 8:16], rest(t))
                    return last

                for c in range(2):
                    dve.wait_ge(s_kept, ONE + 6 * h + 3 * c + 3)
                    carry()
                    last = top16(lambda t: v[:, c, t, :], lambda t: vi[:, c, t, :], lambda t: sc[:, c, t, :],
                                 lambda t: sc2[:, t, :])
                    last.then_inc(s_used[c], 1)
                    if c == 0 and not first:
                        onehots(h - 1)
                    dve.wait_ge(s_used[c], ONE + h + 1)
                    link(nc.vector.tensor_copy(vf[:, c, :, :], vi[:, c, :, :]))

                def half(c, lo, hi):
                    return v[:, c, :, lo:hi]
                nc.vector.tensor_tensor(cs[:, :, 0:2 * R], half(1, 0, TOPK),
                                        half(0, 0, 1).to_broadcast([P, NTT, TOPK]), ALU.add)
                nc.vector.tensor_tensor(cs[:, :, LASTROW * R:NSUM], half(0, R, TOPK),
                                        half(1, 0, 1).to_broadcast([P, NTT, R]), ALU.add)
                link(nc.vector.tensor_tensor(
                    cs[:, :, 2 * R:LASTROW * R].rearrange("p t (i j) -> p t i j", j=R),
                    half(0, 1, R).unsqueeze(3).to_broadcast([P, NTT, R - 1, R]),
                    half(1, 0, R).unsqueeze(2).to_broadcast([P, NTT, R - 1, R]), ALU.add))
                carry()
                link(top16(lambda t: best[:, t, :], lambda t: pos[:, t, :], lambda t: cs[:, t, :],
                           lambda t: cs2[:, t, :]))
                nc.vector.tensor_scalar(prc[:, 0, :, :], pos[:, :, :], 3, None, ALU.logical_shift_right)
                nc.vector.tensor_scalar(prc[:, 1, :, :], pos[:, :, :], R - 1, None, ALU.bitwise_and
                                        ).then_inc(pos_ready, 1)
                link(nc.vector.tensor_copy(top[:, :, ds(h, 1), :].rearrange("p t o k -> p t (o k)"), best[:, :, :]))
                if not first:
                    look_up(h - 1)
                assert link.n == NLINK, link.n

            head(0, True)
            with dve.Fori(1, PH) as h:
                head(h, False)
            onehots(PH - 1)
            look_up(PH - 1)
            dve.wait_ge(looked_up, ONE + PH)
            link = Chain(dve, chain, PH * NLINK)
            nc.vector.tensor_tensor(sub[:, :, :, :], top[:, :, :, :],
                                    top[:, :, :, 0:1].to_broadcast([P, NTT, PH, TOPK]), ALU.subtract
                                    ).then_inc(shifted, 1)
            dve.wait_ge(exped, ONE + 1)
            link(nc.vector.tensor_reduce(sm[:, 0, :].rearrange("p (t h) -> p t h", h=PH), ex[:, :, :, :], AX_X, ALU.add))
            link(nc.vector.reciprocal(sm[:, 1, :], sm[:, 0, :]))
            nc.vector.tensor_tensor(gt[:, :, :, :], ex[:, :, :, :],
                                    sm[:, 1, :].rearrange("p (t h) -> p t h", h=PH).unsqueeze(3)
                                    .to_broadcast([P, NTT, PH, TOPK]), ALU.mult).then_inc(gates_ready, 1)


def gate_phase(nc, a, ps, gT, iT, jT, g_dram, g_sample):
    with Scope(nc) as ctx:
        def sb(n, shape, dt=F32):
            return ctx.enter_context(nc.sbuf_tensor("ga_" + n, shape, dt))

        def sem(n):
            return ctx.sem("ga_" + n)

        GT = 8
        PER = P // GT
        SETS = 4
        io_i, io = sb("iota_i", [P, NK], I32), sb("iota", [P, NK])
        oi, oj = sb("onehot_i", [P, SETS, GT, NK]), sb("onehot_j", [P, 2, GT, NK])
        stage = sb("stage", [P, 2, NK, P])
        io_ready = sem("iota_ready")
        hot_i, hot_j, weighed, done, kept = ([sem(f"{n}{s}") for s in range(SETS)] for n in (
            "onehots_i_ready", "onehots_j_ready", "weighed", "products_done", "kept"))
        out = [sem(f"stored{u}") for u in range(2)]

        block = ctx.block()

        def over_steps(eng, step, tile=None):
            with eng.Fori(0, NT // 2) as tp:
                for u in range(2):
                    if tile:
                        tile(tp, u)
                    with eng.Fori(0, PER // SETS) as g:
                        for s in range(SETS):
                            step((2 * tp + u) * (PER // SETS) + g, s, u, (2 * tp + u) * P + (SETS * g + s) * GT,
                                 (SETS * g + s) * GT)
            step(NT * PER // SETS, 0, None, SEQ, 0)

        @block.gpsimd
        def _(pool):
            nc.gpsimd.iota(io_i[:, :], pattern=[[1, NK]], base=0, channel_multiplier=0).then_inc(io_ready, 1)
            pool.wait_ge(io_ready, ONE + 1)
            nc.gpsimd.tensor_copy(io[:, :], io_i[:, :]).then_inc(io_ready, 1)

            def weigh(n, s, u, col, local):
                pool.wait_ge(hot_i[s], ONE + n + 1)
                nc.gpsimd.tensor_tensor(oi[:, s, :, :], oi[:, s, :, :],
                                        gT[:, ds(col, GT)].unsqueeze(2).to_broadcast([P, GT, NK]),
                                        ALU.mult).then_inc(weighed[s], 1)
            over_steps(pool, weigh)

        @block.vector
        def _(dve):
            dve.wait_ge(io_ready, ONE + 2)

            def onehots(n, s, u, col, local):
                for hot, slot, index, ready, read in (
                        (oi, s, iT, hot_i[s], (done[s], n)),
                        (oj, s % 2, jT, hot_j[s], (done[(s + 2) % SETS], n + s // 2))):
                    dve.wait_ge(read[0], ONE + read[1])
                    last = nc.vector.tensor_tensor(
                        hot[:, slot, :, :], io[:, :].unsqueeze(1).to_broadcast([P, GT, NK]),
                        index[:, ds(col, GT)].unsqueeze(2).to_broadcast([P, GT, NK]), ALU.is_equal)
                    last.then_inc(ready, 1)
            over_steps(dve, onehots)

        @block.tensor
        def _(pe):
            def products(n, s, u, col, local):
                pe.wait_ge(hot_j[s], ONE + n + 1)
                pe.wait_ge(weighed[s], ONE + n + 1)
                pe.wait_ge(kept[s], ONE + n)
                for k in range(GT):
                    last = nc.tensor.matmul(ps[:, 2 * s + k // 4, (k % 4) * NK:(k % 4 + 1) * NK], oj[:, s % 2, k, :],
                                            oi[:, s, k, :], start=True, stop=True)
                last.then_inc(done[s], 1)
            over_steps(pe, products)

        @block.scalar
        def _(act):
            def keep(n, s, u, col, local):
                act.wait_ge(done[s], ONE + n + 1)
                dst = g_sample[:, :, :] if u is None else stage[:, u, :, ds(local, GT)]
                nc.scalar.activation(dst.rearrange("p i t -> p t i"),
                                     ps[:, 2 * s:2 * s + 2, :].rearrange("p b (t i) -> p (b t) i", i=NK),
                                     ACT.Copy).then_inc(kept[s], 1)

            def tile(tp, u):
                act.wait_ge(out[u], ONE + 16 * tp)
            over_steps(act, keep, tile)

        @block.sync
        def _(sp):
            with sp.Fori(0, NT // 2) as tp:
                for u in range(2):
                    for s in range(SETS):
                        sp.wait_ge(kept[s], ONE + (2 * tp + u + 1) * (PER // SETS))
                    sp.dma_start(g_dram[:, :, ds((2 * tp + u) * P, P)].rearrange("i j t -> j i t"),
                                 stage[:, u, :, :]).then_inc(out[u], 16)
            for u in range(2):
                sp.wait_ge(out[u], ONE + 16 * (NT // 2))


def expert_phase(nc, a, ps, ident, z2T, g_dram, g_sample, h_dram, top, left):
    zh = top.enter_context(nc.sbuf_tensor("z2_hi", [P, KD, T], F32R, side="right"))
    zl = top.enter_context(nc.sbuf_tensor("z2_lo", [P, KD, T], F32R, side="right"))
    with Scope(nc) as ctx:
        s_hi, s_lo = ctx.sem("sp_z_hi"), ctx.sem("sp_z_lo")
        block = ctx.block()

        @block.scalar
        def _(act):
            for k in range(KD):
                nc.scalar.activation(zh[:, k, :], z2T[:, k, :], ACT.Copy).then_inc(s_hi, 1)

        @block.vector
        def _(dve):
            for k in range(KD):
                dve.wait_ge(s_hi, ONE + k + 1)
                nc.vector.tensor_tensor(zl[:, k, :], z2T[:, k, :], zh[:, k, :].bitcast(F32),
                                        ALU.subtract).then_inc(s_lo, 1)
    left.close()

    NG = NK // GC
    NB = KD * len(BLOCKS)
    OUT = [(k, lo, hi) for k in range(KD) for lo, hi in BLOCKS]
    outer = ExitStack()
    with outer:
        accT = outer.enter_context(nc.sbuf_tensor("accT", [P, KD, T], F32))
        with Scope(nc) as ctx:
            def sb(n, shape, dt=F32):
                return ctx.enter_context(nc.sbuf_tensor("ex_" + n, shape, dt))

            def sem(n):
                return ctx.sem("ex_" + n)

            Ur, Vr = sb("u", [P, KD, P]), sb("v", [P, D])
            Uh, Ul = sb("u_hi", [P, 2, KD, P], F32R), sb("u_lo", [P, 2, KD, P], F32R)
            Vh, Vl = sb("v_hi", [P, GC, D], F32R), sb("v_lo", [P, GC, D], F32R)
            G = sb("gates", [P, SEQ])
            gl = sb("gelu", [P, 2, T])
            Ah, Al = sb("a_hi", [P, GC, T], F32R), sb("a_lo", [P, GC, T], F32R)
            acc_set, u_in = sem("acc_zeroed"), sem("u_loaded")
            v_in, g_in = ctx.queue_sem("ex_v_loaded"), ctx.queue_sem("ex_gates_loaded")
            u_hi, u_lo, v_hi, v_lo = sem("u_hi_ready"), sem("u_lo_ready"), sem("v_hi_ready"), sem("v_lo_ready")
            h_ready, gelu, weighed = sem("hidden_ready"), sem("gelu_done"), sem("weighed")
            a_hi, a_lo = sem("a_hi_ready"), sem("a_lo_ready")
            f_ready, f_added = sem("f_ready"), sem("f_added")
            block = ctx.block()

            @block.sync
            def _(sp):
                def load_u(n):
                    sp.wait_ge(u_lo, ONE + n)
                    sp.dma_start(Ur[:, :, :], a["expert_uT"][ds(n, 1)].rearrange("o p k e -> p (o k) e")
                                 ).then_inc(u_in, 16)
                load_u(0)
                with sp.Fori(1, NK) as n:
                    load_u(n)

            @block.gpsimd
            def _(pool):
                def load_g(n):
                    pool.wait_ge(weighed, ONE + n)
                    pool.dma_start(G[:, :], g_dram[ds(n, 1)].rearrange("o j t -> j (o t)")).then_inc(g_in, 16)

                def load_v(n):
                    pool.wait_ge(v_lo, ONE + n)
                    pool.dma_start(Vr[:, :], a["expert_v"][ds(n * P, P), :]).then_inc(v_in, 16)

                nc.gpsimd.memset(accT[:, :, :], 0.0).then_inc(acc_set, 1)
                with pool.Fori(0, NG) as g:
                    load_g(GC * g)
                    load_v(GC * g)
                    load_g(GC * g + 1)
                    load_g(GC * g + 2)
                    load_v(GC * g + 1)
                    load_v(GC * g + 2)
                    load_g(GC * g + 3)
                    load_v(GC * g + 3)

            def over_groups(body):
                def run(eng):
                    body(eng, 0, True, False)
                    with eng.Fori(1, NG - 1) as g:
                        body(eng, g, False, False)
                    body(eng, NG - 1, False, True)
                return run

            def hidden(pe, g, c, first):
                n = GC * g + c
                pe.wait_ge(u_lo, ONE + n + 1)
                if not first or c >= 2:
                    pe.wait_ge(gelu, ONE + n - 1)
                if first and c == 0:
                    pe.wait_ge(f_added, ONE)
                s = c % 2
                for b, (lo, hi) in enumerate(BLOCKS):
                    for k in range(KD):
                        for i, (u, z) in enumerate(((Uh, zh), (Uh, zl), (Ul, zh))):
                            last = nc.tensor.matmul(ps[:, 3 * s + b, 0:TB], u[:, s, k, :], z[:, k, lo:hi],
                                                    start=(k == 0 and i == 0), stop=(k == KD - 1 and i == 2))
                last.then_inc(h_ready, 1)

            def values(pe, g):
                pe.wait_ge(a_lo, ONE + GC * g + GC)
                pe.wait_ge(v_lo, ONE + GC * g + GC)
                for m, (k, lo, hi) in enumerate(OUT):
                    pe.wait_ge(f_added, ONE + NB * g + max(m - 1, 0))
                    for c in range(GC):
                        for i, (v, x) in enumerate(((Vh, Ah), (Vh, Al), (Vl, Ah))):
                            last = nc.tensor.matmul(ps[:, 6 + m % 2, 0:TB], v[:, c, k * P:(k + 1) * P],
                                                    x[:, c, lo:hi],
                                                    start=(c == 0 and i == 0), stop=(c == GC - 1 and i == 2))
                    last.then_inc(f_ready, 1)

            @block.tensor
            def _(pe):
                def body(pe, g, first, last):
                    hidden(pe, g, 0, first)
                    hidden(pe, g, 1, first)
                    if not first:
                        values(pe, g - 1)
                    hidden(pe, g, 2, first)
                    hidden(pe, g, 3, first)
                over_groups(body)(pe)
                values(pe, NG - 1)

            @block.scalar
            def _(act):
                def split_u(n, s, first=False):
                    act.wait_ge(u_in, ONE + 16 * n + 16)
                    if not first:
                        act.wait_ge(h_ready, ONE + n - 1)
                    nc.scalar.activation(Uh[:, s, :, :], Ur[:, :, :], ACT.Copy).then_inc(u_hi, 1)

                def gelus(g, c, first):
                    n, s = GC * g + c, c % 2
                    act.wait_ge(h_ready, ONE + n + 1)
                    if not first or c >= 2:
                        act.wait_ge(a_lo, ONE + n - 1)
                    nc.scalar.activation(gl[:, s, :].rearrange("p (b n) -> p b n", b=3),
                                         ps[:, 3 * s:3 * s + 3, 0:TB], ACT.Gelu).then_inc(gelu, 1)

                def split_a(g, c):
                    n = GC * g + c
                    act.wait_ge(weighed, ONE + n + 1)
                    act.wait_ge(f_ready, ONE + NB * g)
                    nc.scalar.activation(Ah[:, c, :], gl[:, c % 2, :], ACT.Copy).then_inc(a_hi, 1)

                def split_v(g, c):
                    act.wait_ge(v_in, 16 * (GC * g + c) + 16)
                    act.wait_ge(f_ready, ONE + NB * g)
                    nc.scalar.activation(Vh[:, c, :], Vr[:, :], ACT.Copy).then_inc(v_hi, 1)

                def body(act, g, first, last):
                    split_u(GC * g + 2, 0)
                    gelus(g, 0, first)
                    split_u(GC * g + 3, 1)
                    gelus(g, 1, first)
                    split_a(g, 0)
                    split_a(g, 1)
                    split_v(g, 0)
                    split_v(g, 1)
                    gelus(g, 2, first)
                    if not last:
                        split_u(GC * g + 4, 0)
                    split_a(g, 2)
                    split_v(g, 2)
                    gelus(g, 3, first)
                    if not last:
                        split_u(GC * g + 5, 1)
                    split_a(g, 3)
                    split_v(g, 3)

                split_u(0, 0, True)
                split_u(1, 1, True)
                over_groups(body)(act)

            @block.vector
            def _(dve):
                def split_u(n, s):
                    dve.wait_ge(u_hi, ONE + n + 1)
                    nc.vector.tensor_tensor(Ul[:, s, :, :], Ur[:, :, :], Uh[:, s, :, :].bitcast(F32),
                                            ALU.subtract).then_inc(u_lo, 1)

                def weigh(g, c):
                    n, s = GC * g + c, c % 2
                    dve.wait_ge(gelu, ONE + n + 1)
                    dve.wait_ge(g_in, 16 * n + 16)
                    nc.vector.tensor_tensor(gl[:, s, SEQ:T], gl[:, s, SEQ:T],
                                            g_sample[:, ds(n, 1), :].rearrange("p o t -> p (o t)"), ALU.mult)
                    nc.vector.tensor_tensor(gl[:, s, 0:SEQ], gl[:, s, 0:SEQ], G[:, :], ALU.mult).then_inc(weighed, 1)

                def split_a(g, c):
                    dve.wait_ge(a_hi, ONE + GC * g + c + 1)
                    nc.vector.tensor_tensor(Al[:, c, :], gl[:, c % 2, :], Ah[:, c, :].bitcast(F32),
                                            ALU.subtract).then_inc(a_lo, 1)

                def split_v(g, c):
                    dve.wait_ge(v_hi, ONE + GC * g + c + 1)
                    nc.vector.tensor_tensor(Vl[:, c, :], Vr[:, :], Vh[:, c, :].bitcast(F32),
                                            ALU.subtract).then_inc(v_lo, 1)

                def add(g, start, end):
                    for m, (k, lo, hi) in list(enumerate(OUT))[start:end]:
                        dve.wait_ge(f_ready, ONE + NB * g + m + 1)
                        nc.vector.tensor_tensor(accT[:, k, lo:hi], accT[:, k, lo:hi], ps[:, 6 + m % 2, 0:TB],
                                                ALU.add).then_inc(f_added, 1)

                def body(dve, g, first, last):
                    split_u(GC * g + 2, 0)
                    weigh(g, 0)
                    split_u(GC * g + 3, 1)
                    if not first:
                        add(g - 1, 0, 2)
                    weigh(g, 1)
                    if not first:
                        add(g - 1, 2, NB)
                    split_a(g, 0)
                    split_a(g, 1)
                    split_v(g, 0)
                    split_v(g, 1)
                    weigh(g, 2)
                    if not last:
                        split_u(GC * g + 4, 0)
                    split_a(g, 2)
                    split_v(g, 2)
                    weigh(g, 3)
                    if not last:
                        split_u(GC * g + 5, 1)
                    split_a(g, 3)
                    split_v(g, 3)

                split_u(0, 0)
                split_u(1, 1)
                dve.wait_ge(acc_set, ONE + 1)
                over_groups(body)(dve)
                add(NG - 1, 0, NB)

        final_phase(nc, a, ps, ident, accT, h_dram)


def final_phase(nc, a, ps, ident, accT, h_dram):
    NTT = NT + 1
    with Scope(nc) as ctx:
        def sb(n, shape):
            return ctx.enter_context(nc.sbuf_tensor("fn_" + n, shape, F32))

        rows, gain, junk, st = sb("rows", [P, NTT, D]), sb("gain", [P, D]), sb("junk", [P, D]), sb("st", [P, 4, NTT])
        s_h, s_g, s_z, turned, added, sq, mean, root, inv, ready, out = (ctx.sem("fn_" + x) for x in (
            "h_loaded", "gain_loaded", "sums_set", "turned", "added", "squares", "mean", "root", "inverse",
            "rows_ready", "stored"))
        block = ctx.block()

        @block.sync
        def _(sp):
            sp.dma_start(rows[:, 0:NT, :], h_dram[0:SEQ, :].rearrange("(t p) d -> p t d", p=P)).then_inc(s_h, 16)
            sp.dma_start(rows[0:NS, NT, :], h_dram[SEQ:T, :]).then_inc(s_h, 16)
            sp.dma_start(gain[:, :], a["g_final"].partition_broadcast(P)).then_inc(s_g, 16)
            for t, lo, r in TILES:
                sp.wait_ge(ready, ONE + t + 1)
                sp.dma_start(a["o_y_p"][lo:lo + r, :] if t < NT else a["o_y_s"], rows[0:r, t, :]).then_inc(out, 16)
            sp.wait_ge(out, ONE + 16 * NTT)

        @block.tensor
        def _(pe):
            for t, lo, r in TILES:
                if t >= 4:
                    pe.wait_ge(added, ONE + t - 3)
                for k in range(KD):
                    last = nc.tensor.transpose(ps[0:r, 2 * (t % 4) + k // 4, (k % 4) * P:(k % 4 + 1) * P],
                                               accT[:, k, lo:lo + r], ident[:, :])
                last.then_inc(turned, 1)

        @block.scalar
        def _(act):
            act.wait_ge(s_z, ONE + 1)
            for t, lo, r in TILES:
                act.wait_ge(added, ONE + t + 1)
                if t:
                    act.wait_ge(sq, ONE + t)
                nc.scalar.activation(junk[0:r, :], rows[0:r, t, :], ACT.Square,
                                     accum_out=st[0:r, 0, t:t + 1]).then_inc(sq, 1)
            act.wait_ge(mean, ONE + 1)
            nc.scalar.activation(st[:, 2, :], st[:, 1, :], ACT.Sqrt).then_inc(root, 1)

        @block.vector
        def _(dve):
            nc.vector.memset(st[:, 0, :], 1.0).then_inc(s_z, 1)
            dve.wait_ge(s_h, ONE + 32)
            for t, lo, r in TILES:
                dve.wait_ge(turned, ONE + t + 1)
                nc.vector.tensor_tensor(rows[0:r, t, :].rearrange("p (b n) -> p b n", n=BANK),
                                        rows[0:r, t, :].rearrange("p (b n) -> p b n", n=BANK),
                                        ps[0:r, 2 * (t % 4):2 * (t % 4) + 2, :], ALU.add).then_inc(added, 1)
            dve.wait_ge(sq, ONE + NTT)
            nc.vector.tensor_scalar(st[:, 1, :], st[:, 0, :], 1.0 / D, EPS, ALU.mult, ALU.add).then_inc(mean, 1)
            dve.wait_ge(root, ONE + 1)
            nc.vector.reciprocal(st[:, 3, :], st[:, 2, :]).then_inc(inv, 1)
            dve.wait_ge(inv, ONE + 1)
            dve.wait_ge(s_g, ONE + 16)
            for t, lo, r in TILES:
                nc.vector.scalar_tensor_tensor(out=rows[0:r, t, :], in0=rows[0:r, t, :], scalar=st[0:r, 3, t:t + 1],
                                               in1=gain[0:r, :], op0=ALU.mult, op1=ALU.mult).then_inc(ready, 1)



def tables():
    f = np.float32
    pos = np.zeros((NT + 1, P), f)
    pos[0:NT] = np.arange(SEQ, dtype=f).reshape(NT, P)
    pos[NT] = PAST
    base = (f(1.0) / (f(10000.0) ** np.linspace(0.0, 1.0, RDK // 2, dtype=f))).astype(f)
    ang = (pos[:, :, None] * base).astype(f)
    inv = (f(500000.0) ** (-np.arange(0, ROT, 2, dtype=f) / f(ROT))).astype(f)
    ang_a = (pos[:, :, None] * inv).astype(f)
    decay = np.log(1.0 - 2.0 ** (-5.0 - np.arange(RH)))
    m, l = np.arange(P)[:, None], np.arange(P)[None, :]
    maskT = np.where((l >= m)[:, None, :], np.exp(decay[None, :, None] * np.maximum(l - m, 0)[:, None, :]), 0.0)
    qdec = np.broadcast_to(np.exp(decay[:, None] * (np.arange(P) + 1.0)), (P, RH, P))
    kdec = np.exp(decay[None, :] * (P - 1.0 - np.arange(P))[:, None]) * RDK ** -0.5
    q, k = np.arange(P)[:, None], np.arange(P)[None, :]
    row = np.arange(2 * AH * NS)
    sample, head, second = row // (2 * AH), (row // 2) % AH, row % 2
    sel = np.concatenate([(second == 0)[:, None], (second == 1)[:, None],
                          sample[:, None] == np.arange(NS), head[:, None] == np.arange(AH)], axis=1)
    return {
        "ident": np.eye(P), "ret_cos": np.cos(ang), "ret_sin": np.sin(ang), "att_cos": np.cos(ang_a),
        "att_sin": np.sin(ang_a), "ret_maskT": maskT, "ret_qdec": qdec, "ret_kdec": kdec,
        "att_mask": np.where(k <= q, 0.0, NEG), "sel": sel,
    }


OUTS = {
    "o_y_p": (SEQ, D), "o_y_s": (NS, D), "o_ret_p": (RH, RDK, RDV), "o_k_p": (SEQ, AH * 2 * ADQ),
    "o_v_p": (SEQ, AH * ADV), "o_ret_s": (NS, RH, RDK, RDV), "o_k_s": (NS, AH * 2 * ADQ), "o_v_s": (NS, AH * ADV),
}


def lay_out(i):
    c = np.ascontiguousarray
    w_in = np.asarray(i["w_in"])[0]
    cols = np.cumsum([0, 512, 512, 1024, 512, 512, 512, D, D])
    rows = lambda w: w.reshape(-1, P, w.shape[1]).transpose(1, 0, 2)
    blocks = lambda w: w.reshape(-1, P, w.shape[1] // P, P).transpose(2, 1, 0, 3)
    U = np.asarray(i["expert_u"])[0]
    gates = blocks(w_in[:, cols[6]:cols[7]]), blocks(w_in[:, cols[7]:cols[8]])
    return {
        "x": c(np.concatenate([np.asarray(i["x_prompt"])[0], np.asarray(i["x_sample"])[:, 0]])),
        "state": c(np.asarray(i["state_ret"])[0]),
        "cache_kT": c(np.asarray(i["cache_k"])[0].transpose(0, 2, 3, 1)),
        "cache_v": c(np.asarray(i["cache_v"])[0].reshape(POOL, PAGE, AH * ADV)),
        "page_table": c(np.asarray(i["page_table"]).reshape(1, NS * NPAGE)),
        "g_mix": c(np.asarray(i["g_mix"]).reshape(KD, P).T), "g_ffn": c(np.asarray(i["g_ffn"]).reshape(KD, P).T),
        "g_subln": c(np.asarray(i["g_subln"]).reshape(ADV, 1)), "g_final": c(np.asarray(i["g_final"])),
        "lams": c(np.concatenate([np.asarray(i[n]) for n in ("lam_q1", "lam_k1", "lam_q2", "lam_k2")])),
        "w_ret": c(rows(w_in[:, 0:cols[3]])), "w_att": c(rows(w_in[:, cols[3]:cols[6]])),
        "w_merge": c(np.concatenate([*gates, blocks(np.asarray(i["w_br_ret"])[0]),
                                     blocks(np.asarray(i["w_br_att"])[0])], axis=2)),
        "w_out": c(rows(np.asarray(i["w_out"])[0])),
        "w_query": c(blocks(np.asarray(i["w_query"])[0])),
        "sub_keysT": c(np.asarray(i["sub_keys"])[0].reshape(2 * PH, NK, P).transpose(2, 0, 1)),
        "expert_uT": c(U.reshape(NK, P, KD, P).transpose(0, 3, 2, 1)),
        "expert_v": c(np.asarray(i["expert_v"])[0]),
        **{n: c(t.astype(np.float32)) for n, t in tables().items()},
    }


def kernel(**inputs):
    import concourse.bacc as bacc
    from concourse.bass_utils import run_bass_kernel_spmd

    nc = bacc.Bacc("TRN2", target_bir_lowering=False, num_devices=1)
    arrays = lay_out(inputs)
    aps = {n: nc.dram_tensor("in_" + n, x.shape, mybir.dt.from_np(x.dtype), kind="ExternalInput").ap()
           for n, x in arrays.items()}
    for n, shape in OUTS.items():
        aps[n] = nc.dram_tensor(n, shape, F32, kind="ExternalOutput").ap()
    build(nc, aps)
    r = run_bass_kernel_spmd(nc, [{"in_" + n: x for n, x in arrays.items()}], core_ids=[0]).results[0]
    return (r["o_y_p"].reshape(1, SEQ, D), r["o_y_s"].reshape(NS, 1, D),
            r["o_ret_p"].reshape(1, 1, RH, RDK, RDV), r["o_k_p"].reshape(1, 1, SEQ, AH, 2 * ADQ),
            r["o_v_p"].reshape(1, 1, SEQ, AH, ADV), r["o_ret_s"].reshape(1, NS, RH, RDK, RDV),
            r["o_k_s"].reshape(1, NS, 1, AH, 2 * ADQ), r["o_v_s"].reshape(1, NS, 1, AH, ADV))
```

```python
from contextlib import ExitStack

import numpy as np
import concourse.bass as bass
from concourse import mybir
from concourse.alu_op_type import AluOpType as ALU

F32 = mybir.dt.float32
F32R = mybir.dt.float32r
U32 = mybir.dt.uint32
I32 = mybir.dt.int32
ACT = mybir.ActivationFunctionType
AX_X = mybir.AxisListType.X
ds = bass.ds

P = 128
D = 1024
KD = D // P
SEQ = 1024
NS = 8
T = SEQ + NS
NT = SEQ // P
TB = T // 3
BLOCKS = [(b * TB, (b + 1) * TB) for b in range(3)]
BANK = 512
RH, RDK, RDV = 4, 128, 256
AH, ADQ, ADV = 4, 64, 128
ROT = ADQ // 4
PAST, PAGE = 512, 128
NPAGE = PAST // PAGE
POOL = 40
PH, NK, TOPK = 8, 128, 16
WR = 2 * RH * RDK + RH * RDV
WA = 2 * AH * 2 * ADQ + AH * ADV
EPS, SUB_EPS = 1e-6, 1e-5
LAM_INIT = 0.8 - 0.6
NEG = -1e30
ONE = 1
GC = 4
TILES = [(t, t * P, P) for t in range(NT)] + [(NT, SEQ, NS)]


class Chain:

    def __init__(self, eng, sem, base=0):
        self.eng, self.sem, self.base, self.n = eng, sem, base, 0

    def __call__(self, ins):
        ins.then_inc(self.sem, 1)
        self.n += 1
        self.eng.wait_ge(self.sem, ONE + self.base + self.n)


class Scope(ExitStack):

    def __init__(self, nc):
        super().__init__()
        self.nc, self.sems, self.queued = nc, [], []

    def sem(self, name):
        self.sems.append(self.enter_context(self.nc.semaphore(name)))
        return self.sems[-1]

    def queue_sem(self, name):
        self.queued.append(self.enter_context(self.nc.semaphore(name)))
        return self.queued[-1]

    def zero(self):
        for s in self.sems + self.queued:
            self.nc.gpsimd.sem_clear(s)
        self.nc.all_engine_barrier()

    def block(self):
        for s in self.sems:
            self.nc.gpsimd.sem_inc(s, ONE)
        self.nc.all_engine_barrier()
        self.callback(self.zero)
        return self.enter_context(self.nc.Block())


def build(nc, a, stop=99):
    top = ExitStack()
    with top:
        def sb(name, shape, dt=F32, ctx=top):
            return ctx.enter_context(nc.sbuf_tensor(name, shape, dt))

        def sem(name, ctx=top):
            return ctx.enter_context(nc.semaphore(name))

        h_dram = nc.dram_tensor("h_scratch", [T, D], F32, kind="Internal").ap()
        g_dram = nc.dram_tensor("gate_scratch", [NK, P, SEQ], F32, kind="Internal").ap()

        ps = top.enter_context(nc.psum_tensor("ps", [P, 8, BANK], F32))
        ident = sb("ident", [P, P])
        lam = sb("lam", [P, 1])

        g_sample = sb("g_sample", [P, NK, NS])
        left = ExitStack()
        zT = sb("zT", [P, KD, T], ctx=left)
        with ExitStack() as mid:
            rT = sb("rT", [P, KD, T], ctx=mid)
            aT = sb("aT", [P, AH, T], ctx=mid)
            with ExitStack() as branches:
                s_rqk = sb("s_rqk", [NS, 2 * RH * RDK], ctx=branches)
                s_rv = sb("s_rv", [NS, RH * RDV], ctx=branches)
                s_aqk = sb("s_aqk", [NS, 2 * AH * 2 * ADQ], ctx=branches)
                s_av = sb("s_av", [NS, AH * ADV], ctx=branches)
                with Scope(nc) as ret:
                    w_ret = sb("w_ret", [P, KD, WR], ctx=ret)
                    w_ret_in = [ret.queue_sem(f"w_ret_loaded{b}") for b in range(WR // BANK)]
                    ret.callback(ret.zero)
                    norm_phase(nc, a, ps, ident, zT, lam, w_ret, w_ret_in)
                    retention_phase(nc, a, ps, ident, zT, rT, s_rqk, s_rv, w_ret, w_ret_in)
                with ExitStack() as att:
                    QT = sb("QT", [P, AH, SEQ], ctx=att)
                    KT = sb("KT", [P, AH, SEQ], ctx=att)
                    VA = sb("VA", [P, NT, AH * ADV], ctx=att)
                    if stop >= 3:
                        attention_projection(nc, a, ps, ident, zT, QT, KT, VA, s_aqk, s_av)
                    if stop >= 4:
                        attention_phase(nc, a, ps, ident, QT, KT, VA, aT, lam)
                if stop >= 5:
                    sample_phase(nc, a, ps, ident, s_rqk, s_rv, s_aqk, s_av, rT, aT, lam)
            if stop >= 6:
                mT = sb("mT", [P, KD, T], ctx=mid)
                w_out = sb("w_out", [P, KD, D], ctx=mid)
                merge_phase(nc, a, ps, zT, rT, aT, mT, w_out)
                residual_phase(nc, a, ps, ident, mT, w_out, h_dram, zT)
        z2T = zT
        if stop >= 7:
            with ExitStack() as route:
                gT = sb("gT", [P, T], ctx=route)
                iT = sb("iT", [P, T], ctx=route)
                jT = sb("jT", [P, T], ctx=route)
                routing_phase(nc, a, ps, ident, z2T, gT, iT, jT)
                gate_phase(nc, a, ps, gT, iT, jT, g_dram, g_sample)
            expert_phase(nc, a, ps, ident, z2T, g_dram, g_sample, h_dram, top, left)


def norm_rows(nc, name, ctx, ps, ident, zT, src, gain_cols, const_ready, consts, extra, after):
    def sb(n, shape):
        return ctx.enter_context(nc.sbuf_tensor(f"{name}_{n}", shape, F32))

    def sem(n):
        return ctx.sem(f"{name}_{n}")

    x = sb("x", [P, 2, D])
    z = sb("z", [P, 2, D])
    junk = sb("junk", [P, D])
    st = sb("st", [P, 2, 4])
    loaded = [sem(f"rows_loaded{u}") for u in range(2)]
    squared = [sem(f"squares_summed{u}") for u in range(2)]
    mean = [sem(f"mean_ready{u}") for u in range(2)]
    root = [sem(f"root_ready{u}") for u in range(2)]
    inverse = [sem(f"inverse_ready{u}") for u in range(2)]
    scaled = [sem(f"rows_scaled{u}") for u in range(2)]
    turned = [sem(f"rows_turned{u}") for u in range(2)]
    kept = [sem(f"columns_kept{u}") for u in range(2)]

    def over_tiles(eng, step):
        with eng.Fori(0, NT // 2) as it:
            for u in range(2):
                step(it, u, P)
        step(NT // 2, 0, NS)

    block = ctx.block()
    extra(block)

    @block.sync
    def _(sp):
        consts(sp)

        def step(it, u, rows):
            sp.wait_ge(scaled[u], ONE + it)
            row = (2 * it + u) * P
            sp.dma_start(x[0:rows, u, :], src[ds(row, rows), :]).then_inc(loaded[u], 16)
        over_tiles(sp, step)
        after(sp)

    @block.scalar
    def _(act):
        def step(it, u, rows):
            act.wait_ge(loaded[u], ONE + 16 * it + 16)
            nc.scalar.activation(junk[0:rows, :], x[0:rows, u, :], ACT.Square,
                                 accum_out=st[0:rows, u, 0:1]).then_inc(squared[u], 1)
            act.wait_ge(mean[u], ONE + it + 1)
            nc.scalar.activation(st[0:rows, u, 2:3], st[0:rows, u, 1:2], ACT.Sqrt).then_inc(root[u], 1)
        over_tiles(act, step)

    @block.vector
    def _(dve):
        def step(it, u, rows):
            dve.wait_ge(squared[u], ONE + it + 1)
            nc.vector.tensor_scalar(st[0:rows, u, 1:2], st[0:rows, u, 0:1], 1.0 / D, EPS,
                                    ALU.mult, ALU.add).then_inc(mean[u], 1)
            dve.wait_ge(root[u], ONE + it + 1)
            nc.vector.reciprocal(st[0:rows, u, 3:4], st[0:rows, u, 2:3]).then_inc(inverse[u], 1)
            dve.wait_ge(inverse[u], ONE + it + 1)
            dve.wait_ge(turned[u], ONE + it)
            nc.vector.tensor_scalar(z[0:rows, u, :], x[0:rows, u, :], st[0:rows, u, 3:4], None,
                                    ALU.mult).then_inc(scaled[u], 1)
            dve.wait_ge(turned[u], ONE + it + 1)
            col = (2 * it + u) * P
            nc.vector.tensor_tensor(
                zT[:, :, ds(col, rows)],
                ps[:, 2 * u:2 * u + 2, :].rearrange("p b (c r) -> p (b c) r", r=P)[:, :, 0:rows],
                gain_cols[:, :].unsqueeze(2).to_broadcast([P, KD, rows]), ALU.mult).then_inc(kept[u], 1)
        over_tiles(dve, step)

    @block.tensor
    def _(pe):
        pe.wait_ge(const_ready[0], ONE + const_ready[1])

        def step(it, u, rows):
            pe.wait_ge(scaled[u], ONE + it + 1)
            pe.wait_ge(kept[u], ONE + it)
            for c in range(KD):
                last = nc.tensor.transpose(ps[:, 2 * u + c // 4, (c % 4) * P:(c % 4) * P + rows],
                                           z[0:rows, u, c * P:(c + 1) * P], ident[0:rows, 0:rows])
            last.then_inc(turned[u], 1)
        over_tiles(pe, step)


def norm_phase(nc, a, ps, ident, zT, lam, w_ret, w_ret_in):
    with Scope(nc) as ctx:
        gain = ctx.enter_context(nc.sbuf_tensor("gain_mix", [P, KD], F32))
        lv = ctx.enter_context(nc.sbuf_tensor("lam_vectors", [P, 4, ADQ], F32))
        lp = ctx.enter_context(nc.sbuf_tensor("lam_products", [P, 2, ADQ], F32))
        le = ctx.enter_context(nc.sbuf_tensor("lam_parts", [P, 4], F32))
        s_const = ctx.sem("consts_loaded")
        s_step = ctx.sem("lam_step")
        s_sum = ctx.sem("lam_sums")
        s_exp = ctx.sem("lam_exps")
        n = 16 * 3
        def consts(sp):
            sp.dma_start(ident[:, :], a["ident"]).then_inc(s_const, 16)
            sp.dma_start(gain[:, :], a["g_mix"]).then_inc(s_const, 16)
            sp.dma_start(lv[:, :, :], a["lams"].partition_broadcast(P)).then_inc(s_const, 16)

        def find_lambda(block):
            @block.vector
            def _(dve):
                link = Chain(dve, s_step)
                dve.wait_ge(s_const, ONE + n)
                link(nc.vector.tensor_tensor(lp[:, :, :], lv[:, 0:4:2, :], lv[:, 1:4:2, :], ALU.mult))
                nc.vector.tensor_reduce(le[:, 0:2], lp[:, :, :], AX_X, ALU.add).then_inc(s_sum, 1)

            @block.scalar
            def _(act):
                act.wait_ge(s_sum, ONE + 1)
                nc.scalar.activation(le[:, 2:4], le[:, 0:2], ACT.Exp).then_inc(s_exp, 1)

            @block.gpsimd
            def _(pool):
                pool.wait_ge(s_exp, ONE + 1)
                nc.gpsimd.tensor_tensor(le[:, 0:1], le[:, 2:3], le[:, 3:4], ALU.subtract).then_inc(s_exp, 1)
                pool.wait_ge(s_exp, ONE + 2)
                nc.gpsimd.tensor_scalar(lam[:, :], le[:, 0:1], LAM_INIT, None, ALU.add).then_inc(s_exp, 1)

        def load_w_ret(sp):
            for b in range(WR // BANK):
                cols = slice(b * BANK, (b + 1) * BANK)
                sp.dma_start(w_ret[:, :, cols], a["w_ret"][:, :, cols]).then_inc(w_ret_in[b], 16)

        norm_rows(nc, "mix", ctx, ps, ident, zT, a["x"], gain, (s_const, n), consts, find_lambda, load_w_ret)


def retention_phase(nc, a, ps, ident, zT, rT, s_rqk, s_rv, W, w_in):
    with Scope(nc) as ctx:
        def sb(n, shape, dt=F32):
            return ctx.enter_context(nc.sbuf_tensor("ret_" + n, shape, dt))

        def sem(n):
            return ctx.sem("ret_" + n)

        zc = sb("z_tile", [P, KD, P])
        cosr, sinr = sb("cos", [P, NT + 1, 64]), sb("sin", [P, NT + 1, 64])
        maskT = sb("maskT", [P, RH, P])
        qdec = sb("q_decay", [P, RH, P])
        kdec = sb("k_decay", [P, RH])
        rot = sb("rotated", [P, 2 * RH, 64, 2])
        t1, t2 = sb("t1", [P, 2 * RH, 64]), sb("t2", [P, 2 * RH, 64])
        kd = sb("k_decayed", [P, RH, P])
        v = sb("v", [P, RH * RDV])
        qT, qdT, kT, sT = (sb(n, [P, RH, P]) for n in ("qT", "qdT", "kT", "sT"))
        state = sb("state", [P, RH, RDV])
        rn = sb("normed", [P, RH, RDV])
        junk = sb("junk", [P, RDV])
        st = sb("st", [P, 4, RH])

        s_tab = sem("tables_loaded")
        state_zero, inv, sq_step = sem("state_zero"), sem("inverse"), sem("square_step")
        z_ready, qk_ready, v_ready = sem("z_tile_ready"), sem("qk_projected"), sem("v_projected")
        v_kept = sem("v_kept")
        chain, rotated, k_dec_ready = sem("chain"), sem("rotated_ready"), sem("kd_ready")
        qk_turned, qk_kept = sem("qk_turned"), sem("qk_kept")
        s_ready, s_kept = sem("scores_ready"), sem("scores_kept")
        out_ready, state_ready, state_kept = sem("out_ready"), sem("state_update_ready"), sem("state_kept")
        squares, mean, root, normed = sem("squares"), sem("mean"), sem("root"), sem("normed_ready")
        turned, kept, stored = sem("out_turned"), sem("out_kept"), sem("stored")
        ACT_V, PROJ = 3, WR // BANK
        SCALE = float(RDK) ** -0.5
        log_decay = np.log(1.0 - 2.0 ** (-5.0 - np.arange(RH)))
        g_chunk = [float(np.exp(x * P)) for x in log_decay]
        NLINK = 5

        block = ctx.block()

        @block.sync
        def _(sp):
            for d_, s_ in ((cosr, "ret_cos"), (sinr, "ret_sin")):
                sp.dma_start(d_[:, :, :], a[s_].rearrange("t p f -> p t f")).then_inc(s_tab, 16)
            for d_, s_ in ((maskT, "ret_maskT"), (qdec, "ret_qdec")):
                sp.dma_start(d_[:, :, :], a[s_]).then_inc(s_tab, 16)
            sp.dma_start(kdec[:, :], a["ret_kdec"]).then_inc(s_tab, 16)
            sp.wait_ge(state_kept, ONE + NT)
            sp.dma_start(a["o_ret_p"].rearrange("h k v -> k h v"), state[:, :, :]).then_inc(stored, 16)
            sp.wait_ge(stored, ONE + 16)

        @block.gpsimd
        def _(pool):
            def copy_tile(t):
                pool.wait_ge(v_ready, ONE + t)
                nc.gpsimd.tensor_copy(zc[:, :, :], zT[:, :, ds(t * P, P)]).then_inc(z_ready, 1)
            nc.gpsimd.memset(state[:, :, :], 0.0).then_inc(state_zero, 1)
            with pool.Fori(0, NT) as t:
                copy_tile(t)

        @block.tensor
        def _(pe):
            def project(t, rows, lhs, banks):
                pe.wait_ge(rotated, ONE + t)
                for b in banks:
                    if b == 2:
                        pe.wait_ge(v_kept, ONE + t)
                    pe.wait_ge(w_in[b], 16)
                    for c in range(KD):
                        last = nc.tensor.matmul(ps[0:rows, b, :], lhs(c), W[:, c, b * BANK:(b + 1) * BANK],
                                                start=(c == 0), stop=(c == KD - 1))
                    if b == 1:
                        last.then_inc(qk_ready, 1)
                    if b == PROJ - 1:
                        last.then_inc(v_ready, 1)

            def tile_project(t, banks):
                pe.wait_ge(z_ready, ONE + t + 1)
                project(t, P, lambda c: zc[:, c, :], banks)

            def chunk(t, following=None):
                pe.wait_ge(rotated, ONE + t + 1)
                pe.wait_ge(normed, ONE + t)
                for i in range(2 * RH):
                    last = nc.tensor.transpose(ps[:, 4 + i // RH, (i % RH) * P:(i % RH + 1) * P],
                                               rot[:, i, :, :].rearrange("p f two -> p (f two)"), ident[:, :])
                last.then_inc(qk_turned, 1)
                if following:
                    following([0])
                pe.wait_ge(qk_kept, ONE + t + 1)
                pe.wait_ge(kept, ONE + t)
                for h in range(RH):
                    last = nc.tensor.matmul(ps[:, 6, h * P:(h + 1) * P], kT[:, h, :], qT[:, h, :],
                                            start=True, stop=True)
                last.then_inc(s_ready, 1)
                if following:
                    following([1])
                pe.wait_ge(s_kept, ONE + t + 1)
                pe.wait_ge(v_kept, ONE + t + 1)
                pe.wait_ge(state_kept, ONE + t)
                for h in range(RH):
                    o = ps[:, 4 + h // 2, (h % 2) * RDV:(h % 2 + 1) * RDV]
                    vh = v[:, h * RDV:(h + 1) * RDV]
                    nc.tensor.matmul(o, sT[:, h, :], vh, start=True, stop=False)
                    last = nc.tensor.matmul(o, qdT[:, h, :], state[:, h, :], start=False, stop=True)
                last.then_inc(out_ready, 1)
                pe.wait_ge(k_dec_ready, ONE + t + 1)
                for h in range(RH):
                    last = nc.tensor.matmul(ps[:, 6 + h // 2, (h % 2) * RDV:(h % 2 + 1) * RDV], kd[:, h, :],
                                            v[:, h * RDV:(h + 1) * RDV], start=True, stop=True)
                last.then_inc(state_ready, 1)

            def turn_out(t):
                pe.wait_ge(normed, ONE + t + 1)
                pe.wait_ge(state_kept, ONE + t + 1)
                for c in range(KD):
                    last = nc.tensor.transpose(ps[:, 6 + c // 4, (c % 4) * P:(c % 4 + 1) * P],
                                               rn[:, :, :].rearrange("p h e -> p (h e)")[:, c * P:(c + 1) * P],
                                               ident[:, :])
                last.then_inc(turned, 1)

            pe.wait_ge(state_zero, ONE + 1)
            tile_project(0, range(PROJ))
            with pe.Fori(0, NT - 1) as t:
                chunk(t, lambda banks: tile_project(t + 1, banks))
                tile_project(t + 1, range(2, PROJ))
                turn_out(t)
            chunk(NT - 1)
            project(NT, NS, lambda c: zT[:, c, SEQ:T], range(PROJ))
            turn_out(NT - 1)

        @block.vector
        def _(dve):
            def rotate(t, rows, out, base):
                dve.wait_ge(qk_ready, ONE + t + 1)
                dve.wait_ge(state_ready, ONE + t)
                x = ps[0:rows, 0:2, :].rearrange("p b (h f two) -> p (b h) f two", h=RH, two=2)
                cb = cosr[0:rows, ds(t, 1), :].to_broadcast([rows, 2 * RH, 64])
                sb_ = sinr[0:rows, ds(t, 1), :].to_broadcast([rows, 2 * RH, 64])
                link = Chain(dve, chain, base)
                u1, u2 = t1[0:rows], t2[0:rows]
                link(nc.vector.tensor_tensor(u1, x[:, :, :, 0], cb, ALU.mult))
                link(nc.vector.tensor_tensor(u2, x[:, :, :, 1], sb_, ALU.mult))
                link(nc.vector.tensor_tensor(out[:, :, :, 0], u1, u2, ALU.subtract))
                link(nc.vector.tensor_tensor(u1, x[:, :, :, 1], cb, ALU.mult))
                link(nc.vector.tensor_tensor(u2, x[:, :, :, 0], sb_, ALU.mult))
                nc.vector.tensor_tensor(out[:, :, :, 1], u1, u2, ALU.add).then_inc(rotated, 1)

            def tile_rotate(t):
                rotate(t, P, rot[:, :, :, :], t * NLINK)
                dve.wait_ge(rotated, ONE + t + 1)
                nc.vector.tensor_tensor(kd[:, :, :], rot[:, RH:, :, :].rearrange("p h f two -> p h (f two)"),
                                        kdec[:, :].unsqueeze(2).to_broadcast([P, RH, P]),
                                        ALU.mult).then_inc(k_dec_ready, 1)

            def chunk(t):
                dve.wait_ge(qk_turned, ONE + t + 1)
                q_ps = ps[:, 4, :].rearrange("p (h l) -> p h l", h=RH)
                nc.vector.tensor_copy(qT[:, :, :], q_ps)
                nc.vector.tensor_tensor(qdT[:, :, :], q_ps, qdec[:, :, :], ALU.mult)
                nc.vector.tensor_scalar(kT[:, :, :], ps[:, 5, :].rearrange("p (h l) -> p h l", h=RH), SCALE,
                                        None, ALU.mult).then_inc(qk_kept, 1)
                dve.wait_ge(s_ready, ONE + t + 1)
                nc.vector.tensor_tensor(sT[:, :, :], ps[:, 6, :].rearrange("p (h l) -> p h l", h=RH),
                                        maskT[:, :, :], ALU.mult).then_inc(s_kept, 1)
                dve.wait_ge(squares, ONE + t + 1)
                nc.vector.tensor_scalar(st[:, 1, :], st[:, 0, :], 1.0 / RDV, EPS, ALU.mult,
                                        ALU.add).then_inc(mean, 1)
                dve.wait_ge(root, ONE + t + 1)
                nc.vector.reciprocal(st[:, 3, :], st[:, 2, :]).then_inc(inv, 1)
                dve.wait_ge(state_ready, ONE + t + 1)
                for h in range(RH):
                    last = nc.vector.scalar_tensor_tensor(
                        out=state[:, h, :], in0=state[:, h, :], scalar=g_chunk[h],
                        in1=ps[:, 6 + h // 2, (h % 2) * RDV:(h % 2 + 1) * RDV], op0=ALU.mult, op1=ALU.add)
                last.then_inc(state_kept, 1)
                dve.wait_ge(inv, ONE + t + 1)
                dve.wait_ge(turned, ONE + t)
                nc.vector.tensor_tensor(rn[:, :, :], ps[:, 4:6, :].rearrange("p b (h e) -> p (b h) e", h=2),
                                        st[:, 3, :].unsqueeze(2).to_broadcast([P, RH, RDV]),
                                        ALU.mult).then_inc(normed, 1)

            dve.wait_ge(s_tab, ONE + 16 * 5)
            tile_rotate(0)
            with dve.Fori(0, NT - 1) as t:
                chunk(t)
                tile_rotate(t + 1)
            chunk(NT - 1)
            rotate(NT, NS, s_rqk[:, :].rearrange("p (h f two) -> p h f two", f=64, two=2), NT * NLINK)

        @block.scalar
        def _(act):
            def keep_v(t, rows, out):
                act.wait_ge(v_ready, ONE + t + 1)
                nc.scalar.activation(out, ps[0:rows, 2:4, :].rearrange("p b n -> p (b n)"),
                                     ACT.Copy).then_inc(v_kept, 1)

            def chunk(t):
                act.wait_ge(out_ready, ONE + t + 1)
                for h in range(RH):
                    if h:
                        act.wait_ge(sq_step, ONE + (RH - 1) * t + h)
                    ins = nc.scalar.activation(junk[:, :], ps[:, 4 + h // 2, (h % 2) * RDV:(h % 2 + 1) * RDV],
                                               ACT.Square, accum_out=st[:, 0, h:h + 1])
                    ins.then_inc(sq_step if h < RH - 1 else squares, 1)
                act.wait_ge(mean, ONE + t + 1)
                nc.scalar.activation(st[:, 2, :], st[:, 1, :], ACT.Sqrt).then_inc(root, 1)

            def keep_out(t):
                act.wait_ge(turned, ONE + t + 1)
                nc.scalar.activation(rT[:, :, ds(t * P, P)],
                                     ps[:, 6:8, :].rearrange("p b (c r) -> p (b c) r", r=P),
                                     ACT.Copy).then_inc(kept, 1)

            keep_v(0, P, v[:, :])
            with act.Fori(0, NT - 1) as t:
                chunk(t)
                act.wait_ge(state_ready, ONE + t + 1)
                keep_v(t + 1, P, v[:, :])
                keep_out(t)
            chunk(NT - 1)
            keep_v(NT, NS, s_rv[:, :])
            keep_out(NT - 1)


def attention_projection(nc, a, ps, ident, zT, QT, KT, VA, s_aqk, s_av):
    with Scope(nc) as ctx:
        def sb(n, shape, dt=F32):
            return ctx.enter_context(nc.sbuf_tensor("ap_" + n, shape, dt))

        def sem(n):
            return ctx.sem("ap_" + n)

        W = sb("w", [P, KD, WA])
        zc = sb("z_tile", [P, KD, P])
        cosa, sina = sb("cos", [P, NT + 1, 8]), sb("sin", [P, NT + 1, 8])
        NG = 4 * AH
        qk = sb("qk", [P, NG, ADQ])
        prod = sb("products", [P, 4, NG, 8])
        s_w, s_tab, z_ready = [sem(f"w_loaded{b}") for b in range(3)], sem("tables_loaded"), sem("z_tile_ready")
        projected, copied, rotated = sem("projected"), sem("straight_part_kept"), sem("rotated")
        prods, v_kept, turned, kept = sem("products"), sem("v_kept"), sem("qk_turned"), sem("qk_kept")
        k_stored, v_stored = sem("k_rows_stored"), sem("v_rows_stored")

        block = ctx.block()

        @block.sync
        def _(sp):
            for b in range(3):
                cols = slice(b * BANK, (b + 1) * BANK)
                sp.dma_start(W[:, :, cols], a["w_att"][:, :, cols]).then_inc(s_w[b], 16)
            for d_, s_ in ((cosa, "att_cos"), (sina, "att_sin")):
                sp.dma_start(d_[:, :, :], a[s_].rearrange("t p f -> p t f")).then_inc(s_tab, 16)
            with sp.Fori(0, NT) as t:
                sp.wait_ge(rotated, ONE + t + 1)
                sp.dma_start(a["o_k_p"][ds(t * P, P), :], qk[:, NG // 2:, :]).then_inc(k_stored, 16)
                sp.wait_ge(v_kept, ONE + t + 1)
                sp.dma_start(a["o_v_p"][ds(t * P, P), :], VA[:, ds(t, 1), :].rearrange("p o n -> p (o n)")
                             ).then_inc(v_stored, 16)
            sp.wait_ge(rotated, ONE + NT + 1)
            sp.dma_start(a["o_k_s"], s_aqk[:, 512:1024]).then_inc(k_stored, 16)
            sp.wait_ge(v_kept, ONE + NT + 1)
            sp.dma_start(a["o_v_s"], s_av[:, :]).then_inc(v_stored, 16)
            sp.wait_ge(k_stored, ONE + 16 * (NT + 1))
            sp.wait_ge(v_stored, ONE + 16 * (NT + 1))

        @block.tensor
        def _(pe):
            def project(t, u, rows, lhs, first=False):
                if not first:
                    pe.wait_ge(rotated, ONE + t - 1)
                    pe.wait_ge(v_kept, ONE + t - 1)
                for b in range(3):
                    pe.wait_ge(s_w[b], ONE + 16)
                    for c in range(KD):
                        last = nc.tensor.matmul(ps[0:rows, 3 * u + b, :], lhs(c), W[:, c, b * BANK:(b + 1) * BANK],
                                                start=(c == 0), stop=(c == KD - 1))
                last.then_inc(projected, 1)

            def tile(t, u, first=False):
                pe.wait_ge(z_ready, ONE + t + 1)
                project(t, u, P, lambda c: zc[:, c, :], first)

            def turn(t):
                pe.wait_ge(rotated, ONE + t + 1)
                pe.wait_ge(kept, ONE + t)
                for i in range(2 * AH):
                    last = nc.tensor.transpose(ps[:, 6 + i // AH, (i % AH) * P:(i % AH + 1) * P],
                                               qk[:, 2 * i:2 * i + 2, :].rearrange("p c d -> p (c d)"), ident[:, :])
                last.then_inc(turned, 1)

            tile(0, 0, True)
            tile(1, 1, True)
            turn(0)
            with pe.Fori(1, NT // 2) as it:
                tile(2 * it, 0)
                turn(2 * it - 1)
                tile(2 * it + 1, 1)
                turn(2 * it)
            project(NT, 0, NS, lambda c: zT[:, c, SEQ:T])
            turn(NT - 1)

        @block.vector
        def _(dve):
            def rotate(t, rows, out, x):
                dve.wait_ge(projected, ONE + t + 1)
                dve.wait_ge(copied, ONE + t + 1)
                cb = cosa[0:rows, ds(t, 1), :].to_broadcast([rows, NG, 8])
                sb_ = sina[0:rows, ds(t, 1), :].to_broadcast([rows, NG, 8])
                x1, x2 = x[:, :, 0:8], x[:, :, 8:16]
                w = prod[0:rows]
                nc.vector.tensor_tensor(w[:, 0], x1, cb, ALU.mult)
                nc.vector.tensor_tensor(w[:, 1], x2, sb_, ALU.mult)
                nc.vector.tensor_tensor(w[:, 2], x2, cb, ALU.mult)
                nc.vector.tensor_tensor(w[:, 3], x1, sb_, ALU.mult).then_inc(prods, 1)
                dve.wait_ge(prods, ONE + t + 1)
                nc.vector.tensor_tensor(out[:, :, 0:8], w[:, 0], w[:, 1], ALU.subtract)
                nc.vector.tensor_tensor(out[:, :, 8:16], w[:, 2], w[:, 3], ALU.add).then_inc(rotated, 1)

            dve.wait_ge(s_tab, ONE + 32)
            with dve.Fori(0, NT // 2) as it:
                for u in range(2):
                    t = 2 * it + u
                    rotate(t, P, qk[:, :, :], ps[:, 3 * u:3 * u + 2, :].rearrange("p b (g d) -> p (b g) d", d=ADQ))
                    dve.wait_ge(turned, ONE + t + 1)
                    nc.vector.tensor_copy(QT[:, :, ds(t * P, P)], ps[:, 6, :].rearrange("p (h l) -> p h l", h=AH))
                    nc.vector.tensor_copy(KT[:, :, ds(t * P, P)],
                                          ps[:, 7, :].rearrange("p (h l) -> p h l", h=AH)).then_inc(kept, 1)
            rotate(NT, NS, s_aqk[:, :].rearrange("p (g d) -> p g d", d=ADQ),
                   ps[0:NS, 0:2, :].rearrange("p b (g d) -> p (b g) d", d=ADQ))

        @block.scalar
        def _(act):
            def copy_tile(t):
                act.wait_ge(projected, ONE + t)
                nc.scalar.activation(zc[:, :, :], zT[:, :, ds(t * P, P)], ACT.Copy).then_inc(z_ready, 1)

            def keep(t, u, rows, out, vout):
                act.wait_ge(projected, ONE + t + 1)
                act.wait_ge(turned, ONE + t)
                act.wait_ge(k_stored, ONE + 16 * t)
                x = ps[0:rows, 3 * u:3 * u + 2, :].rearrange("p b (g d) -> p (b g) d", d=ADQ)
                nc.scalar.activation(out[:, :, ROT:ADQ], x[:, :, ROT:ADQ], ACT.Copy).then_inc(copied, 1)
                nc.scalar.activation(vout, ps[0:rows, 3 * u + 2, :], ACT.Copy).then_inc(v_kept, 1)

            def keep_tile(t, u):
                keep(t, u, P, qk[:, :, :], VA[:, ds(t, 1), :].rearrange("p o n -> p (o n)"))

            copy_tile(0)
            with act.Fori(0, NT // 2 - 1) as it:
                for u in range(2):
                    copy_tile(2 * it + u + 1)
                    keep_tile(2 * it + u, u)
            copy_tile(NT - 1)
            keep_tile(NT - 2, 0)
            keep_tile(NT - 1, 1)
            keep(NT, 0, NS, s_aqk[:, :].rearrange("p (g d) -> p g d", d=ADQ), s_av[:, :])


def attention_phase(nc, a, ps, ident, QT, KT, VA, aT, lam):
    with Scope(nc) as ctx:
        def sb(n, shape, dt=F32):
            return ctx.enter_context(nc.sbuf_tensor("at_" + n, shape, dt))

        def sem(n):
            return ctx.sem("at_" + n)

        mask = sb("mask", [P, P])
        pr = sb("probs", [P, 2, 2, SEQ])
        wT = sb("weights_T", [P, 2, SEQ])
        mx = sb("max", [P, 2, 4])
        sm = sb("sums", [P, 2, 4])
        o, sq = sb("out", [P, NT, AH, ADV]), sb("squares", [P, AH, ADV])
        st = sb("st", [P, 4, NT, AH])
        gain = sb("gain", [P, 1])
        s_tab = sem("tables_loaded")
        scored, maxed, exped = sem("scores_ready"), sem("max_ready"), sem("exp_done")
        combined = sem("weights_ready")
        turned, kept, summed = sem("weights_turned"), sem("weights_kept"), sem("values_summed")
        chain, squares = sem("chain"), sem("squares")
        out_kept, mean, root = sem("out_kept"), sem("mean"), sem("root")
        normed, out_turned, out_stored = sem("normed"), sem("out_turned"), sem("out_columns_kept")
        SC = float(ADQ) ** -0.5
        steps = [(t, h) for t in range(NT) for h in range(AH)]
        N = len(steps)

        def score_ps(c, nk):
            return ps[:, 2 * c:2 * c + 2, :].rearrange("p b n -> p (b n)")[:, 0:nk]

        block = ctx.block()

        @block.sync
        def _(sp):
            sp.dma_start(mask[:, :], a["att_mask"]).then_inc(s_tab, 16)
            sp.dma_start(gain[:, :], a["g_subln"]).then_inc(s_tab, 16)

        @block.tensor
        def _(pe):
            def scores(s, c):
                t, h = steps[s]
                nk = (t + 1) * P
                if s:
                    pe.wait_ge(exped, ONE + 2 * (s - 1) + c + 1)
                for b in range(0, nk, BANK):
                    w = min(BANK, nk - b)
                    last = nc.tensor.matmul(ps[:, 2 * c + b // BANK, 0:w],
                                            QT[c * ADQ:(c + 1) * ADQ, h, t * P:(t + 1) * P],
                                            KT[c * ADQ:(c + 1) * ADQ, h, b:b + w], start=True, stop=True)
                last.then_inc(scored, 1)

            def turn_weights(s):
                t, h = steps[s]
                pe.wait_ge(combined, ONE + s + 1)
                if s:
                    pe.wait_ge(kept, ONE + s)
                for b in range(t + 1):
                    last = nc.tensor.transpose(ps[:, 4 + b // 4, (b % 4) * P:(b % 4 + 1) * P],
                                               pr[:, s % 2, 0, b * P:(b + 1) * P], ident[:, :])
                last.then_inc(turned, 1)

            def values(s):
                t, h = steps[s]
                pe.wait_ge(kept, ONE + s + 1)
                if h == 0 and t >= 2:
                    pe.wait_ge(out_kept, ONE + t - 1)
                for b in range(t + 1):
                    last = nc.tensor.matmul(ps[:, 6 + t % 2, h * P:(h + 1) * P], wT[:, s % 2, b * P:(b + 1) * P],
                                            VA[:, b, h * ADV:(h + 1) * ADV], start=(b == 0), stop=(b == t))
                last.then_inc(summed, 1)

            scores(0, 0)
            scores(0, 1)
            for s in range(N):
                if s + 1 < N:
                    scores(s + 1, 0)
                if s:
                    values(s - 1)
                if s + 1 < N:
                    scores(s + 1, 1)
                turn_weights(s)
            values(N - 1)
            for t in range(NT):
                pe.wait_ge(normed, ONE + t + 1)
                for h in range(AH):
                    last = nc.tensor.transpose(ps[:, t, h * P:(h + 1) * P], o[:, t, h, :], ident[:, :])
                last.then_inc(out_turned, 1)

        @block.vector
        def _(dve):
            link = Chain(dve, chain)

            def maximum(s, c):
                t, h = steps[s]
                nk = (t + 1) * P
                dve.wait_ge(scored, ONE + 2 * s + c + 1)
                sc = score_ps(c, nk)
                diag = sc[:, t * P:nk]
                link(nc.vector.tensor_tensor(diag, diag, mask[:, :], ALU.add))
                m = mx[:, s % 2, :]
                link(nc.vector.tensor_reduce(m[:, c:c + 1], sc, AX_X, ALU.max))
                nc.vector.tensor_scalar(m[:, 2 + c:3 + c], m[:, c:c + 1], -SC, None, ALU.mult).then_inc(maxed, 1)

            def combine(s):
                t, h = steps[s]
                nk = (t + 1) * P
                dve.wait_ge(exped, ONE + 2 * s + 2)
                w = sm[:, s % 2, :]
                link(nc.vector.reciprocal(w[:, 2:4], w[:, 0:2]))
                p0, p1 = pr[:, s % 2, 0, 0:nk], pr[:, s % 2, 1, 0:nk]
                link(nc.vector.tensor_scalar(p1, p1, w[:, 3:4], lam[:, 0:1], ALU.mult, ALU.mult))
                nc.vector.scalar_tensor_tensor(out=p0, in0=p0, scalar=w[:, 2:3], in1=p1, op0=ALU.mult,
                                               op1=ALU.subtract).then_inc(combined, 1)

            def square_tile(t):
                dve.wait_ge(out_kept, ONE + t + 1)
                if t:
                    dve.wait_ge(squares, ONE + 2 * t)
                nc.vector.tensor_tensor(sq[:, :, :], o[:, t, :, :], o[:, t, :, :], ALU.mult).then_inc(squares, 1)
                dve.wait_ge(squares, ONE + 2 * t + 1)
                nc.vector.tensor_reduce(st[:, 0, t, :], sq[:, :, :], AX_X, ALU.add).then_inc(squares, 1)

            dve.wait_ge(s_tab, ONE + 32)
            for c in range(2):
                maximum(0, c)
            for s, (t, h) in enumerate(steps):
                if s + 1 < N:
                    maximum(s + 1, 0)
                combine(s)
                if s + 1 < N:
                    maximum(s + 1, 1)
                if t and h == 2:
                    square_tile(t - 1)
            square_tile(NT - 1)
            dve.wait_ge(squares, ONE + 2 * NT)
            nc.vector.tensor_scalar(st[:, 1, :, :], st[:, 0, :, :], 1.0 / ADV, SUB_EPS, ALU.mult,
                                    ALU.add).then_inc(mean, 1)
            dve.wait_ge(root, ONE + 1)
            link(nc.vector.reciprocal(st[:, 3, :, :], st[:, 2, :, :]))
            flat = o[:, :, :, :].rearrange("p t h e -> p (t h) e")
            inv = st[:, 3, :, :].rearrange("p t h -> p (t h)").unsqueeze(2)
            for t in range(NT):
                q = slice(t * AH, (t + 1) * AH)
                nc.vector.tensor_tensor(flat[:, q, :], flat[:, q, :], inv[:, q, :].to_broadcast([P, AH, ADV]),
                                        ALU.mult).then_inc(normed, 1)
            for t in range(NT):
                dve.wait_ge(out_turned, ONE + t + 1)
                nc.vector.tensor_scalar(aT[:, :, t * P:(t + 1) * P], ps[:, t, :].rearrange("p (h l) -> p h l", h=AH),
                                        gain[:, 0:1], 1.0 - LAM_INIT, ALU.mult, ALU.mult).then_inc(out_stored, 1)

        @block.scalar
        def _(act):
            def exps(s, c):
                t, h = steps[s]
                nk = (t + 1) * P
                act.wait_ge(maxed, ONE + 2 * s + c + 1)
                if s >= 2 and c == 0:
                    act.wait_ge(turned, ONE + s - 1)
                nc.scalar.activation(pr[:, s % 2, c, 0:nk], score_ps(c, nk), ACT.Exp,
                                     bias=mx[:, s % 2, 2 + c:3 + c], scale=SC,
                                     accum_out=sm[:, s % 2, c:c + 1]).then_inc(exped, 1)

            def keep_out(t):
                act.wait_ge(summed, ONE + AH * (t + 1))
                nc.scalar.activation(o[:, t, :, :].rearrange("p h e -> p (h e)"), ps[:, 6 + t % 2, :],
                                     ACT.Copy).then_inc(out_kept, 1)

            def keep_weights(s):
                t, h = steps[s]
                nk = (t + 1) * P
                act.wait_ge(turned, ONE + s + 1)
                if s >= 2:
                    act.wait_ge(summed, ONE + s - 1)
                nc.scalar.activation(wT[:, s % 2, 0:nk],
                                     ps[:, 4:6, :].rearrange("p b n -> p (b n)")[:, 0:nk],
                                     ACT.Copy).then_inc(kept, 1)

            exps(0, 0)
            exps(0, 1)
            for s, (t, h) in enumerate(steps):
                if s + 1 < N:
                    exps(s + 1, 0)
                keep_weights(s)
                if s + 1 < N:
                    exps(s + 1, 1)
                if t and h == 1:
                    keep_out(t - 1)
            keep_out(NT - 1)
            act.wait_ge(mean, ONE + 1)
            nc.scalar.activation(st[:, 2, :, :], st[:, 1, :, :], ACT.Sqrt).then_inc(root, 1)


def sample_phase(nc, a, ps, ident, s_rqk, s_rv, s_aqk, s_av, rT, aT, lam):
    J = NS * RH
    R = 2 * J
    with Scope(nc) as ctx:
        def sb(n, shape, dt=F32):
            return ctx.enter_context(nc.sbuf_tensor("sa_" + n, shape, dt))

        def sem(n):
            return ctx.sem("sa_" + n)

        state = sb("state", [P, J, RDV])
        qz = sb("q_padded", [P, J * J])
        km = sb("k_masked", [NS, 2, RH * RDK])
        rn = sb("ret_normed", [J, RDV])
        junk = sb("junk", [R, BANK])
        st = sb("st", [R, 8])
        qb = sb("att_q_padded", [P, J * R])
        kT = sb("att_kT", [P, AH, NS])
        kpg = sb("key_pages", [P, 2, NPAGE, AH, PAGE])
        vpg = sb("value_pages", [P, 2, NPAGE, AH * ADV])
        sc = sb("scores", [R, PAST + 1])
        pr = sb("probs", [R, PAST + 1])
        pz = sb("probs_padded", [P, NPAGE, NS * (R + 8)])
        pn, pnT = sb("probs_self", [R, NS]), sb("probs_self_T", [NS, R])
        sel = sb("selectors", [R, 2 + NS + AH])
        o2, o3 = sb("out_rows", [R, AH, ADV]), sb("out", [NS, AH, ADV])
        on, osq = sb("out_normed", [NS, AH, ADV]), sb("out_squares", [NS, AH, ADV])
        ost = sb("out_st", [NS, 4, AH])
        gain = sb("gain", [P, 1])
        pt = sb("page_table", [1, NS * NPAGE], I32)
        s_tab, s_pt, s_state = sem("tables_loaded"), sem("page_table_loaded"), sem("states_loaded")
        k_in = [sem(f"key_pages{u}") for u in range(2)]
        v_in = [ctx.queue_sem(f"sa_value_pages{u}") for u in range(2)]
        zeroed, q_turned, q_kept = sem("padding_zeroed"), sem("q_turned"), sem("q_kept")
        kv_ready, state_new, stored = sem("outer_products"), sem("state_new"), sem("stored")
        r_out, r_sq, r_mean, r_root, r_norm = (sem("ret_" + n) for n in ("out", "squares", "mean", "root", "normed"))
        r_turned, r_kept = sem("ret_turned"), sem("ret_kept")
        km_ready, scored, s_used, s_evac = sem("k_masked"), sem("scored"), sem("keys_used"), sem("scores_kept")
        maxed, exped, p_turned, p_kept, v_used, summed = (sem(n) for n in (
            "maxed", "exped", "probs_turned", "probs_kept", "values_used", "values_summed"))
        o2_ready, picked, o3_ready, a_mean, a_root, a_norm, a_turned, a_kept = (sem(n) for n in (
            "rows_weighted", "rows_picked", "out_kept", "out_mean", "out_root", "out_normed", "out_turned",
            "out_columns_kept"))
        self_ready, self_turned = sem("self_ready"), sem("self_turned")
        chain = sem("chain")
        SCALE, SC = float(RDK) ** -0.5, float(ADQ) ** -0.5
        gamma = [float(np.exp(np.log(1.0 - 2.0 ** (-5.0 - h)))) for h in range(RH)]

        block = ctx.block()

        @block.sync
        def _(sp):
            sp.dma_start(pt[:, :], a["page_table"]).then_inc(s_pt, 16)
            sp.dma_start(sel[:, :], a["sel"]).then_inc(s_tab, 16)
            sp.dma_start(gain[:, :], a["g_subln"]).then_inc(s_tab, 16)
            sp.wait_ge(s_pt, ONE + 16)
            for b in range(NS):
                u = b % 2
                for pg in range(NPAGE):
                    n = b * NPAGE + pg
                    pid = sp.value_load(pt[0:1, n:n + 1], min_val=0, max_val=POOL - 1)
                    if b >= 2 and pg == 0:
                        sp.wait_ge(s_used, ONE + b - 1)
                    sp.dma_start(kpg[:, u, pg, :, :], a["cache_kT"][ds(pid, 1)].rearrange("o h p n -> p (o h) n")
                                 ).then_inc(k_in[u], 16)

        @block.gpsimd
        def _(pool):
            nc.gpsimd.memset(qz[:, :], 0.0).then_inc(zeroed, 1)
            nc.gpsimd.memset(qb[:, :], 0.0).then_inc(zeroed, 1)
            nc.gpsimd.memset(pz[:, :, :], 0.0).then_inc(zeroed, 1)
            pool.wait_ge(s_pt, ONE + 16)
            for b in range(NS):
                u = b % 2
                for pg in range(NPAGE):
                    n = b * NPAGE + pg
                    pid = pool.value_load(pt[0:1, n:n + 1], min_val=0, max_val=POOL - 1)
                    if b >= 2 and pg == 0:
                        pool.wait_ge(v_used, ONE + b - 1)
                    pool.dma_start(vpg[:, u, pg, :], a["cache_v"][ds(pid, 1)].rearrange("o p n -> p (o n)")
                                   ).then_inc(v_in[u], 16)

        @block.scalar
        def _(act):
            act.dma_start(state[:, :, :], a["state"].rearrange("b h k v -> k (b h) v")).then_inc(s_state, 16)
            act.wait_ge(r_out, ONE + 1)
            nc.scalar.activation(junk[0:J, 0:RDV], ps[0:J, 4, 0:RDV], ACT.Square,
                                 accum_out=st[0:J, 0:1]).then_inc(r_sq, 1)
            act.wait_ge(r_mean, ONE + 1)
            nc.scalar.activation(st[0:J, 2:3], st[0:J, 1:2], ACT.Sqrt).then_inc(r_root, 1)
            act.wait_ge(state_new, ONE + NS)
            act.dma_start(a["o_ret_s"].rearrange("b h k v -> k (b h) v"), state[:, :, :]).then_inc(stored, 16)
            act.wait_ge(maxed, ONE + 1)
            nc.scalar.activation(pr[:, :], sc[:, :], ACT.Exp, bias=st[:, 5:6], scale=SC,
                                 accum_out=st[:, 6:7]).then_inc(exped, 1)
            act.wait_ge(a_mean, ONE + 1)
            nc.scalar.activation(ost[:, 2, :], ost[:, 1, :], ACT.Sqrt).then_inc(a_root, 1)
            act.wait_ge(stored, ONE + 16)

        @block.tensor
        def _(pe):
            for bank, src, off in ((0, s_rqk, 0), (1, s_aqk, 0), (2, s_aqk, AH * 2 * ADQ)):
                for h in range(RH):
                    last = nc.tensor.transpose(ps[:, bank, h * NS:(h + 1) * NS],
                                               src[:, off + h * P:off + (h + 1) * P], ident[0:NS, 0:NS])
            last.then_inc(q_turned, 1)
            pe.wait_ge(q_kept, ONE + 1)
            for b in range(NS):
                pe.wait_ge(km_ready, ONE + b + 1)
                if b >= 2:
                    pe.wait_ge(state_new, ONE + b - 1)
                for h in range(RH):
                    last = nc.tensor.matmul(ps[:, 2 * (b % 2) + h // 2, (h % 2) * RDV:(h % 2 + 1) * RDV],
                                            km[:, b % 2, h * RDK:(h + 1) * RDK], s_rv[:, h * RDV:(h + 1) * RDV],
                                            start=True, stop=True)
                last.then_inc(kv_ready, 1)
                pe.wait_ge(k_in[b % 2], ONE + 16 * NPAGE * (b // 2 + 1))
                for h in range(AH):
                    j = b * AH + h
                    last = nc.tensor.matmul(ps[0:R, 5, :], qb[:, j * R:(j + 1) * R], kpg[:, b % 2, :, h, :],
                                            start=(j == 0), stop=(j == J - 1))
                last.then_inc(s_used, 1)
            pe.wait_ge(state_new, ONE + NS)
            for j in range(J):
                last = nc.tensor.matmul(ps[0:J, 4, 0:RDV], qz[:, j * J:(j + 1) * J], state[:, j, :],
                                        start=(j == 0), stop=(j == J - 1))
            last.then_inc(r_out, 1)
            for b in range(NS):
                for h in range(AH):
                    j = b * AH + h
                    last = nc.tensor.matmul(ps[0:R, 6, 0:1], qb[:, j * R:(j + 1) * R], kT[:, h, b:b + 1],
                                            start=(j == 0), stop=(j == J - 1))
            last.then_inc(scored, 1)
            pe.wait_ge(r_norm, ONE + 1)
            for half in range(2):
                last = nc.tensor.transpose(ps[:, 7, half * J:(half + 1) * J], rn[:, half * P:(half + 1) * P],
                                           ident[0:J, 0:J])
            last.then_inc(r_turned, 1)
            pe.wait_ge(exped, ONE + 1)
            for pg in range(NPAGE):
                last = nc.tensor.transpose(ps[:, 0, pg * R:(pg + 1) * R], pr[:, pg * PAGE:(pg + 1) * PAGE],
                                           ident[0:R, 0:R])
            last.then_inc(p_turned, 1)
            pe.wait_ge(self_ready, ONE + 1)
            nc.tensor.transpose(ps[0:NS, 1, 0:R], pn[:, :], ident[0:R, 0:R]).then_inc(self_turned, 1)
            pe.wait_ge(p_kept, ONE + 2)
            for b in range(NS):
                pe.wait_ge(v_in[b % 2], 16 * NPAGE * (b // 2 + 1))
                for pg in range(NPAGE):
                    last = nc.tensor.matmul(ps[0:R, 3, :], pz[:, pg, b * R:(b + 1) * R], vpg[:, b % 2, pg, :],
                                            start=(b == 0 and pg == 0), stop=False)
                last.then_inc(v_used, 1)
            nc.tensor.matmul(ps[0:R, 3, :], pnT[:, :], s_av[:, :], start=False, stop=True).then_inc(summed, 1)
            pe.wait_ge(o2_ready, ONE + 1)
            nc.tensor.matmul(ps[0:NS, 2, :], sel[:, 2:2 + NS], o2[:, :, :].rearrange("p h e -> p (h e)"),
                             start=True, stop=True).then_inc(picked, 1)
            pe.wait_ge(a_norm, ONE + 1)
            pe.wait_ge(p_kept, ONE + 2)
            for h in range(AH):
                last = nc.tensor.transpose(ps[:, 4, h * NS:(h + 1) * NS], on[:, h, :], ident[0:NS, 0:NS])
            last.then_inc(a_turned, 1)

        @block.vector
        def _(dve):
            link = Chain(dve, chain)
            def mask_k(b):
                if b >= 2:
                    dve.wait_ge(kv_ready, ONE + b - 1)
                nc.vector.tensor_scalar(km[:, b % 2, :], s_rqk[:, RH * RDK:], ident[0:NS, b:b + 1], SCALE,
                                        ALU.mult, ALU.mult).then_inc(km_ready, 1)

            mask_k(0)
            mask_k(1)
            dve.wait_ge(zeroed, ONE + 3)
            dve.wait_ge(q_turned, ONE + 1)
            by_head = "p (h b) -> p b h"
            nc.vector.tensor_copy(qz[:, 0:J * J:J + 1].rearrange("p (b h) -> p b h", b=NS),
                                  ps[:, 0, 0:J].rearrange(by_head, b=NS))
            for c in range(2):
                rows = slice(c * ADQ, (c + 1) * ADQ)
                nc.vector.tensor_copy(qb[rows, c:J * R:R + 2].rearrange("p (b h) -> p b h", b=NS),
                                      ps[rows, 1, 0:J].rearrange(by_head, b=NS))
            nc.vector.tensor_copy(kT[:, :, :], ps[:, 2, 0:J].rearrange("p (h b) -> p h b", b=NS)).then_inc(q_kept, 1)
            dve.wait_ge(s_state, ONE + 16)
            for b in range(NS):
                dve.wait_ge(kv_ready, ONE + b + 1)
                if b + 2 < NS:
                    mask_k(b + 2)
                for h in range(RH):
                    j = b * RH + h
                    last = nc.vector.scalar_tensor_tensor(
                        out=state[:, j, :], in0=state[:, j, :], scalar=gamma[h],
                        in1=ps[:, 2 * (b % 2) + h // 2, (h % 2) * RDV:(h % 2 + 1) * RDV],
                        op0=ALU.mult, op1=ALU.add)
                last.then_inc(state_new, 1)
            dve.wait_ge(r_sq, ONE + 1)
            nc.vector.tensor_scalar(st[0:J, 1:2], st[0:J, 0:1], 1.0 / RDV, EPS, ALU.mult, ALU.add).then_inc(r_mean, 1)
            dve.wait_ge(r_root, ONE + 1)
            link(nc.vector.reciprocal(st[0:J, 3:4], st[0:J, 2:3]))
            nc.vector.tensor_scalar(rn[:, :], ps[0:J, 4, 0:RDV], st[0:J, 3:4], None, ALU.mult).then_inc(r_norm, 1)
            dve.wait_ge(scored, ONE + 1)
            nc.vector.tensor_copy(sc[:, 0:PAST], ps[0:R, 5, :])
            link(nc.vector.tensor_copy(sc[:, PAST:], ps[0:R, 6, 0:1]))
            link(nc.vector.tensor_reduce(st[:, 4:5], sc[:, :], AX_X, ALU.max))
            nc.vector.tensor_scalar(st[:, 5:6], st[:, 4:5], -SC, None, ALU.mult).then_inc(maxed, 1)
            dve.wait_ge(r_turned, ONE + 1)
            for half in range(2):
                last = nc.vector.tensor_copy(rT[:, half:KD:2, SEQ:T],
                                             ps[:, 7, half * J:(half + 1) * J].rearrange("p (b h) -> p h b", b=NS))
            last.then_inc(r_kept, 1)
            dve.wait_ge(exped, ONE + 1)
            dve.wait_ge(s_tab, ONE + 32)
            nc.vector.tensor_scalar(pn[:, :], sel[:, 2:2 + NS], pr[:, PAST:], None, ALU.mult).then_inc(self_ready, 1)
            link(nc.vector.reciprocal(st[:, 7:8], st[:, 6:7]))
            link(nc.vector.scalar_tensor_tensor(out=st[:, 4:5], in0=sel[:, 1:2], scalar=lam[0:R, 0:1],
                                                in1=sel[:, 0:1], op0=ALU.mult, op1=ALU.subtract))
            link(nc.vector.tensor_scalar(st[:, 5:6], st[:, 4:5], st[:, 7:8], -1.0, ALU.mult, ALU.mult))
            dve.wait_ge(p_turned, ONE + 1)
            for pg in range(NPAGE):
                last = nc.vector.tensor_copy(
                    pz[:, pg, :].rearrange("p (b w) -> p b w", b=NS)[:, :, 0:8],
                    ps[:, 0, pg * R:(pg + 1) * R].rearrange("p (b w) -> p b w", b=NS))
            last.then_inc(p_kept, 1)
            dve.wait_ge(self_turned, ONE + 1)
            nc.vector.tensor_copy(pnT[:, :], ps[0:NS, 1, 0:R]).then_inc(p_kept, 1)
            dve.wait_ge(summed, ONE + 1)
            nc.vector.scalar_tensor_tensor(
                out=o2[:, :, :], in0=ps[0:R, 3, :].rearrange("p (h e) -> p h e", h=AH), scalar=st[:, 5:6],
                in1=sel[:, 2 + NS:].unsqueeze(2).to_broadcast([R, AH, ADV]), op0=ALU.mult,
                op1=ALU.mult).then_inc(o2_ready, 1)
            dve.wait_ge(picked, ONE + 1)
            link(nc.vector.tensor_copy(o3[:, :, :], ps[0:NS, 2, :].rearrange("p (h e) -> p h e", h=AH)))
            link(nc.vector.tensor_tensor(osq[:, :, :], o3[:, :, :], o3[:, :, :], ALU.mult))
            link(nc.vector.tensor_reduce(ost[:, 0, :], osq[:, :, :], AX_X, ALU.add))
            nc.vector.tensor_scalar(ost[:, 1, :], ost[:, 0, :], 1.0 / ADV, SUB_EPS, ALU.mult, ALU.add).then_inc(a_mean, 1)
            dve.wait_ge(a_root, ONE + 1)
            link(nc.vector.reciprocal(ost[:, 3, :], ost[:, 2, :]))
            nc.vector.tensor_tensor(on[:, :, :], o3[:, :, :], ost[:, 3, :].unsqueeze(2).to_broadcast([NS, AH, ADV]),
                                    ALU.mult).then_inc(a_norm, 1)
            dve.wait_ge(a_turned, ONE + 1)
            nc.vector.tensor_scalar(aT[:, :, SEQ:T], ps[:, 4, 0:J].rearrange("p (h b) -> p h b", b=NS),
                                    gain[:, 0:1], 1.0 - LAM_INIT, ALU.mult, ALU.mult).then_inc(a_kept, 1)


def merge_phase(nc, a, ps, zT, rT, aT, mT, w_out):
    NW = 2 * KD + KD + AH
    with Scope(nc) as ctx:
        w = ctx.enter_context(nc.sbuf_tensor("mg_w", [P, 2, NW, P], F32))
        sg = ctx.enter_context(nc.sbuf_tensor("mg_gates", [P, 2, 2, TB], F32))
        pd = ctx.enter_context(nc.sbuf_tensor("mg_products", [P, 2, 2, TB], F32))

        def sem(n):
            return ctx.sem("mg_" + n)

        w_in, s_wo = [sem(f"w_loaded{u}") for u in range(2)], sem("w_out_loaded")
        ready, gated, mult, merged = ([sem(f"{n}{s}") for s in range(2)] for n in
                                      ("products_ready", "gates_ready", "gated", "merged"))
        steps = [(u, b) for u in range(2) for b in range(3)]

        block = ctx.block()

        @block.sync
        def _(sp):
            def load(it, u):
                sp.dma_start(w[:, u, :, :], a["w_merge"][ds(2 * it + u, 1)].rearrange("o p k n -> p (o k) n")
                             ).then_inc(w_in[u], 16)

            load(0, 0)
            load(0, 1)
            sp.dma_start(w_out[:, :, :], a["w_out"]).then_inc(s_wo, 16)
            with sp.Fori(1, KD // 2) as it:
                sp.wait_ge(ready[0], ONE + 3 * it - 1)
                load(it, 0)
                sp.wait_ge(ready[1], ONE + 3 * it)
                load(it, 1)
            sp.wait_ge(s_wo, ONE + 16)

        @block.tensor
        def _(pe):
            with pe.Fori(0, KD // 2) as it:
                for k, (u, b) in enumerate(steps):
                    s, lo, hi = k % 2, *BLOCKS[b]
                    if b == 0:
                        pe.wait_ge(w_in[u], ONE + 16 * it + 16)
                    pe.wait_ge(merged[s], ONE + 3 * it + k // 2)
                    n = 0
                    for bank, x, cnt in ((0, zT, KD), (1, zT, KD), (2, rT, KD), (3, aT, AH)):
                        for c in range(cnt):
                            last = nc.tensor.matmul(ps[:, 4 * s + bank, 0:TB], w[:, u, n, :], x[:, c, lo:hi],
                                                    start=(c == 0), stop=(c == cnt - 1))
                            n += 1
                    last.then_inc(ready[s], 1)

        @block.scalar
        def _(act):
            with act.Fori(0, KD // 2) as it:
                for k in range(6):
                    s = k % 2
                    act.wait_ge(ready[s], ONE + 3 * it + k // 2 + 1)
                    act.wait_ge(merged[s], ONE + 3 * it + k // 2)
                    nc.scalar.activation(sg[:, s, :, :], ps[:, 4 * s:4 * s + 2, 0:TB],
                                         ACT.Sigmoid).then_inc(gated[s], 1)

        @block.vector
        def _(dve):
            with dve.Fori(0, KD // 2) as it:
                for k, (u, b) in enumerate(steps):
                    s, lo, hi = k % 2, *BLOCKS[b]
                    n = 3 * it + k // 2
                    dve.wait_ge(gated[s], ONE + n + 1)
                    nc.vector.tensor_tensor(pd[:, s, :, :], sg[:, s, :, :], ps[:, 4 * s + 2:4 * s + 4, 0:TB],
                                            ALU.mult).then_inc(mult[s], 1)
                    dve.wait_ge(mult[s], ONE + n + 1)
                    nc.vector.tensor_tensor(mT[:, ds(2 * it + u, 1), lo:hi], pd[:, s, 0:1, :], pd[:, s, 1:2, :],
                                            ALU.add).then_inc(merged[s], 1)


def residual_phase(nc, a, ps, ident, mT, w, h_dram, z2T):
    with Scope(nc) as ctx:
        def sb(n, shape):
            return ctx.enter_context(nc.sbuf_tensor("rs_" + n, shape, F32))

        gain = sb("gain_ffn", [P, KD])
        mc = sb("m_tile", [P, 2, KD, P])
        x, h, z = sb("x", [P, 2, D]), sb("h", [P, 2, D]), sb("z", [P, D])
        junk = sb("junk", [P, D])
        st = sb("st", [P, 2, 4])

        def sem(n):
            return ctx.sem("rs_" + n)

        s_gain = sem("gain_ffn_loaded")
        scaled, turned = sem("rows_scaled"), sem("rows_turned")
        m_in, x_in, ready, added, out, squared, mean, root, inverse, kept = ([sem(f"{n}{u}") for u in range(2)]
            for n in ("m_tile_ready", "x_loaded", "product_ready", "added", "stored", "squares_summed", "mean_ready",
                      "root_ready", "inverse_ready", "columns_kept"))

        def over_tiles(eng, step):
            with eng.Fori(0, NT // 2) as it:
                for u in range(2):
                    step(it, u, P)
            step(NT // 2, 0, NS)

        def with_previous(step, previous):
            def run(eng):
                step(0, 0, P)
                step(0, 1, P)
                previous(0, 0, P)
                with eng.Fori(1, NT // 2) as it:
                    step(it, 0, P)
                    previous(it - 1, 1, P)
                    step(it, 1, P)
                    previous(it, 0, P)
                step(NT // 2, 0, NS)
                previous(NT // 2 - 1, 1, P)
                previous(NT // 2, 0, NS)
            return run

        block = ctx.block()

        @block.sync
        def _(sp):
            sp.dma_start(gain[:, :], a["g_ffn"]).then_inc(s_gain, 16)

            def load(it, u, rows):
                sp.wait_ge(added[u], ONE + it)
                sp.dma_start(x[0:rows, u, :], a["x"][ds((2 * it + u) * P, rows), :]).then_inc(x_in[u], 16)
            over_tiles(sp, load)

        @block.scalar
        def _(act):
            def step(it, u, rows):
                act.wait_ge(added[u], ONE + it + 1)
                act.dma_start(h_dram[ds((2 * it + u) * P, rows), :], h[0:rows, u, :]).then_inc(out[u], 16)
                nc.scalar.activation(junk[0:rows, :], h[0:rows, u, :], ACT.Square,
                                     accum_out=st[0:rows, u, 0:1]).then_inc(squared[u], 1)
                act.wait_ge(mean[u], ONE + it + 1)
                nc.scalar.activation(st[0:rows, u, 2:3], st[0:rows, u, 1:2], ACT.Sqrt).then_inc(root[u], 1)
            over_tiles(act, step)
            act.wait_ge(out[0], ONE + 16 * (NT // 2 + 1))
            act.wait_ge(out[1], ONE + 16 * (NT // 2))

        @block.gpsimd
        def _(pool):
            def copy(it, u, rows):
                pool.wait_ge(ready[u], ONE + it)
                nc.gpsimd.tensor_copy(mc[:, u, :, 0:rows], mT[:, :, ds((2 * it + u) * P, rows)]).then_inc(m_in[u], 1)
            over_tiles(pool, copy)

        @block.tensor
        def _(pe):
            def product(it, u, rows):
                pe.wait_ge(m_in[u], ONE + it + 1)
                pe.wait_ge(added[u], ONE + it)
                for b in range(2):
                    for c in range(KD):
                        last = nc.tensor.matmul(ps[0:rows, 2 * u + b, :], mc[:, u, c, 0:rows],
                                                w[:, c, b * BANK:(b + 1) * BANK], start=(c == 0), stop=(c == KD - 1))
                last.then_inc(ready[u], 1)

            def turn(it, u, rows):
                pe.wait_ge(scaled, ONE + 2 * it + u + 1)
                pe.wait_ge(kept[u], ONE + it)
                for c in range(KD):
                    last = nc.tensor.transpose(ps[:, 4 + 2 * u + c // 4, (c % 4) * P:(c % 4) * P + rows],
                                               z[0:rows, c * P:(c + 1) * P], ident[0:rows, 0:rows])
                last.then_inc(turned, 1)
            with_previous(product, turn)(pe)

        @block.vector
        def _(dve):
            def add(it, u, rows):
                dve.wait_ge(ready[u], ONE + it + 1)
                dve.wait_ge(x_in[u], ONE + 16 * it + 16)
                dve.wait_ge(out[u], ONE + 16 * it)
                dve.wait_ge(inverse[u], ONE + it)
                nc.vector.tensor_tensor(h[0:rows, u, :], x[0:rows, u, :],
                                        ps[0:rows, 2 * u:2 * u + 2, :].rearrange("p b n -> p (b n)"),
                                        ALU.add).then_inc(added[u], 1)

            def scale(it, u, rows):
                dve.wait_ge(squared[u], ONE + it + 1)
                nc.vector.tensor_scalar(st[0:rows, u, 1:2], st[0:rows, u, 0:1], 1.0 / D, EPS,
                                        ALU.mult, ALU.add).then_inc(mean[u], 1)
                dve.wait_ge(root[u], ONE + it + 1)
                nc.vector.reciprocal(st[0:rows, u, 3:4], st[0:rows, u, 2:3]).then_inc(inverse[u], 1)
                dve.wait_ge(inverse[u], ONE + it + 1)
                dve.wait_ge(turned, ONE + 2 * it + u)
                nc.vector.tensor_scalar(z[0:rows, :], h[0:rows, u, :], st[0:rows, u, 3:4], None,
                                        ALU.mult).then_inc(scaled, 1)

            def keep(it, u, rows):
                dve.wait_ge(turned, ONE + 2 * it + u + 1)
                nc.vector.tensor_tensor(
                    z2T[:, :, ds((2 * it + u) * P, rows)],
                    ps[:, 4 + 2 * u:6 + 2 * u, :].rearrange("p b (c r) -> p (b c) r", r=P)[:, :, 0:rows],
                    gain[:, :].unsqueeze(2).to_broadcast([P, KD, rows]), ALU.mult).then_inc(kept[u], 1)

            dve.wait_ge(s_gain, ONE + 16)
            add(0, 0, P)
            scale(0, 0, P)
            add(0, 1, P)
            keep(0, 0, P)
            scale(0, 1, P)
            with dve.Fori(1, NT // 2) as it:
                add(it, 0, P)
                keep(it - 1, 1, P)
                scale(it, 0, P)
                add(it, 1, P)
                keep(it, 0, P)
                scale(it, 1, P)
            add(NT // 2, 0, NS)
            keep(NT // 2 - 1, 1, P)
            scale(NT // 2, 0, NS)
            keep(NT // 2, 0, NS)


def routing_phase(nc, a, ps, ident, z2T, gT, iT, jT):
    NTT = NT + 1
    with Scope(nc) as ctx:
        def sb(n, shape, dt=F32):
            return ctx.enter_context(nc.sbuf_tensor("rt_" + n, shape, dt))

        def sem(n):
            return ctx.sem("rt_" + n)

        wq = sb("wq", [P, 2, KD, P])
        sk = sb("sub_keys", [P, 2 * PH, NK])
        qT = sb("qT", [P, 2, T])
        sc, sc2 = sb("scores", [P, 2, NTT, NK]), sb("scores_rest", [P, NTT, NK])
        v = sb("best", [P, 2, NTT, TOPK])
        vi = sb("best_index", [P, 2, NTT, TOPK], U32)
        vf = sb("best_index_f", [P, 2, NTT, TOPK])
        R = TOPK // 2
        LASTROW = R + 1
        NSUM = (LASTROW + 1) * R
        cs, cs2 = sb("sums", [P, NTT, NSUM]), sb("sums_rest", [P, NTT, NSUM])
        pos, prc = sb("pos", [P, NTT, TOPK], U32), sb("pos_row_column", [P, 2, NTT, TOPK], U32)
        prcf, ranks = sb("pos_row_column_f", [P, 2, NTT, TOPK]), sb("ranks", [P, 2, NTT, TOPK])
        index = sb("index_by_rank", [P, 2, NTT, TOPK])
        flag = sb("flag", [P, 2, NTT, TOPK])
        hot = sb("rank_onehots", [P, 2 * NTT, TOPK, TOPK])
        it_i, it_f = sb("iota_i", [P, TOPK], I32), sb("iota_f", [P, TOPK])
        best = sb("best_sums", [P, NTT, TOPK])
        top = sb("top", [P, NTT, PH, TOPK])
        tij = sb("top_ij", [P, 2 * NTT, PH, TOPK])
        sub, ex, gt = sb("shifted", [P, NTT, PH, TOPK]), sb("exps", [P, NTT, PH, TOPK]), sb("gates", [P, NTT, PH, TOPK])
        carrier, pool_carrier = sb("wait_carrier", [P, 1]), sb("pool_wait_carrier", [P, 1])
        sm = sb("sums_e", [P, 2, NTT * PH])

        s_sk = sem("sub_keys_loaded")
        w_in = [sem(f"wq_loaded{c}") for c in range(2)]
        q_ready, q_kept = [sem(f"q_ready{c}") for c in range(2)], [sem(f"q_kept{c}") for c in range(2)]
        s_ready, s_kept = sem("scores_ready"), sem("scores_kept")
        s_kept_c = [sem(f"scores_kept{c}") for c in range(2)]
        s_used = [sem(f"scores_used{c}") for c in range(2)]
        chain, zeroed, it_ready = sem("chain"), sem("zeroed"), sem("iota_ready")
        pos_ready, decoded, pool_chain = sem("pos_ready"), sem("ranks_ready"), sem("pool_chain")
        hots_ready, picked, looked_up = sem("onehots_ready"), sem("onehots_times_index"), sem("looked_up")
        shifted, exped, gates_ready, turned, kept = (sem(n) for n in (
            "shifted", "exped", "gates_ready", "turned", "kept"))
        GROUPS = [(0, 3), (3, 6), (6, 9)]
        NEGBIG = -3.0e38
        NLINK = 2 * 4 + 1 + 5
        NDECODE = 4

        block = ctx.block()

        @block.sync
        def _(sp):
            def load(h, c):
                sp.wait_ge(q_ready[c], ONE + h)
                sp.dma_start(wq[:, c, :, :], a["w_query"][ds(2 * h + c, 1)].rearrange("o p k n -> p (o k) n")
                             ).then_inc(w_in[c], 16)
            load(0, 0)
            load(0, 1)
            sp.dma_start(sk[:, :, :], a["sub_keysT"]).then_inc(s_sk, 16)
            with sp.Fori(1, PH) as h:
                for c in range(2):
                    load(h, c)

        @block.gpsimd
        def _(pool):
            for c in range(2):
                nc.gpsimd.memset(sc[:, c, NT, :], 0.0).then_inc(zeroed, 1)
            nc.gpsimd.iota(it_i[:, :], pattern=[[1, TOPK]], base=0, channel_multiplier=0).then_inc(zeroed, 1)
            pool.wait_ge(zeroed, ONE + 3)
            nc.gpsimd.tensor_copy(it_f[:, :], it_i[:, :]).then_inc(it_ready, 1)

            pool.wait_ge(it_ready, ONE + 1)

            def carry():
                nc.gpsimd.tensor_tensor(pool_carrier[:, :], it_f[:, 0:1], it_f[:, 0:1], ALU.mult)

            with pool.Fori(0, PH) as h:
                step = Chain(pool, pool_chain, h * NDECODE)
                pool.wait_ge(pos_ready, ONE + h + 1)
                pool.wait_ge(picked, ONE + h)
                row, col = prcf[:, 0, :, :], prcf[:, 1, :, :]
                carry()
                nc.gpsimd.tensor_copy(index[:, :, :, :], vf[:, :, :, :])
                step(nc.gpsimd.tensor_copy(prcf[:, :, :, :], prc[:, :, :, :]))
                carry()
                nc.gpsimd.tensor_scalar(flag[:, 0, :, :], row, float(LASTROW), None, ALU.is_equal)
                nc.gpsimd.tensor_scalar(flag[:, 1, :, :], row, 1.0, float(R), ALU.is_equal, ALU.mult)
                step(nc.gpsimd.tensor_scalar(ranks[:, 0, :, :], row, -1.0, 0.0, ALU.add, ALU.max))
                step(nc.gpsimd.tensor_tensor(flag[:, 0, :, :], flag[:, 0, :, :], col, ALU.mult))
                nc.gpsimd.tensor_tensor(ranks[:, 0, :, :], ranks[:, 0, :, :], flag[:, 0, :, :], ALU.add)
                step(nc.gpsimd.tensor_tensor(ranks[:, 1, :, :], col, flag[:, 0, :, :], ALU.subtract))
                nc.gpsimd.tensor_tensor(ranks[:, 1, :, :], ranks[:, 1, :, :], flag[:, 1, :, :], ALU.add
                                        ).then_inc(decoded, 1)
                assert step.n == NDECODE, step.n
                pool.wait_ge(hots_ready, ONE + h + 1)
                nc.gpsimd.tensor_tensor(hot[:, :, :, :], hot[:, :, :, :],
                                        index[:, :, :, :].rearrange("p c t r -> p (c t) r").unsqueeze(2)
                                        .to_broadcast([P, 2 * NTT, TOPK, TOPK]), ALU.mult).then_inc(picked, 1)

        @block.tensor
        def _(pe):
            def queries(h, c):
                pe.wait_ge(w_in[c], ONE + 16 * h + 16)
                pe.wait_ge(q_kept[c], ONE + h)
                for b, (lo, hi) in enumerate(BLOCKS):
                    for k in range(KD):
                        last = nc.tensor.matmul(ps[:, 3 * c + b, 0:TB], wq[:, c, k, :], z2T[:, k, lo:hi],
                                                start=(k == 0), stop=(k == KD - 1))
                last.then_inc(q_ready[c], 1)

            def scores(h, c):
                pe.wait_ge(q_kept[c], ONE + h + 1)
                for n, (lo, hi) in enumerate(GROUPS):
                    m = 3 * c + n
                    if not isinstance(h, int) or 6 * h + m >= 2:
                        pe.wait_ge(s_kept, ONE + 6 * h + m - 1)
                    for t in range(lo, hi):
                        r = P if t < NT else NS
                        last = nc.tensor.matmul(ps[0:r, 6 + m % 2, (t - lo) * NK:(t - lo + 1) * NK],
                                                qT[:, c, t * P:t * P + r],
                                                sk[:, ds(2 * h + c, 1), :].rearrange("p o n -> p (o n)"),
                                                start=True, stop=True)
                    last.then_inc(s_ready, 1)

            queries(0, 0)
            pe.wait_ge(s_sk, ONE + 16)
            scores(0, 0)
            queries(0, 1)
            scores(0, 1)
            with pe.Fori(1, PH) as h:
                queries(h, 0)
                queries(h, 1)
                scores(h, 0)
                scores(h, 1)
            pe.wait_ge(gates_ready, ONE + 1)
            pe.wait_ge(s_kept, ONE + 6 * PH)
            for n, src in enumerate((gt, tij[:, 0:NTT], tij[:, NTT:2 * NTT])):
                if n == 1:
                    pe.wait_ge(looked_up, ONE + PH)
                if n == 2:
                    pe.wait_ge(kept, ONE + 1)
                for t, lo, r in TILES:
                    last = nc.tensor.transpose(ps[:, 3 * (n % 2) + t // 4, (t % 4) * P:(t % 4) * P + r],
                                               src[0:r, t, :, :].rearrange("p h k -> p (h k)"), ident[0:r, 0:r])
                last.then_inc(turned, 1)

        @block.scalar
        def _(act):
            act.wait_ge(zeroed, ONE + 3)

            def keep_queries(h, c, first=False):
                act.wait_ge(q_ready[c], ONE + h + 1)
                if not first:
                    act.wait_ge(s_ready, ONE + 6 * h - 3 + 3 * c)
                nc.scalar.activation(qT[:, c, :].rearrange("p (b n) -> p b n", b=3), ps[:, 3 * c:3 * c + 3, 0:TB],
                                     ACT.Copy).then_inc(q_kept[c], 1)

            def keep_scores(h, c):
                act.wait_ge(s_used[c], ONE + h)
                for n, (lo, hi) in enumerate(GROUPS):
                    m = 3 * c + n
                    act.wait_ge(s_ready, ONE + 6 * h + m + 1)
                    parts = [(lo, hi, P)] if hi <= NT else [(lo, NT, P), (NT, hi, NS)]
                    for x, y, r in parts:
                        last = nc.scalar.activation(
                            sc[0:r, c, x:y, :],
                            ps[0:r, 6 + m % 2, (x - lo) * NK:(y - lo) * NK].rearrange("p (t n) -> p t n", n=NK),
                            ACT.Copy)
                    last.then_inc(s_kept, 1)

            keep_queries(0, 0, True)
            keep_scores(0, 0)
            keep_queries(0, 1, True)
            keep_scores(0, 1)
            with act.Fori(1, PH) as h:
                keep_queries(h, 0)
                keep_queries(h, 1)
                keep_scores(h, 0)
                keep_scores(h, 1)
            act.wait_ge(shifted, ONE + 1)
            nc.scalar.activation(ex[:, :, :, :].rearrange("p t h k -> p (t h k)"),
                                 sub[:, :, :, :].rearrange("p t h k -> p (t h k)"), ACT.Exp).then_inc(exped, 1)
            for n, dst in enumerate((gT, iT, jT)):
                act.wait_ge(turned, ONE + n + 1)
                nc.scalar.activation(dst[:, :], ps[:, 3 * (n % 2):3 * (n % 2) + 3, :]
                                     .rearrange("p b n -> p (b n)")[:, 0:T], ACT.Copy).then_inc(kept, 1)

        @block.vector
        def _(dve):
            dve.wait_ge(it_ready, ONE + 1)

            def onehots(h):
                dve.wait_ge(decoded, ONE + h + 1)
                dve.wait_ge(looked_up, ONE + h)
                nc.vector.tensor_tensor(
                    hot[:, :, :, :],
                    ranks[:, :, :, :].rearrange("p c t k -> p (c t) k").unsqueeze(3)
                    .to_broadcast([P, 2 * NTT, TOPK, TOPK]),
                    it_f[:, :].unsqueeze(1).unsqueeze(1).to_broadcast([P, 2 * NTT, TOPK, TOPK]), ALU.is_equal
                    ).then_inc(hots_ready, 1)

            def look_up(h):
                dve.wait_ge(picked, ONE + h + 1)
                nc.vector.tensor_reduce(tij[:, :, ds(h, 1), :].rearrange("p t o k -> p t (o k)"),
                                        hot[:, :, :, :], AX_X, ALU.add).then_inc(looked_up, 1)

            def head(h, first):
                link = Chain(dve, chain, h * NLINK)

                def carry():
                    nc.vector.memset(carrier[:, :], 0.0)

                def top16(val, idx, src, rest):
                    for t in range(NTT):
                        last = nc.vector.max(val(t)[:, 0:8], src(t))
                    link(last)
                    carry()
                    for t in range(NTT):
                        nc.vector.max_index(idx(t)[:, 0:8], val(t)[:, 0:8], src(t))
                        last = nc.vector.match_replace(rest(t), val(t)[:, 0:8], src(t), NEGBIG)
                    link(last)
                    carry()
                    for t in range(NTT):
                        last = nc.vector.max(val(t)[:, 8:16], rest(t))
                    link(last)
                    carry()
                    for t in range(NTT):
                        last = nc.vector.max_index(idx(t)[:, 8:16], val(t)[:, 8:16], rest(t))
                    return last

                for c in range(2):
                    dve.wait_ge(s_kept, ONE + 6 * h + 3 * c + 3)
                    carry()
                    last = top16(lambda t: v[:, c, t, :], lambda t: vi[:, c, t, :], lambda t: sc[:, c, t, :],
                                 lambda t: sc2[:, t, :])
                    last.then_inc(s_used[c], 1)
                    if c == 0 and not first:
                        onehots(h - 1)
                    dve.wait_ge(s_used[c], ONE + h + 1)
                    link(nc.vector.tensor_copy(vf[:, c, :, :], vi[:, c, :, :]))

                def half(c, lo, hi):
                    return v[:, c, :, lo:hi]
                nc.vector.tensor_tensor(cs[:, :, 0:2 * R], half(1, 0, TOPK),
                                        half(0, 0, 1).to_broadcast([P, NTT, TOPK]), ALU.add)
                nc.vector.tensor_tensor(cs[:, :, LASTROW * R:NSUM], half(0, R, TOPK),
                                        half(1, 0, 1).to_broadcast([P, NTT, R]), ALU.add)
                link(nc.vector.tensor_tensor(
                    cs[:, :, 2 * R:LASTROW * R].rearrange("p t (i j) -> p t i j", j=R),
                    half(0, 1, R).unsqueeze(3).to_broadcast([P, NTT, R - 1, R]),
                    half(1, 0, R).unsqueeze(2).to_broadcast([P, NTT, R - 1, R]), ALU.add))
                carry()
                link(top16(lambda t: best[:, t, :], lambda t: pos[:, t, :], lambda t: cs[:, t, :],
                           lambda t: cs2[:, t, :]))
                nc.vector.tensor_scalar(prc[:, 0, :, :], pos[:, :, :], 3, None, ALU.logical_shift_right)
                nc.vector.tensor_scalar(prc[:, 1, :, :], pos[:, :, :], R - 1, None, ALU.bitwise_and
                                        ).then_inc(pos_ready, 1)
                link(nc.vector.tensor_copy(top[:, :, ds(h, 1), :].rearrange("p t o k -> p t (o k)"), best[:, :, :]))
                if not first:
                    look_up(h - 1)
                assert link.n == NLINK, link.n

            head(0, True)
            with dve.Fori(1, PH) as h:
                head(h, False)
            last_links = Chain(dve, chain, PH * NLINK)
            nc.vector.tensor_tensor(sub[:, :, :, :], top[:, :, :, :],
                                    top[:, :, :, 0:1].to_broadcast([P, NTT, PH, TOPK]), ALU.subtract
                                    ).then_inc(shifted, 1)
            onehots(PH - 1)
            dve.wait_ge(exped, ONE + 1)
            last_links(nc.vector.tensor_reduce(sm[:, 0, :].rearrange("p (t h) -> p t h", h=PH), ex[:, :, :, :],
                                               AX_X, ALU.add))
            last_links(nc.vector.reciprocal(sm[:, 1, :], sm[:, 0, :]))
            nc.vector.tensor_tensor(gt[:, :, :, :], ex[:, :, :, :],
                                    sm[:, 1, :].rearrange("p (t h) -> p t h", h=PH).unsqueeze(3)
                                    .to_broadcast([P, NTT, PH, TOPK]), ALU.mult).then_inc(gates_ready, 1)
            look_up(PH - 1)


def gate_phase(nc, a, ps, gT, iT, jT, g_dram, g_sample):
    with Scope(nc) as ctx:
        def sb(n, shape, dt=F32):
            return ctx.enter_context(nc.sbuf_tensor("ga_" + n, shape, dt))

        def sem(n):
            return ctx.sem("ga_" + n)

        GT = 8
        PER = P // GT
        SETS = 4
        SLOT = (0, 1, 0, 2)
        io_i, io = sb("iota_i", [P, NK], I32), sb("iota", [P, NK])
        oi, oj = sb("onehot_i", [P, SETS, GT, NK]), sb("onehot_j", [P, 3, GT, NK])
        stage = sb("stage", [P, 2, NK, P])
        io_ready = sem("iota_ready")
        hot_i, hot_j, weighed, done, kept = ([sem(f"{n}{s}") for s in range(SETS)] for n in (
            "onehots_i_ready", "onehots_j_ready", "weighed", "products_done", "kept"))
        out = [sem(f"stored{u}") for u in range(2)]
        distances = sem("distances")

        block = ctx.block()

        def over_steps(eng, step, tile=None):
            with eng.Fori(0, NT // 2) as tp:
                for u in range(2):
                    if tile:
                        tile(tp, u)
                    with eng.Fori(0, PER // SETS) as g:
                        for s in range(SETS):
                            step((2 * tp + u) * (PER // SETS) + g, s, u, (2 * tp + u) * P + (SETS * g + s) * GT,
                                 (SETS * g + s) * GT)
            step(NT * PER // SETS, 0, None, SEQ, 0)

        @block.gpsimd
        def _(pool):
            nc.gpsimd.iota(io_i[:, :], pattern=[[1, NK]], base=0, channel_multiplier=0).then_inc(io_ready, 1)
            pool.wait_ge(io_ready, ONE + 1)
            nc.gpsimd.tensor_copy(io[:, :], io_i[:, :]).then_inc(io_ready, 1)

            def weigh(n, s, u, col, local):
                pool.wait_ge(hot_i[s], ONE + n + 1)
                nc.gpsimd.tensor_tensor(oi[:, s, :, :], oi[:, s, :, :],
                                        gT[:, ds(col, GT)].unsqueeze(2).to_broadcast([P, GT, NK]),
                                        ALU.mult).then_inc(weighed[s], 1)
            over_steps(pool, weigh)

        @block.vector
        def _(dve):
            dve.wait_ge(io_ready, ONE + 2)

            def onehots(n, s, u, col, local):
                def make(hot, index, first, ready):
                    nc.vector.tensor_tensor(
                        hot, io[:, :].unsqueeze(1).to_broadcast([P, GT, NK]),
                        index[:, ds(first, GT)].unsqueeze(2).to_broadcast([P, GT, NK]), ALU.is_equal
                        ).then_inc(ready, 1)

                dve.wait_ge(done[s], ONE + n)
                make(oi[:, s, :, :], iT, col, hot_i[s])
                j, first = (0, col) if u is None else (s - 1, col - GT)
                if j >= 0:
                    user, count = ((done[2], n), (done[1], n), (done[0], n + 1))[j]
                    dve.wait_ge(user, ONE + count)
                    make(oj[:, SLOT[j], :, :], jT, first, hot_j[j])
            over_steps(dve, onehots)

        @block.tensor
        def _(pe):
            def products(n, s, u, col, local):
                pe.wait_ge(hot_j[s], ONE + n + 1)
                pe.wait_ge(weighed[s], ONE + n + 1)
                pe.wait_ge(kept[s], ONE + n)
                for k in range(GT):
                    last = nc.tensor.matmul(ps[:, 2 * s + k // 4, (k % 4) * NK:(k % 4 + 1) * NK], oj[:, SLOT[s], k, :],
                                            oi[:, s, k, :], start=True, stop=True)
                last.then_inc(done[s], 1)
            over_steps(pe, products)

        @block.scalar
        def _(act):
            def onehots(n, col):
                s = SETS - 1
                act.wait_ge(done[s], ONE + n)
                for k in range(GT):
                    last = nc.scalar.activation(oj[:, SLOT[s], k, :], io[:, :], ACT.Square,
                                                bias=jT[:, ds(col + k, 1)], scale=-1.0)
                last.then_inc(distances, 1)
                act.wait_ge(distances, ONE + n + 1)
                nc.scalar.activation(oj[:, SLOT[s], :, :], oj[:, SLOT[s], :, :], ACT.Relu, bias=1.0,
                                     scale=-1.0).then_inc(hot_j[s], 1)

            def keep(n, s, u, col, local):
                act.wait_ge(done[s], ONE + n + 1)
                dst = g_sample[:, :, :] if u is None else stage[:, u, :, ds(local, GT)]
                nc.scalar.activation(dst.rearrange("p i t -> p t i"),
                                     ps[:, 2 * s:2 * s + 2, :].rearrange("p b (t i) -> p (b t) i", i=NK),
                                     ACT.Copy).then_inc(kept[s], 1)
                if s == 0 and u is not None:
                    onehots(n, col + (SETS - 1) * GT)

            def tile(tp, u):
                act.wait_ge(out[u], ONE + 16 * tp)
            act.wait_ge(io_ready, ONE + 2)
            over_steps(act, keep, tile)

        @block.sync
        def _(sp):
            with sp.Fori(0, NT // 2) as tp:
                for u in range(2):
                    for s in range(SETS):
                        sp.wait_ge(kept[s], ONE + (2 * tp + u + 1) * (PER // SETS))
                    sp.dma_start(g_dram[:, :, ds((2 * tp + u) * P, P)].rearrange("i j t -> j i t"),
                                 stage[:, u, :, :]).then_inc(out[u], 16)
            for u in range(2):
                sp.wait_ge(out[u], ONE + 16 * (NT // 2))


def expert_phase(nc, a, ps, ident, z2T, g_dram, g_sample, h_dram, top, left):
    zh = top.enter_context(nc.sbuf_tensor("z2_hi", [P, KD, T], F32R, side="right"))
    zl = top.enter_context(nc.sbuf_tensor("z2_lo", [P, KD, T], F32R, side="right"))
    with Scope(nc) as ctx:
        s_hi, s_lo = ctx.sem("sp_z_hi"), ctx.sem("sp_z_lo")
        block = ctx.block()

        @block.scalar
        def _(act):
            for k in range(KD):
                nc.scalar.activation(zh[:, k, :], z2T[:, k, :], ACT.Copy).then_inc(s_hi, 1)

        @block.vector
        def _(dve):
            for k in range(KD):
                dve.wait_ge(s_hi, ONE + k + 1)
                nc.vector.tensor_tensor(zl[:, k, :], z2T[:, k, :], zh[:, k, :].bitcast(F32),
                                        ALU.subtract).then_inc(s_lo, 1)
    left.close()

    NG = NK // GC
    NB = KD * len(BLOCKS)
    OUT = [(k, lo, hi) for k in range(KD) for lo, hi in BLOCKS]
    outer = ExitStack()
    with outer:
        accT = outer.enter_context(nc.sbuf_tensor("accT", [P, KD, T], F32))
        with Scope(nc) as ctx:
            def sb(n, shape, dt=F32):
                return ctx.enter_context(nc.sbuf_tensor("ex_" + n, shape, dt))

            def sem(n):
                return ctx.sem("ex_" + n)

            Ur, Vr = sb("u", [P, KD, P]), sb("v", [P, D])
            Uh, Ul = sb("u_hi", [P, 2, KD, P], F32R), sb("u_lo", [P, 2, KD, P], F32R)
            Vh, Vl = sb("v_hi", [P, GC, D], F32R), sb("v_lo", [P, GC, D], F32R)
            G = sb("gates", [P, SEQ])
            gl = sb("gelu", [P, 2, T])
            Ah, Al = sb("a_hi", [P, GC, T], F32R), sb("a_lo", [P, GC, T], F32R)
            acc_set, u_in = sem("acc_zeroed"), sem("u_loaded")
            v_in, g_in = ctx.queue_sem("ex_v_loaded"), ctx.queue_sem("ex_gates_loaded")
            u_hi, u_lo, v_hi, v_lo = sem("u_hi_ready"), sem("u_lo_ready"), sem("v_hi_ready"), sem("v_lo_ready")
            h_ready, gelu, weighed = sem("hidden_ready"), sem("gelu_done"), sem("weighed")
            a_hi, a_lo = sem("a_hi_ready"), sem("a_lo_ready")
            f_ready, f_added = sem("f_ready"), sem("f_added")
            block = ctx.block()

            @block.sync
            def _(sp):
                def load_u(n):
                    sp.wait_ge(u_lo, ONE + n)
                    sp.dma_start(Ur[:, :, :], a["expert_uT"][ds(n, 1)].rearrange("o p k e -> p (o k) e")
                                 ).then_inc(u_in, 16)
                load_u(0)
                with sp.Fori(1, NK) as n:
                    load_u(n)

            @block.gpsimd
            def _(pool):
                def load_g(n):
                    pool.wait_ge(weighed, ONE + n)
                    pool.dma_start(G[:, :], g_dram[ds(n, 1)].rearrange("o j t -> j (o t)")).then_inc(g_in, 16)

                def load_v(n):
                    pool.wait_ge(v_lo, ONE + n)
                    pool.dma_start(Vr[:, :], a["expert_v"][ds(n * P, P), :]).then_inc(v_in, 16)

                nc.gpsimd.memset(accT[:, :, :], 0.0).then_inc(acc_set, 1)
                with pool.Fori(0, NG) as g:
                    load_g(GC * g)
                    load_v(GC * g)
                    load_g(GC * g + 1)
                    load_g(GC * g + 2)
                    load_v(GC * g + 1)
                    load_v(GC * g + 2)
                    load_g(GC * g + 3)
                    load_v(GC * g + 3)

            def over_groups(body):
                def run(eng):
                    body(eng, 0, True, False)
                    with eng.Fori(1, NG - 1) as g:
                        body(eng, g, False, False)
                    body(eng, NG - 1, False, True)
                return run

            def hidden(pe, g, c, first):
                n = GC * g + c
                pe.wait_ge(u_lo, ONE + n + 1)
                if not first or c >= 2:
                    pe.wait_ge(gelu, ONE + n - 1)
                if first and c == 0:
                    pe.wait_ge(f_added, ONE)
                s = c % 2
                for b, (lo, hi) in enumerate(BLOCKS):
                    for k in range(KD):
                        for i, (u, z) in enumerate(((Uh, zh), (Uh, zl), (Ul, zh))):
                            last = nc.tensor.matmul(ps[:, 3 * s + b, 0:TB], u[:, s, k, :], z[:, k, lo:hi],
                                                    start=(k == 0 and i == 0), stop=(k == KD - 1 and i == 2))
                last.then_inc(h_ready, 1)

            def values(pe, g):
                pe.wait_ge(a_lo, ONE + GC * g + GC)
                pe.wait_ge(v_lo, ONE + GC * g + GC)
                for m, (k, lo, hi) in enumerate(OUT):
                    pe.wait_ge(f_added, ONE + NB * g + max(m - 1, 0))
                    for c in range(GC):
                        for i, (v, x) in enumerate(((Vh, Ah), (Vh, Al), (Vl, Ah))):
                            last = nc.tensor.matmul(ps[:, 6 + m % 2, 0:TB], v[:, c, k * P:(k + 1) * P],
                                                    x[:, c, lo:hi],
                                                    start=(c == 0 and i == 0), stop=(c == GC - 1 and i == 2))
                    last.then_inc(f_ready, 1)

            @block.tensor
            def _(pe):
                def body(pe, g, first, last):
                    hidden(pe, g, 0, first)
                    hidden(pe, g, 1, first)
                    if not first:
                        values(pe, g - 1)
                    hidden(pe, g, 2, first)
                    hidden(pe, g, 3, first)
                over_groups(body)(pe)
                values(pe, NG - 1)

            @block.scalar
            def _(act):
                def split_u(n, s, first=False):
                    act.wait_ge(u_in, ONE + 16 * n + 16)
                    if not first:
                        act.wait_ge(h_ready, ONE + n - 1)
                    nc.scalar.activation(Uh[:, s, :, :], Ur[:, :, :], ACT.Copy).then_inc(u_hi, 1)

                def gelus(g, c, first):
                    n, s = GC * g + c, c % 2
                    act.wait_ge(h_ready, ONE + n + 1)
                    if not first or c >= 2:
                        act.wait_ge(a_lo, ONE + n - 1)
                    nc.scalar.activation(gl[:, s, :].rearrange("p (b n) -> p b n", b=3),
                                         ps[:, 3 * s:3 * s + 3, 0:TB], ACT.Gelu).then_inc(gelu, 1)

                def split_a(g, c):
                    n = GC * g + c
                    act.wait_ge(weighed, ONE + n + 1)
                    act.wait_ge(f_ready, ONE + NB * g)
                    nc.scalar.activation(Ah[:, c, :], gl[:, c % 2, :], ACT.Copy).then_inc(a_hi, 1)

                def split_v(g, c):
                    act.wait_ge(v_in, 16 * (GC * g + c) + 16)
                    act.wait_ge(f_ready, ONE + NB * g)
                    nc.scalar.activation(Vh[:, c, :], Vr[:, :], ACT.Copy).then_inc(v_hi, 1)

                def body(act, g, first, last):
                    split_u(GC * g + 2, 0)
                    gelus(g, 0, first)
                    split_u(GC * g + 3, 1)
                    gelus(g, 1, first)
                    split_a(g, 0)
                    split_a(g, 1)
                    split_v(g, 0)
                    split_v(g, 1)
                    gelus(g, 2, first)
                    if not last:
                        split_u(GC * g + 4, 0)
                    split_a(g, 2)
                    split_v(g, 2)
                    gelus(g, 3, first)
                    if not last:
                        split_u(GC * g + 5, 1)
                    split_a(g, 3)
                    split_v(g, 3)

                split_u(0, 0, True)
                split_u(1, 1, True)
                over_groups(body)(act)

            @block.vector
            def _(dve):
                def split_u(n, s):
                    dve.wait_ge(u_hi, ONE + n + 1)
                    nc.vector.tensor_tensor(Ul[:, s, :, :], Ur[:, :, :], Uh[:, s, :, :].bitcast(F32),
                                            ALU.subtract).then_inc(u_lo, 1)

                def weigh(g, c):
                    n, s = GC * g + c, c % 2
                    dve.wait_ge(gelu, ONE + n + 1)
                    dve.wait_ge(g_in, 16 * n + 16)
                    nc.vector.tensor_tensor(gl[:, s, SEQ:T], gl[:, s, SEQ:T],
                                            g_sample[:, ds(n, 1), :].rearrange("p o t -> p (o t)"), ALU.mult)
                    nc.vector.tensor_tensor(gl[:, s, 0:SEQ], gl[:, s, 0:SEQ], G[:, :], ALU.mult).then_inc(weighed, 1)

                def split_a(g, c):
                    dve.wait_ge(a_hi, ONE + GC * g + c + 1)
                    nc.vector.tensor_tensor(Al[:, c, :], gl[:, c % 2, :], Ah[:, c, :].bitcast(F32),
                                            ALU.subtract).then_inc(a_lo, 1)

                def split_v(g, c):
                    dve.wait_ge(v_hi, ONE + GC * g + c + 1)
                    nc.vector.tensor_tensor(Vl[:, c, :], Vr[:, :], Vh[:, c, :].bitcast(F32),
                                            ALU.subtract).then_inc(v_lo, 1)

                def add(g, start, end):
                    for m, (k, lo, hi) in list(enumerate(OUT))[start:end]:
                        dve.wait_ge(f_ready, ONE + NB * g + m + 1)
                        nc.vector.tensor_tensor(accT[:, k, lo:hi], accT[:, k, lo:hi], ps[:, 6 + m % 2, 0:TB],
                                                ALU.add).then_inc(f_added, 1)

                def body(dve, g, first, last):
                    split_u(GC * g + 2, 0)
                    weigh(g, 0)
                    split_u(GC * g + 3, 1)
                    if not first:
                        add(g - 1, 0, 2)
                    weigh(g, 1)
                    if not first:
                        add(g - 1, 2, NB)
                    split_a(g, 0)
                    split_a(g, 1)
                    split_v(g, 0)
                    split_v(g, 1)
                    weigh(g, 2)
                    if not last:
                        split_u(GC * g + 4, 0)
                    split_a(g, 2)
                    split_v(g, 2)
                    weigh(g, 3)
                    if not last:
                        split_u(GC * g + 5, 1)
                    split_a(g, 3)
                    split_v(g, 3)

                split_u(0, 0)
                split_u(1, 1)
                dve.wait_ge(acc_set, ONE + 1)
                over_groups(body)(dve)
                add(NG - 1, 0, NB)

        final_phase(nc, a, ps, ident, accT, h_dram)


def final_phase(nc, a, ps, ident, accT, h_dram):
    NTT = NT + 1
    with Scope(nc) as ctx:
        def sb(n, shape):
            return ctx.enter_context(nc.sbuf_tensor("fn_" + n, shape, F32))

        rows, gain, junk, st = sb("rows", [P, NTT, D]), sb("gain", [P, D]), sb("junk", [P, D]), sb("st", [P, 4, NTT])
        s_h = [ctx.sem(f"fn_h_loaded{u}") for u in range(2)]
        s_g, turned, added, sq, mean, root, inv, ready, out = (ctx.sem("fn_" + x) for x in (
            "gain_loaded", "turned", "added", "squares", "mean", "root", "inverse",
            "rows_ready", "stored"))
        block = ctx.block()

        @block.sync
        def _(sp):
            for t, lo, r in TILES:
                if t >= 2:
                    sp.wait_ge(s_h[t % 2], ONE + 16 * (t // 2))
                sp.dma_start(rows[0:r, t, :], h_dram[lo:lo + r, :]).then_inc(s_h[t % 2], 16)
                if t == 1:
                    sp.dma_start(gain[:, :], a["g_final"].partition_broadcast(P)).then_inc(s_g, 16)
            for t, lo, r in TILES:
                sp.wait_ge(ready, ONE + t + 1)
                sp.dma_start(a["o_y_p"][lo:lo + r, :] if t < NT else a["o_y_s"], rows[0:r, t, :]).then_inc(out, 16)
            sp.wait_ge(out, ONE + 16 * NTT)

        @block.tensor
        def _(pe):
            for t, lo, r in TILES:
                if t >= 4:
                    pe.wait_ge(added, ONE + t - 3)
                for k in range(KD):
                    last = nc.tensor.transpose(ps[0:r, 2 * (t % 4) + k // 4, (k % 4) * P:(k % 4 + 1) * P],
                                               accT[:, k, lo:lo + r], ident[:, :])
                last.then_inc(turned, 1)

        @block.scalar
        def _(act):
            for t, lo, r in TILES:
                act.wait_ge(added, ONE + t + 1)
                if t:
                    act.wait_ge(sq, ONE + t)
                nc.scalar.activation(junk[0:r, :], rows[0:r, t, :], ACT.Square,
                                     accum_out=st[0:r, 0, t:t + 1]).then_inc(sq, 1)
                act.wait_ge(mean, ONE + t + 1)
                nc.scalar.activation(st[0:r, 2, t:t + 1], st[0:r, 1, t:t + 1], ACT.Sqrt).then_inc(root, 1)

        @block.vector
        def _(dve):

            def add(t, lo, r):
                dve.wait_ge(s_h[t % 2], ONE + 16 * (t // 2 + 1))
                dve.wait_ge(turned, ONE + t + 1)
                dst = rows[0:r, t, :].rearrange("p (b n) -> p b n", n=BANK)
                nc.vector.tensor_tensor(dst, dst, ps[0:r, 2 * (t % 4):2 * (t % 4) + 2, :], ALU.add).then_inc(added, 1)

            def scale(t, lo, r):
                dve.wait_ge(sq, ONE + t + 1)
                nc.vector.tensor_scalar(st[0:r, 1, t:t + 1], st[0:r, 0, t:t + 1], 1.0 / D, EPS, ALU.mult,
                                        ALU.add).then_inc(mean, 1)
                dve.wait_ge(root, ONE + t + 1)
                nc.vector.reciprocal(st[0:r, 3, t:t + 1], st[0:r, 2, t:t + 1]).then_inc(inv, 1)
                dve.wait_ge(inv, ONE + t + 1)
                dve.wait_ge(s_g, ONE + 16)
                nc.vector.scalar_tensor_tensor(out=rows[0:r, t, :], in0=rows[0:r, t, :], scalar=st[0:r, 3, t:t + 1],
                                               in1=gain[0:r, :], op0=ALU.mult, op1=ALU.mult).then_inc(ready, 1)

            add(*TILES[0])
            for tile, following in zip(TILES, TILES[1:]):
                add(*following)
                scale(*tile)
            scale(*TILES[-1])



def tables():
    f = np.float32
    pos = np.zeros((NT + 1, P), f)
    pos[0:NT] = np.arange(SEQ, dtype=f).reshape(NT, P)
    pos[NT] = PAST
    base = (f(1.0) / (f(10000.0) ** np.linspace(0.0, 1.0, RDK // 2, dtype=f))).astype(f)
    ang = (pos[:, :, None] * base).astype(f)
    inv = (f(500000.0) ** (-np.arange(0, ROT, 2, dtype=f) / f(ROT))).astype(f)
    ang_a = (pos[:, :, None] * inv).astype(f)
    decay = np.log(1.0 - 2.0 ** (-5.0 - np.arange(RH)))
    m, l = np.arange(P)[:, None], np.arange(P)[None, :]
    maskT = np.where((l >= m)[:, None, :], np.exp(decay[None, :, None] * np.maximum(l - m, 0)[:, None, :]), 0.0)
    qdec = np.broadcast_to(np.exp(decay[:, None] * (np.arange(P) + 1.0)), (P, RH, P))
    kdec = np.exp(decay[None, :] * (P - 1.0 - np.arange(P))[:, None]) * RDK ** -0.5
    q, k = np.arange(P)[:, None], np.arange(P)[None, :]
    row = np.arange(2 * AH * NS)
    sample, head, second = row // (2 * AH), (row // 2) % AH, row % 2
    sel = np.concatenate([(second == 0)[:, None], (second == 1)[:, None],
                          sample[:, None] == np.arange(NS), head[:, None] == np.arange(AH)], axis=1)
    return {
        "ident": np.eye(P), "ret_cos": np.cos(ang), "ret_sin": np.sin(ang), "att_cos": np.cos(ang_a),
        "att_sin": np.sin(ang_a), "ret_maskT": maskT, "ret_qdec": qdec, "ret_kdec": kdec,
        "att_mask": np.where(k <= q, 0.0, NEG), "sel": sel,
    }


OUTS = {
    "o_y_p": (SEQ, D), "o_y_s": (NS, D), "o_ret_p": (RH, RDK, RDV), "o_k_p": (SEQ, AH * 2 * ADQ),
    "o_v_p": (SEQ, AH * ADV), "o_ret_s": (NS, RH, RDK, RDV), "o_k_s": (NS, AH * 2 * ADQ), "o_v_s": (NS, AH * ADV),
}


def lay_out(i):
    c = np.ascontiguousarray
    w_in = np.asarray(i["w_in"])[0]
    cols = np.cumsum([0, 512, 512, 1024, 512, 512, 512, D, D])
    rows = lambda w: w.reshape(-1, P, w.shape[1]).transpose(1, 0, 2)
    blocks = lambda w: w.reshape(-1, P, w.shape[1] // P, P).transpose(2, 1, 0, 3)
    U = np.asarray(i["expert_u"])[0]
    gates = blocks(w_in[:, cols[6]:cols[7]]), blocks(w_in[:, cols[7]:cols[8]])
    return {
        "x": c(np.concatenate([np.asarray(i["x_prompt"])[0], np.asarray(i["x_sample"])[:, 0]])),
        "state": c(np.asarray(i["state_ret"])[0]),
        "cache_kT": c(np.asarray(i["cache_k"])[0].transpose(0, 2, 3, 1)),
        "cache_v": c(np.asarray(i["cache_v"])[0].reshape(POOL, PAGE, AH * ADV)),
        "page_table": c(np.asarray(i["page_table"]).reshape(1, NS * NPAGE)),
        "g_mix": c(np.asarray(i["g_mix"]).reshape(KD, P).T), "g_ffn": c(np.asarray(i["g_ffn"]).reshape(KD, P).T),
        "g_subln": c(np.asarray(i["g_subln"]).reshape(ADV, 1)), "g_final": c(np.asarray(i["g_final"])),
        "lams": c(np.concatenate([np.asarray(i[n]) for n in ("lam_q1", "lam_k1", "lam_q2", "lam_k2")])),
        "w_ret": c(rows(w_in[:, 0:cols[3]])), "w_att": c(rows(w_in[:, cols[3]:cols[6]])),
        "w_merge": c(np.concatenate([*gates, blocks(np.asarray(i["w_br_ret"])[0]),
                                     blocks(np.asarray(i["w_br_att"])[0])], axis=2)),
        "w_out": c(rows(np.asarray(i["w_out"])[0])),
        "w_query": c(blocks(np.asarray(i["w_query"])[0])),
        "sub_keysT": c(np.asarray(i["sub_keys"])[0].reshape(2 * PH, NK, P).transpose(2, 0, 1)),
        "expert_uT": c(U.reshape(NK, P, KD, P).transpose(0, 3, 2, 1)),
        "expert_v": c(np.asarray(i["expert_v"])[0]),
        **{n: c(t.astype(np.float32)) for n, t in tables().items()},
    }


def kernel(**inputs):
    import concourse.bacc as bacc
    from concourse.bass_utils import run_bass_kernel_spmd

    nc = bacc.Bacc("TRN2", target_bir_lowering=False, num_devices=1)
    arrays = lay_out(inputs)
    aps = {n: nc.dram_tensor("in_" + n, x.shape, mybir.dt.from_np(x.dtype), kind="ExternalInput").ap()
           for n, x in arrays.items()}
    for n, shape in OUTS.items():
        aps[n] = nc.dram_tensor(n, shape, F32, kind="ExternalOutput").ap()
    build(nc, aps)
    r = run_bass_kernel_spmd(nc, [{"in_" + n: x for n, x in arrays.items()}], core_ids=[0]).results[0]
    return (r["o_y_p"].reshape(1, SEQ, D), r["o_y_s"].reshape(NS, 1, D),
            r["o_ret_p"].reshape(1, 1, RH, RDK, RDV), r["o_k_p"].reshape(1, 1, SEQ, AH, 2 * ADQ),
            r["o_v_p"].reshape(1, 1, SEQ, AH, ADV), r["o_ret_s"].reshape(1, NS, RH, RDK, RDV),
            r["o_k_s"].reshape(1, NS, 1, AH, 2 * ADQ), r["o_v_s"].reshape(1, NS, 1, AH, ADV))
```
